# Optimizing a Trainium2 kernel written in Bass

```python
import jax, jax.numpy as jnp
from jax import lax
import numpy as np

D_MODEL = 1024
BATCH = 1
SEQ = 512
DEPTH = 2
DEC_BATCH = 8
DEC_SEQ = 1
PAST_LEN = 2048
PAGE_SIZE = 128

N_META = 16
N_HEADS = 8
HEAD_DIM = 64
N_KV_HEADS = 4
GROUP = N_HEADS // N_KV_HEADS
ROT_DIM = HEAD_DIM // 4
ROPE_THETA = 500000.0
ATT_W = N_HEADS * HEAD_DIM
KV_W = N_KV_HEADS * HEAD_DIM
N_IDX_HEADS = 8
IDX_DIM = 64
IDX_ROT_DIM = IDX_DIM // 4
IDX_W_SCALE = (N_IDX_HEADS * IDX_DIM) ** -0.5
TOPK_MAX = 256
QBLOCK = 128
N_REC_HEADS = 4
REC_KEY_DIM = 128
REC_VAL_DIM = 128
REC_W = N_REC_HEADS * REC_KEY_DIM
REC_V = N_REC_HEADS * REC_VAL_DIM
REC_CHUNK = 64
D_FF = -(-8 * D_MODEL // (3 * 256)) * 256
EPS = 1e-6
SPLIT_SIZES = (ATT_W, KV_W, KV_W, N_IDX_HEADS * IDX_DIM, IDX_DIM, N_IDX_HEADS,
               REC_W, REC_W, REC_V, REC_V, D_MODEL, D_MODEL)
D_IN = sum(SPLIT_SIZES)

kernel_name = "meta_dsa_hgrn2_gated_hybrid_step"

def rms_norm(x, g):
    xf = x.astype(jnp.float32)
    y = xf * lax.rsqrt(jnp.mean(xf * xf, axis=-1, keepdims=True) + EPS)
    return (y * g.astype(jnp.float32)).astype(x.dtype)

def rope(x, pos, rot_dim):
    xf = x.astype(jnp.float32)
    half = rot_dim // 2
    inv = jnp.power(ROPE_THETA, -2.0 * jnp.arange(half, dtype=jnp.float32) / rot_dim)
    ang = pos.astype(jnp.float32)[:, None] * inv[None, :]
    cos = jnp.cos(ang)[:, None, :]
    sin = jnp.sin(ang)[:, None, :]
    x1 = xf[..., :half]
    x2 = xf[..., half:rot_dim]
    out = jnp.concatenate([x1 * cos - x2 * sin, x2 * cos + x1 * sin, xf[..., rot_dim:]], axis=-1)
    return out.astype(x.dtype)

def split_columns(u):
    offs, acc = [], 0
    for s in SPLIT_SIZES[:-1]:
        acc += s
        offs.append(acc)
    return jnp.split(u, offs, axis=-1)

def indexer_scores(qi, wi, ki):
    dots = jnp.einsum('bthd,bsd->bths', qi.astype(jnp.float32), ki.astype(jnp.float32))
    return jnp.einsum('bths,bth->bts', jax.nn.relu(dots), wi.astype(jnp.float32))

def attend_selected(q, k_sel, v_sel, valid):
    B, T = q.shape[:2]
    qg = q.reshape(B, T, N_KV_HEADS, GROUP, HEAD_DIM).astype(jnp.float32)
    s = jnp.einsum('btngd,btknd->btngk', qg, k_sel.astype(jnp.float32)) * (HEAD_DIM ** -0.5)
    s = jnp.where(valid[:, :, None, None, :], s, -jnp.inf)
    p = jax.nn.softmax(s, axis=-1)
    o = jnp.einsum('btngk,btknd->btngd', p, v_sel.astype(jnp.float32))
    return o.reshape(B, T, ATT_W).astype(q.dtype)

def take_rows(a, idx):
    return jax.vmap(lambda arr, i: arr[i])(a, idx)

def prompt_attention_block(q, qi, wi, qpos, k, v, ki, top_k):
    S = k.shape[1]
    kpos = jnp.arange(S, dtype=jnp.int32)
    sc = indexer_scores(qi, wi, ki)
    sc = jnp.where(kpos[None, None, :] <= qpos[None, :, None], sc, -jnp.inf)
    _, idx = lax.top_k(sc, top_k)
    valid = idx <= qpos[None, :, None]
    return attend_selected(q, take_rows(k, idx), take_rows(v, idx), valid)

def gla_chunk(S0, q, k, v, logf):
    q = q.astype(jnp.float32)
    k = k.astype(jnp.float32)
    v = v.astype(jnp.float32)
    S0 = S0.astype(jnp.float32)
    b = jnp.cumsum(logf.astype(jnp.float32), axis=1)
    C = q.shape[1]
    causal = jnp.tril(jnp.ones((C, C), dtype=bool))
    diff = b[:, :, None] - b[:, None, :]
    decay = jnp.exp(jnp.where(causal[None, :, :, None, None], diff, -jnp.inf))
    scores = jnp.einsum('bthk,bshk,btshk->bths', q, k, decay)
    o = jnp.einsum('bths,bshv->bthv', scores, v) + jnp.einsum('bthk,bhkv->bthv', q * jnp.exp(b), S0)
    b_last = b[:, -1]
    S = jnp.exp(b_last)[..., None] * S0 + jnp.einsum('bshk,bshv->bhkv', k * jnp.exp(b_last[:, None] - b), v)
    return o, S

def mixer_front(x, pos, w_in_l, g_mix, g_q, g_k, lb):
    B, T, _ = x.shape
    h = rms_norm(x, g_mix)
    q, k, v, qi, ki, wi, qr, fr, ir, gr, ga, gb = split_columns(h @ w_in_l)
    q = rope(rms_norm(q.reshape(B, T, N_HEADS, HEAD_DIM), g_q), pos, ROT_DIM)
    k = rope(rms_norm(k.reshape(B, T, N_KV_HEADS, HEAD_DIM), g_k), pos, ROT_DIM)
    v = v.reshape(B, T, N_KV_HEADS, HEAD_DIM)
    qi = rope(qi.reshape(B, T, N_IDX_HEADS, IDX_DIM), pos, IDX_ROT_DIM)
    ki = rope(ki.reshape(B, T, 1, IDX_DIM), pos, IDX_ROT_DIM)[:, :, 0]
    wi = wi * IDX_W_SCALE
    f = lb + (1.0 - lb) * jax.nn.sigmoid(fr.astype(jnp.float32))
    rq = jax.nn.silu(qr).reshape(B, T, N_REC_HEADS, REC_KEY_DIM)
    rk = (1.0 - f).reshape(B, T, N_REC_HEADS, REC_KEY_DIM)
    rv = ir.reshape(B, T, N_REC_HEADS, REC_VAL_DIM)
    rlogf = jnp.log(f).reshape(B, T, N_REC_HEADS, REC_KEY_DIM)
    return (q, k, v, qi, ki, wi), (rq, rk, rv, rlogf), (gr, ga, gb)

def mixer_back(x, att, rec_o, gates, g_rec, w_pa_l, w_pb_l, w_o_l):
    gr, ga, gb = gates
    B, T, _ = x.shape
    rec = rms_norm(rec_o.astype(x.dtype), g_rec) * jax.nn.silu(gr.reshape(B, T, N_REC_HEADS, REC_VAL_DIM))
    a = att @ w_pa_l
    b = rec.reshape(B, T, REC_V) @ w_pb_l
    return x + (jax.nn.sigmoid(ga) * a + jax.nn.sigmoid(gb) * b) @ w_o_l

def swiglu_ffn(x, g, w_gu_l, w_down_l):
    h = rms_norm(x, g)
    gate, up = jnp.split(h @ w_gu_l, 2, axis=-1)
    return x + (jax.nn.silu(gate) * up) @ w_down_l

def prompt_mixer(x, w_in_l, g_mix, g_q, g_k, lb, g_rec, w_pa_l, w_pb_l, w_o_l):
    B, T, _ = x.shape
    n_real = T - N_META
    pos = jnp.arange(T, dtype=jnp.int32)
    (q, k, v, qi, ki, wi), (rq, rk, rv, rlogf), gates = mixer_front(x, pos, w_in_l, g_mix, g_q, g_k, lb)

    top_k = min(TOPK_MAX, n_real // 4)
    attend = lambda qb, qib, wib, pb: prompt_attention_block(qb, qib, wib, pb, k, v, ki, top_k)
    att_meta = attend(q[:, :N_META], qi[:, :N_META], wi[:, :N_META], pos[:N_META])
    n_blk = n_real // QBLOCK

    def to_qblocks(a):
        a = a[:, N_META:]
        return a.reshape((B, n_blk, QBLOCK) + a.shape[2:]).swapaxes(0, 1)

    att_real = lax.map(lambda xs: attend(*xs),
                       (to_qblocks(q), to_qblocks(qi), to_qblocks(wi), pos[N_META:].reshape(n_blk, QBLOCK)))
    att = jnp.concatenate([att_meta, att_real.swapaxes(0, 1).reshape(B, n_real, ATT_W)], axis=1)

    S0 = jnp.zeros((B, N_REC_HEADS, REC_KEY_DIM, REC_VAL_DIM), jnp.float32)
    o_meta, S = gla_chunk(S0, rq[:, :N_META], rk[:, :N_META], rv[:, :N_META], rlogf[:, :N_META])
    n_chunk = n_real // REC_CHUNK

    def to_chunks(a):
        a = a[:, N_META:]
        return a.reshape((B, n_chunk, REC_CHUNK) + a.shape[2:]).swapaxes(0, 1)

    def step(carry, xs):
        o, carry = gla_chunk(carry, *xs)
        return carry, o

    S, o_real = lax.scan(step, S, (to_chunks(rq), to_chunks(rk), to_chunks(rv), to_chunks(rlogf)))
    rec_o = jnp.concatenate([o_meta, o_real.swapaxes(0, 1).reshape(B, n_real, N_REC_HEADS, REC_VAL_DIM)], axis=1)

    y = mixer_back(x, att, rec_o, gates, g_rec, w_pa_l, w_pb_l, w_o_l)
    return y, k, v, ki, S

def sample_mixer(x, cache_k, cache_v, cache_idx_k, state_l, page_table, layer,
                 w_in_l, g_mix, g_q, g_k, lb, g_rec, w_pa_l, w_pb_l, w_o_l):
    DB, Tq, _ = x.shape
    past_len = page_table.shape[1] * PAGE_SIZE
    pos = past_len + jnp.arange(Tq, dtype=jnp.int32)
    (q, k, v, qi, ki, wi), (rq, rk, rv, rlogf), gates = mixer_front(x, pos, w_in_l, g_mix, g_q, g_k, lb)

    past_ki = cache_idx_k[layer, page_table].reshape(DB, past_len, IDX_DIM).astype(ki.dtype)
    all_ki = jnp.concatenate([past_ki, ki], axis=1)
    L = past_len + Tq
    sc = indexer_scores(qi, wi, all_ki)
    sc = jnp.where(jnp.arange(L, dtype=jnp.int32)[None, None, :] <= pos[None, :, None], sc, -jnp.inf)
    _, idx = lax.top_k(sc, min(TOPK_MAX, L // 4))

    is_past = idx < past_len
    pidx = jnp.minimum(idx, past_len - 1)
    phys = jax.vmap(lambda pt, i: pt[i])(page_table, pidx // PAGE_SIZE)
    off = pidx % PAGE_SIZE
    nidx = jnp.clip(idx - past_len, 0, Tq - 1)
    k_sel = jnp.where(is_past[..., None, None], cache_k[layer, phys, off].astype(k.dtype), take_rows(k, nidx))
    v_sel = jnp.where(is_past[..., None, None], cache_v[layer, phys, off].astype(v.dtype), take_rows(v, nidx))
    att = attend_selected(q, k_sel, v_sel, idx <= pos[None, :, None])

    rec_o, S = gla_chunk(state_l, rq, rk, rv, rlogf)

    y = mixer_back(x, att, rec_o, gates, g_rec, w_pa_l, w_pb_l, w_o_l)
    return y, k, v, ki, S

def setup_inputs(seed: int = 0) -> dict:
    key = jax.random.key(seed)
    ks = jax.random.split(key, 24)
    f32 = jnp.float32
    n_pages = PAST_LEN // PAGE_SIZE
    n_pool = (DEC_BATCH * n_pages * 5) // 4

    def nrm(k, shape, scale):
        return jax.random.normal(k, shape, f32) * scale

    def gain(k, shape):
        return 1.0 + 0.01 * jax.random.normal(k, shape, f32)

    page_table = jax.random.permutation(ks[7], n_pool)[:DEC_BATCH * n_pages].reshape(DEC_BATCH, n_pages).astype(jnp.int32)
    return {
        "x_prompt": nrm(ks[0], (BATCH, SEQ, D_MODEL), 1.0),
        "x_sample": nrm(ks[1], (DEC_BATCH, DEC_SEQ, D_MODEL), 1.0),
        "cache_k": nrm(ks[2], (DEPTH, n_pool, PAGE_SIZE, N_KV_HEADS, HEAD_DIM), 1.0),
        "cache_v": nrm(ks[3], (DEPTH, n_pool, PAGE_SIZE, N_KV_HEADS, HEAD_DIM), 1.0),
        "cache_idx_k": nrm(ks[4], (DEPTH, n_pool, PAGE_SIZE, IDX_DIM), 1.0),
        "state_rec": nrm(ks[5], (DEPTH, DEC_BATCH, N_REC_HEADS, REC_KEY_DIM, REC_VAL_DIM), 0.5),
        "page_table": page_table,
        "meta_tokens": nrm(ks[6], (N_META, D_MODEL), 1.0),
        "w_in": nrm(ks[8], (DEPTH, D_MODEL, D_IN), D_MODEL ** -0.5),
        "norm_mix": gain(ks[9], (DEPTH, D_MODEL)),
        "q_norm": gain(ks[10], (DEPTH, HEAD_DIM)),
        "k_norm": gain(ks[11], (DEPTH, HEAD_DIM)),
        "lb_raw": nrm(ks[12], (DEPTH, REC_W), 0.1),
        "rec_norm": gain(ks[13], (DEPTH, REC_VAL_DIM)),
        "w_pa": nrm(ks[14], (DEPTH, ATT_W, D_MODEL), ATT_W ** -0.5),
        "w_pb": nrm(ks[15], (DEPTH, REC_V, D_MODEL), REC_V ** -0.5),
        "w_o": nrm(ks[16], (DEPTH, D_MODEL, D_MODEL), D_MODEL ** -0.5),
        "norm_ffn": gain(ks[17], (DEPTH, D_MODEL)),
        "w_gu": nrm(ks[18], (DEPTH, D_MODEL, 2 * D_FF), D_MODEL ** -0.5),
        "w_down": nrm(ks[19], (DEPTH, D_FF, D_MODEL), D_FF ** -0.5),
    }

def reference(x_prompt, x_sample, cache_k, cache_v, cache_idx_k, state_rec, page_table, meta_tokens,
              w_in, norm_mix, q_norm, k_norm, lb_raw, rec_norm, w_pa, w_pb, w_o, norm_ffn, w_gu, w_down):
    sm = jax.nn.softmax(lb_raw.astype(jnp.float32), axis=0)
    lower_bounds = jnp.cumsum(sm, axis=0) - sm[0:1]

    B = x_prompt.shape[0]
    xp = jnp.concatenate([jnp.broadcast_to(meta_tokens[None].astype(x_prompt.dtype), (B, N_META, D_MODEL)), x_prompt], axis=1)
    xs = x_sample
    pk, pv, pki, ps = [], [], [], []
    sk, sv, ski, ss = [], [], [], []
    for l in range(DEPTH):
        front = (w_in[l], norm_mix[l], q_norm[l], k_norm[l], lower_bounds[l])
        back = (rec_norm[l], w_pa[l], w_pb[l], w_o[l])
        xp, k_, v_, ki_, S_ = prompt_mixer(xp, *front, *back)
        xp = swiglu_ffn(xp, norm_ffn[l], w_gu[l], w_down[l])
        pk.append(k_); pv.append(v_); pki.append(ki_); ps.append(S_)
        xs, k_, v_, ki_, S_ = sample_mixer(xs, cache_k, cache_v, cache_idx_k, state_rec[l], page_table, l, *front, *back)
        xs = swiglu_ffn(xs, norm_ffn[l], w_gu[l], w_down[l])
        sk.append(k_); sv.append(v_); ski.append(ki_); ss.append(S_)

    y_prompt = xp[:, N_META:]
    y_sample = xs
    return (y_prompt, y_sample, jnp.stack(pk), jnp.stack(pv), jnp.stack(pki), jnp.stack(ps),
            jnp.stack(sk), jnp.stack(sv), jnp.stack(ski), jnp.stack(ss))


_drawn_inputs = setup_inputs


def setup_inputs(seed=0):
    import zlib

    import numpy as np

    out = dict(_drawn_inputs(seed))
    spreads = {}
    factors = {'norm_mix': 4.014, 'q_norm': 8.0, 'k_norm': 5.218, 'rec_norm': 8.0, 'norm_ffn': 4.936}
    for name, (base, spread) in spreads.items():
        noise = np.random.default_rng([zlib.crc32(name.encode()), seed]).standard_normal(out[name].shape)
        drawn = base * np.exp(spread * noise) if base else spread * noise
        out[name] = __import__('jax').numpy.asarray(drawn.astype(out[name].dtype))
    for name, factor in factors.items():
        out[name] = (out[name] * factor).astype(out[name].dtype)
    return out
```

```python
def constants():
    import numpy as np

    P, T, TP = 128, 536, 528
    parts, where, at = [], {}, 0

    def add(name, a):
        nonlocal at
        full = np.zeros((P, a.shape[1]), np.float32)
        full[: a.shape[0]] = a
        where[name] = (at, a.shape[0], a.shape[1])
        parts.append(full)
        at += a.shape[1]

    i = np.arange(P)
    add("ident", np.eye(P))
    add("ones", np.ones((P, P)))
    add("head_ones", (i[:, None] // 64 == i[None, :] // 64).astype(np.float32))
    rot = np.zeros((P, P), np.float32)
    for base in (0, 64):
        for d in range(8):
            rot[base + d, base + d + 8] = -1.0
            rot[base + d + 8, base + d] = 1.0
    add("rot", rot.T)
    swap = np.zeros((P, P), np.float32)
    swap[i, (i + 64) % P] = 1.0
    add("swap", swap)
    add("causal", np.where(i[None, :] <= i[:, None], 0.0, -1e30))
    b8 = np.arange(8)
    add("page_row", (i[:, None] // 16 == b8[None, :]).astype(np.float32))
    add("row_page", (b8[:, None] == i[None, :] // 16).astype(np.float32))
    add("row_head", (b8[:, None] == np.arange(64)[None, :] // 8).astype(np.float32))
    add("head_row", (np.arange(64)[:, None] // 8 == b8[None, :]).astype(np.float32))
    add("iota16", np.tile(np.arange(16, dtype=np.float32), (8, 1)))
    resident = at
    pos = np.concatenate([np.arange(TP), np.full(T - TP, 2048)]).astype(np.float32)
    inv = np.power(np.float32(500000.0), np.float32(-2.0) * np.arange(8, dtype=np.float32) / np.float32(16))
    cos, sin = np.ones((P, T), np.float32), np.zeros((P, T), np.float32)
    for p in range(P):
        if p % 64 < 16:
            ang = (pos * inv[p % 8].astype(np.float32)).astype(np.float32)
            cos[p], sin[p] = np.cos(ang), np.sin(ang)
    add("cos", cos)
    add("sin", sin)
    levels = np.zeros((P, 8, P), np.float32)
    for lev in range(7):
        half = 64 >> lev
        same = i[:, None] // (2 * half) == i[None, :] // (2 * half)
        levels[:, lev] = same & (i[:, None] % (2 * half) < half) & (i[None, :] % (2 * half) >= half)
    levels[:, 7] = np.eye(P)
    return np.concatenate(parts, 1), levels, where, resident


def build(nc, t, out):
    from contextlib import ExitStack

    import concourse.bass as bass
    from concourse import mybir

    f32, f32r, i32, u32, u8 = (mybir.dt.float32, mybir.dt.float32r, mybir.dt.int32, mybir.dt.uint32, mybir.dt.uint8)
    ACT, ALU, AX = mybir.ActivationFunctionType, mybir.AluOpType, mybir.AxisListType
    ds = bass.ds

    P = 128
    DEPTH, DM, DFF = 2, 1024, 2816
    NP, NB = 512, 8
    META = 16
    TP = NP + META
    T = TP + NB
    HT = T // 2
    KT = DM // P
    NPOOL, PAGE, PAGES, PAST = 160, 128, 16, 2048
    TOPK_P, TOPK_S = 128, 256
    EPS, NEG, PICKED = 1e-6, -1e30, -3e38
    IDX_SCALE = (8 * 64) ** -0.5
    ATT_SCALE = 64 ** -0.5
    TILES = [(128 * j, min(128, TP - 128 * j)) for j in range(5)]
    TILES_ALL = TILES[:4] + [(512, 24)]
    WIDTH = [128, 256, 384, 512, 528]
    SC_AT = [0, 0, 256, 640, 1152]
    HALVES = [64, 32, 16, 8, 4, 2, 1]

    A_TILES = [12, 8, 9, 10, 11, 4, 5, 6, 7, 0, 1, 2, 3]
    UA, UB, UM, UO = 0, 16, 32, 64
    HID = [12, 10]
    UG = [72, 112]
    UD = [96, 132]
    UNITS = 148
    OA, OB, OM, OO = 0, 14, 30, 62
    OG = [70, 102]
    OD = [94, 122]
    OUTS = 130

    items = ["norm1", ("rope", 12)]
    items += [("rope", n) for n in (8, 9, 10, 11)]
    order = [4, 5, 0, 1, 2, 3]
    items += [("sumsq", 4)]
    for n, nxt in zip(order, order[1:] + [None]):
        if nxt is not None:
            items.append(("sumsq", nxt))
        items.append(("rope", n))
    items += ["sample_tokens"] + [("tokens", j) for j in range(5)]
    items += ["swapped", "index_weights", "new_key_dots"]
    items += [("key_turn", 0)]
    for r in range(8):
        if r < 7:
            items.append(("key_turn", r + 1))
        items.append(("key_dots", r))
    items += [("dots", j, h) for j in range(1, 5) for h in range(8)]
    for n in range(4):
        for j in range(5):
            items += [("qk", 2 * n, j), ("qk", 2 * n + 1, j), ("turn", 2 * n, j), ("turn", 2 * n + 1, j), ("pv", n, j)]
    items += ["rows_turn"]
    items += [("sel_turn", 0), ("sel_turn", 1), ("sel_dots", 0), ("sel_turn", 2), ("sel_dots", 1), ("sel_turn", 3),
              ("sel_dots", 2), ("sel_dots", 3)]
    items += ["sel_rows", "sel_probs", "sel_pv", "sel_swap"]
    for lev in range(8):
        items += [("level", lev, 0), ("level", lev, 1)] + ([("level_tail", lev)] if lev >= 3 else [])
    items += [("v_turn", c) for c in range(5)] + ["v_sample", "k_sample"]
    for c in range(5):
        items += [("decayed", c), ("rec_out", c), ("state", c)]
    for h in range(4):
        items += [("rank1", h), ("rec_sample", h)]
    items += [("rec_sumsq", h) for h in range(4)]
    items += ["norm2"]
    if len(items) % 2:
        items.append("none")
    ITEM = {name: n for n, name in enumerate(items)}
    ITEMS = len(items)

    csts, where = t["constants"], t["where"]
    ctx = ExitStack()
    with ctx:
        def sb(name, shape, dt=f32):
            return ctx.enter_context(nc.sbuf_tensor(name, shape, dt))

        def sem(name):
            return ctx.enter_context(nc.semaphore(name))

        x = sb("x", [P, KT, T])
        normed = sb("normed", [P, 2, KT, T], f32r)
        raw = [sb(f"raw{i}", [P, 8, P]) for i in range(4)]
        w_hi = [sb(f"w_hi{i}", [P, 8, P], f32r) for i in range(2)]
        w_lo = [sb(f"w_lo{i}", [P, 8, P], f32r) for i in range(2)]
        cst = sb("cst", [P, t["resident"]])
        level_mask = sb("level_mask", [P, 8, P], u8)
        params = sb("params", [P, DEPTH, 27])
        par = sb("par", [P, 27])
        lb_tmp = sb("lb_tmp", [P, 6, 4])
        eps = sb("eps", [P, 1])
        state = sb("state", [P, 4, P])
        last_decay = sb("last_decay", [P, 4, 5])
        pages_i = sb("pages_i", [P, 1], i32)
        pages_f = sb("pages_f", [P, 1])
        page_rows = sb("page_rows", [P, 4], i32)
        page_rows_f = sb("page_rows_f", [P, 4])
        table_i = sb("table_i", [NB, PAGES], i32)
        table_f = sb("table_f", [NB, PAGES])
        top8 = sb("top8", [P, 8])
        top8s = sb("top8s", [NB, 8])
        row_idx = sb("row_idx", [P, 16], i32)
        new_mask = sb("new_mask", [P, 16])
        flag = sb("flag", [NB, 1])
        row_base = sb("row_base", [P, 1])
        s_tok = sb("s_tok", [NB, 328])
        w_tok = sb("w_tok", [P, 5, 8])
        w_page = sb("w_page", [P, 8, 8])
        w_new = sb("w_new", [NB, 8, 8])
        swapped = sb("swapped", [P, 8, NB])
        q_idx = sb("q_idx", [P, P])
        q_sel = sb("q_sel", [P, 2, NB, 8])
        sc_page = sb("sc_page", [P, P])
        new_tmp = sb("new_tmp", [NB, 64])
        sel_s = sb("sel_s", [P, 2, 64])
        sel_p = sb("sel_p", [64, 260])
        sel_c = sb("sel_c", [64, 4])
        sel_new = sb("sel_new", [64, 8])
        sel_pT = sb("sel_pT", [P, 192])
        sel_o = sb("sel_o", [P, 2, NB, 4])
        row_st = sb("row_st", [P, 2, 4])

        base = (nc.sbuf_base + 63) // 64 * 64
        size = nc.sbuf_usable_end - base

        def place(name, shape, offset, dt=f32):
            n = 1
            for d in shape[1:]:
                n *= d
            n *= 1 if dt == u8 else 4
            assert offset + n <= size, (name, offset + n, size)
            return nc.alloc_sbuf_tensor_at(name, shape, dt, offset=base + offset)

        TB = T * 4
        A = place("proj_att", [P, 13, T], 0)
        PB0 = 29248
        B = place("proj_rec", [P, 16, T], PB0)
        idx_pages = place("idx_pages", [P, 2, 2048], PB0)
        idx_turned = place("idx_turned", [P, 2, 1024], PB0 + 16384)
        idx_relu = place("idx_relu", [P, 2, 1024], PB0 + 24576)
        o = PB0 + 16 * TB
        tok = place("tok", [P, 5, 584], o); o_tok = o; o += 5 * 584 * 4
        k_dup = place("k_dup", [P, 2, T], o); o += 2 * TB
        sc = place("sc", [P, 1680], o); o_sc = o; o += 1680 * 4
        ki_dup = place("ki_dup", [P, T], o); o_ss = o; o += TB
        ss = place("ss", [NB, PAST + 1], o)
        o += 8224
        o_v = o
        k_sel = place("k_sel", [P, 16, 256], 6 * TB)
        v_sel = place("v_sel", [P, 16, 256], o_v)
        found = place("found", [NB, TOPK_S], 6 * TB, u32)
        pick_i = place("pick_i", [NB, 2, TOPK_S], 6 * TB + 1024, u32)
        pick_f = place("pick_f", [NB, 4, TOPK_S], 6 * TB + 3072)
        page_eq = place("page_eq", [NB, TOPK_S, PAGES], o_v)
        E = place("E", [P, 2, TP], o_ss)
        pT = place("pT", [P, 2, 5, P], o_ss + 2 * TP * 4)
        sel_turned = place("sel_turned", [P, 2, 1024], o_sc - 2048)
        sq = place("sq", [P, 2, T], o_v)
        std = place("std", [P, T], o_v + 2 * TB)
        tmp = place("tmp", [P, 2, T], o_v + 3 * TB)
        rope = place("rope", [P, 2, T], o_v + 5 * TB)
        relu = place("relu", [P, 2, TP], o_v + 5 * TB)
        X1 = place("X1", [P, 4, TP], 0)
        K = place("K", [P, 4, T], 4 * TB)
        X0 = place("X0", [P, 4, TP], 8 * TB)
        X = [X0, X1]
        s0 = place("s0", [P, 2, NB, P], 0)
        att_hl = place("att_hl", [P, 2, 4, T], o_tok, f32r)
        rec_hl = place("rec_hl", [P, 2, 4, T], o_tok + 8 * TB, f32r)
        v_tok = place("v_tok", [P, 5, 512], o_tok + 8 * TB)
        decayed = place("decayed", [P, 2, 512], o_tok + 8 * TB + 10240)
        v_s = place("v_s", [NB, 512], o_tok + 8 * TB + 14336)
        k_s = place("k_s", [NB, 512], 8 * TB + 4 * TP * 4)
        o_A = o_tok + 16 * TB
        Asc = place("Asc", [P, 4, 512], o_A)
        Atail = place("Atail", [16, 4, 16], o_A + 8192)
        v_blk = place("v_blk", [NB, NB, P], o_A + 8448)
        merged = place("merged", [P, 2, KT, T], 0, f32r)
        gate_s = place("gate_s", [P, 2, T], 16 * TB)
        mix = place("mix", [P, 2, T], 18 * TB)
        hidden = place("hidden", [P, 2, 12, T], 0, f32r)
        silu = place("silu", [P, T], 24 * TB)
        act_f = place("act_f", [P, T], 25 * TB)
        x_rows = place("x_rows", [P, 5, DM], 0)
        y_rows = place("y_rows", [P, 2, DM], 12 * TB)
        level_f = place("level_f", [P, 8, P], 12 * TB)

        acc = [ctx.enter_context(nc.psum_tensor(f"acc{i}", [P, 2, 512], f32)) for i in range(2)]
        work = [ctx.enter_context(nc.psum_tensor(f"work{i}", [P, 1024], f32)) for i in range(2)]

        def pair(w):
            return w[:, :].rearrange("p (a b) -> p a b", a=2)[:, :, 0:HT]

        def halves(ap):
            return ap.rearrange("p (a b) -> p a b", a=2)

        def C(name, rows=None):
            at, r, c = where[name]
            return cst[0:(rows or r), at:at + c]

        raw_ready = [sem(f"raw_ready{i}") for i in range(4)]
        hi_done, lo_done = sem("hi_done"), sem("lo_done")
        unit_done = sem("unit_done")
        taken = [sem(f"taken{i}") for i in range(2)]
        filled = [sem(f"filled{i}") for i in range(2)]
        drained = [sem(f"drained{i}") for i in range(2)]
        S = {n: sem(n) for n in (
            "vector_order scalar_order gpsimd_order loads_ready x_landed x_ready par_ready squares squares_used "
            "normed_f normed_hi normed_lo qk_squares qk_normed roped dup_landed ki_dup_landed rope_landed "
            "page_rows_ready pages_gathered0 pages_gathered1 pages_used key_turned index_done dots_done topk sample_topk found_part bounds_exp x_turned "
            "scores_sent scores_landed weights_ready "
            "masks_ready setup picks_ready rows_ready k_gathered v_gathered row_mask exps probs att_hi att_lo q_sel_ready "
            "sel_scores sel_exp sel_probs_ready sel_turned_ready sel_out att_ready tok_stored "
            "forget log_forget decay_sum lev_diff lev_exp lev_ready q_decayed decay_last k_exp k_decayed state_ready state_stored "
            "v_blk_ready s0_landed0 s0_landed1 s0_ready s0_stored rec_squares rec_f rec_hi rec_lo mixed merged_hi merged_lo "
            "x_updated silu_done act_done hid_hi hid_lo layer_begun held y_ready y_stored0 y_stored1").split()}

        NORMS = 2

        def wait(eng, name, L, per, n):
            eng.wait_ge(S[name], L * per + n)

        def hold(eng):
            eng.sem_inc(S["held"], 1)

        def slot_of(item):
            return ITEM[item] % 2

        def wait_filled(eng, L, item):
            eng.wait_ge(filled[ITEM[item] % 2], L * (ITEMS // 2) + ITEM[item] // 2 + 1)
            return work[ITEM[item] % 2][:, :]

        def wait_drained(eng, L, item):
            eng.wait_ge(drained[ITEM[item] % 2], L * (ITEMS // 2) + ITEM[item] // 2 + 2)

        class Order:

            def __init__(self, eng, s, L, per):
                self.eng, self.s, self.L, self.per, self.n = eng, s, L, per, 0

            def __call__(self, ins):
                ins.then_inc(self.s, 1)
                self.n += 1

            def settle(self):
                self.eng.wait_ge(self.s, self.L * self.per + self.n)

            def end(self, start=0):
                assert self.n == self.per, ("signals a layer", self.n, "declared", self.per)

        VEC, SCA = t["steps"]

        def wait_unit(eng, L, u):
            eng.wait_ge(unit_done, L * UNITS + u + 3)

        def take(ins, o):
            ins.then_inc(taken[o % 2], 1)

        def store_state(sync, L, h):
            wait(sync, "s0_ready", L, 32, 8 * h + 8)
            sync.dma_start(out[9][ds(L, 1), :, h, :, :].rearrange("l b k v -> k (l b) v"), s0[:, h % 2, :, :])\
                .then_inc(S["s0_stored"], 16)

        def relu_buf(m, n, w):
            return relu[0:n, m % 2, 0:w]

        block = ctx.enter_context(nc.Block())

        @block.sync
        def _(sync):
            sync.sem_inc(hi_done, 4)
            sync.sem_inc(lo_done, 4)
            sync.sem_inc(unit_done, 2)
            sync.sem_inc(S["x_updated"], 1)
            sync.sem_inc(S["state_stored"], 16)
            for i in range(2):
                sync.sem_inc(taken[i], 1)
                sync.sem_inc(drained[i], 1)
            sync.dma_start(x_rows[0:META, 0, :], t["meta_tokens"]).then_inc(S["x_landed"], 16)
            xp = t["x_prompt"][0]
            sync.dma_start(x_rows[META:P, 0, :], xp[0:P - META, :]).then_inc(S["x_landed"], 16)
            sync.dma_start(x_rows[:, 1:4, :], xp[112:496, :].rearrange("(j p) d -> p j d", p=P)).then_inc(S["x_landed"], 16)
            sync.dma_start(x_rows[0:16, 4, :], xp[496:512, :]).then_inc(S["x_landed"], 16)
            sync.dma_start(x_rows[16:24, 4, :], t["x_sample"][:, 0, :]).then_inc(S["x_landed"], 16)
            sync.dma_start(cst[:, :], csts[:, 0:t["resident"]]).then_inc(S["loads_ready"], 16)
            sync.dma_start(level_f[:, :, :], t["levels"]).then_inc(S["loads_ready"], 16)
            pt = t["page_table"]
            sync.dma_start(pages_i[:, :], pt.rearrange("b (g o) -> (b g) o", o=1)).then_inc(S["loads_ready"], 16)
            sync.dma_start(table_i[:, :], pt).then_inc(S["loads_ready"], 16)
            for l in range(DEPTH):
                for at, src, n in ((0, t["norm_mix"][l], KT), (8, t["norm_ffn"][l], KT), (18, t["rec_norm"][l], 1),
                                   (19, t["lb_raw"][l], 4)):
                    sync.dma_start(params[:, l, at:at + n], src.rearrange("(k p) -> p k", p=P),
                                   allow_slow_non_contiguous=True).then_inc(S["loads_ready"], 16)
                for at, src in ((16, t["q_norm"][l]), (17, t["k_norm"][l])):
                    for half in range(2):
                        sync.dma_start(params[64 * half:64 * half + 64, l, at:at + 1],
                                       src.rearrange("(p o) -> p o", o=1)).then_inc(S["loads_ready"], 16)

            with sync.Fori(0, DEPTH) as L:
                def load(u, q, slot, src, kt):
                    sync.wait_ge(hi_done, L * UNITS + u + 1)
                    sync.wait_ge(lo_done, L * UNITS + u + 1)
                    if isinstance(u, int):
                        hold(sync)
                    sync.dma_start(raw[slot][:, 0:kt, :], src).then_inc(raw_ready[slot], 16)

                def cols(w, col, lo=0, kt=KT):
                    return w[ds(L, 1), lo * P:(lo + kt) * P, ds(col, P)].rearrange("l (k p) n -> p (l k) n", p=P)

                first = where["cos"][0]
                sync.wait_ge(S["layer_begun"], L + 1)
                hold(sync)
                sync.dma_start(rope[:, :, :], csts[:, first:first + 2 * T].rearrange("p (a t) -> p a t", a=2))\
                    .then_inc(S["rope_landed"], 16)
                for n, tile in enumerate(A_TILES):
                    load(n, n // 4, n % 4, cols(t["w_in"], tile * P), KT)
                for n in range(13, 16):
                    sync.wait_ge(lo_done, L * UNITS + n + 1)
                    sync.sem_inc(raw_ready[n % 4], 16)
                with sync.Fori(0, 4) as g:
                    for i in range(4):
                        load(UB + g * 4 + i, UB // 4 + g, i, cols(t["w_in"], 1608 + g * 512 + i * P), KT)
                wait_drained(sync, L, ("tokens", 4))
                wait_drained(sync, L, ("tokens", 3))
                kp, vp, kip, ksm, vsm, kism = out[2], out[3], out[4], out[6], out[7], out[8]
                for dst, lo, n in ((kp, 0, 256), (vp, 256, 256), (kip, 512, 64)):
                    d = dst[ds(L, 1), 0, :, :].rearrange("l t c -> (l t) c")
                    sync.dma_start(d[0:512, :].rearrange("(j p) c -> p j c", p=P), tok[:, 0:4, lo:lo + n])\
                        .then_inc(S["tok_stored"], 16)
                    sync.dma_start(d[512:528, :], tok[0:16, 4, lo:lo + n]).then_inc(S["tok_stored"], 16)
                for dst, lo, n in ((ksm, 0, 256), (vsm, 256, 256), (kism, 512, 64)):
                    sync.dma_start(dst[ds(L, 1), :, 0, :].rearrange("l b c -> (l b) c"), tok[16:24, 4, lo:lo + n])\
                        .then_inc(S["tok_stored"], 16)
                for h in range(4):
                    if h < 2:
                        wait_filled(sync, L, ("decayed", 4))
                    else:
                        sync.wait_ge(S["s0_stored"], L * 64 + 16 * (h - 1))
                        hold(sync)
                        wait_filled(sync, L, ("rec_sample", h - 2))
                        hold(sync)
                    sync.dma_start(s0[:, h % 2, :, :],
                                   t["state_rec"][ds(L, 1), :, h, :, :].rearrange("l b k v -> k (l b) v"))\
                        .then_inc(S[f"s0_landed{h % 2}"], 16)
                    if h == 0:
                        wait(sync, "state_ready", L, 20, 20)
                        sync.dma_start(out[5][ds(L, 1), 0, :, :, :].rearrange("l h k v -> k (l h) v"), state[:, :, :])\
                            .then_inc(S["state_stored"], 16)
                    if h >= 1:
                        store_state(sync, L, h - 1)
                store_state(sync, L, 3)
                hold(sync)
                with sync.Fori(0, KT) as g:
                    load(UM + g * 4, UM // 4 + g, 0, cols(t["w_in"], 3656 + g * P), KT)
                    load(UM + g * 4 + 1, UM // 4 + g, 1, cols(t["w_in"], 4680 + g * P), KT)
                    load(UM + g * 4 + 2, UM // 4 + g, 2, cols(t["w_pa"], g * P, 0, 4), 4)
                    load(UM + g * 4 + 3, UM // 4 + g, 3, cols(t["w_pb"], g * P, 0, 4), 4)
                with sync.Fori(0, 2) as g:
                    for i in range(4):
                        load(UO + g * 4 + i, UO // 4 + g, i, cols(t["w_o"], g * 512 + i * P), KT)
                for part in range(2):
                    n0 = 12 * part
                    with sync.Fori(0, HID[part] // 2) as g:
                        for i in range(4):
                            col = (i % 2) * DFF + (n0 + i // 2) * P
                            load(UG[part] + g * 4 + i, UG[part] // 4 + g, i, cols(t["w_gu"], g * 256 + col), KT)
                    kt = HID[part] // 2
                    with sync.Fori(0, 4) as g:
                        for i in range(4):
                            load(UD[part] + g * 4 + i, UD[part] // 4 + g, i,
                                 cols(t["w_down"], g * 256 + (i // 2) * P, n0 + kt * (i % 2), kt), kt)
                sync.wait_ge(S["tok_stored"], L * 144 + 144)
                hold(sync)
            for j, (r0, n) in enumerate(TILES_ALL):
                sync.wait_ge(S["y_ready"], j + 1)
                if j == 0:
                    sync.dma_start(out[0][0, 0:112, :], y_rows[16:128, 0, :]).then_inc(S[f"y_stored{j % 2}"], 16)
                elif j < 4:
                    sync.dma_start(out[0][0, 128 * j - 16:128 * j + 112, :], y_rows[:, j % 2, :])\
                        .then_inc(S[f"y_stored{j % 2}"], 16)
                else:
                    sync.dma_start(out[0][0, 496:512, :], y_rows[0:16, 0, :]).then_inc(S[f"y_stored{j % 2}"], 16)
                    sync.dma_start(out[1][:, 0, :], y_rows[16:24, 0, :]).then_inc(S[f"y_stored{j % 2}"], 16)
            sync.wait_ge(S["y_stored0"], 64)
            sync.wait_ge(S["y_stored1"], 32)
            sync.wait_ge(S["s0_stored"], 64 * DEPTH)
            sync.wait_ge(S["state_stored"], 16 * DEPTH + 16)

        @block.gpsimd
        def _(pool):
            pool.wait_ge(S["par_ready"], 1)
            with pool.Fori(0, DEPTH) as L:
                def split(u, q, slot, kt):
                    s = slot % 2
                    pool.wait_ge(raw_ready[slot], L * (UNITS // 4 * 16) + q * 16 + 16)
                    pool.wait_ge(unit_done, L * UNITS + u + 1)
                    hold(pool)
                    pool.tensor_copy(w_hi[s][:, 0:kt, :], raw[slot][:, 0:kt, :]).then_inc(hi_done, 1)
                    pool.wait_ge(hi_done, L * UNITS + u + 5)
                    pool.tensor_tensor(w_lo[s][:, 0:kt, :], raw[slot][:, 0:kt, :], w_hi[s][:, 0:kt, :].bitcast(f32),
                                       ALU.subtract).then_inc(lo_done, 1)

                pool.wait_ge(S["page_rows_ready"], L * 8 + 8)
                pages = t["cache_idx_k"].rearrange("l g (q s) d -> (l g q) (s d)", q=4)

                def gather_pages(q):
                    if q >= 2:
                        wait(pool, "pages_used", L, 4, q - 1)
                    hold(pool)
                    pool.indirect_dma_start(idx_pages[:, q % 2, :], None, pages,
                                            bass.IndirectOffsetOnAxis(page_rows[:, q:q + 1].bitcast(u32), 0))\
                        .then_inc(S[f"pages_gathered{q % 2}"], 16)

                gather_pages(0)
                gather_pages(1)
                for n in range(13):
                    split(n, n // 4, n % 4, KT)
                pool.wait_ge(raw_ready[1], L * (UNITS // 4 * 16) + 3 * 16 + 16)
                pool.wait_ge(raw_ready[2], L * (UNITS // 4 * 16) + 3 * 16 + 16)
                pool.wait_ge(raw_ready[3], L * (UNITS // 4 * 16) + 3 * 16 + 16)
                hold(pool)
                pool.drain().then_inc(hi_done, 3)
                pool.drain().then_inc(lo_done, 3)
                gather_pages(2)
                gather_pages(3)
                with pool.Fori(0, 4) as g:
                    for i in range(4):
                        split(UB + g * 4 + i, UB // 4 + g, i, KT)
                wait(pool, "rows_ready", L, 2, 1)
                hold(pool)
                for src, dst, done in ((t["cache_k"], k_sel, "k_gathered"), (t["cache_v"], v_sel, "v_gathered")):
                    rows = src.rearrange("l g s n d -> (l g s) (n d)")
                    for i in range(16):
                        pool.indirect_dma_start(dst[:, i, :], None, rows,
                                                bass.IndirectOffsetOnAxis(row_idx[:, i:i + 1].bitcast(u32), 0))\
                            .then_inc(S[done], 16)
                with pool.Fori(0, KT) as g:
                    for i in range(4):
                        split(UM + g * 4 + i, UM // 4 + g, i, KT if i < 2 else 4)
                with pool.Fori(0, 2) as g:
                    for i in range(4):
                        split(UO + g * 4 + i, UO // 4 + g, i, KT)
                for part in range(2):
                    with pool.Fori(0, HID[part] // 2) as g:
                        for i in range(4):
                            split(UG[part] + g * 4 + i, UG[part] // 4 + g, i, KT)
                    with pool.Fori(0, 4) as g:
                        for i in range(4):
                            split(UD[part] + g * 4 + i, UD[part] // 4 + g, i, HID[part] // 2)

        @block.tensor
        def _(pe):
            ident = C("ident")

            def transpose(dst, src):
                k = src.shape[0]
                return pe.transpose(dst, src, ident[0:k, 0:k])

            pe.wait_ge(S["loads_ready"], 320)
            pe.wait_ge(S["x_landed"], 80)
            for k in range(KT):
                if k >= 2:
                    pe.wait_ge(S["x_ready"], k - 1)
                for j, (r0, n) in enumerate(TILES_ALL):
                    mm = transpose(acc[k % 2][:, :, :].rearrange("p a b -> p (a b)")[:, r0:r0 + n],
                                   x_rows[0:n, j, k * P:(k + 1) * P])
                mm.then_inc(S["x_turned"], 1)
            with pe.Fori(0, DEPTH) as L:
                def begin(item):
                    pe.wait_ge(drained[slot_of(item)], L * (ITEMS // 2) + ITEM[item] // 2 + 1)
                    return work[slot_of(item)][:, :]

                def finish(mm, item):
                    mm.then_inc(filled[slot_of(item)], 1)

                def unit(u, s, kt, mov, k0, o, q, start=True, stop=True):
                    pe.wait_ge(lo_done, L * UNITS + u + 5)
                    if start:
                        pe.wait_ge(taken[o], L * (OUTS // 2) + q + 1)
                    n = 0
                    for k in range(kt):
                        for w, part in ((w_hi, 0), (w_hi, 1), (w_lo, 0)):
                            for half in range(2):
                                mm = pe.matmul(acc[o][:, half, 0:HT], w[s][:, k, :],
                                               mov[:, part, k0 + k, half * HT:(half + 1) * HT],
                                               start=start and n == 0, stop=stop and n == 3 * kt - 1)
                            n += 1
                    mm.then_inc(unit_done, 1)

                def norm(item, w):
                    ps = begin(item)
                    for k in range(KT):
                        wait(pe, "squares", L, NORMS * KT, w * KT + k + 1)
                        for half in range(2):
                            mm = pe.matmul(pair(ps)[:, half, :], C("ones"), sq[:, k % 2, half * HT:(half + 1) * HT],
                                           start=k == 0, stop=k == KT - 1)
                        if k < KT - 1:
                            mm.then_inc(S["squares_used"], 1)
                    finish(mm, item)
                    wait(pe, "normed_lo", L, NORMS * KT, w * KT + KT)
                    wait(pe, "normed_hi", L, NORMS * KT, w * KT + KT)
                    hold(pe)

                norm("norm1", 0)
                with pe.Fori(0, 6) as g:
                    for i in range(2):
                        unit(UA + g * 2 + i, i, KT, normed, 0, i, g)
                unit(12, 0, KT, normed, 0, 0, 6)
                pe.drain().then_inc(unit_done, 3)

                def rope_item(n):
                    ps = begin(("rope", n))
                    if n < 6:
                        wait(pe, "qk_normed", L, 6, order.index(n) + 1)
                    else:
                        pe.wait_ge(taken[0], L * (OUTS // 2) + 8)
                        pe.wait_ge(taken[1], L * (OUTS // 2) + 8)
                    for half in range(2):
                        mm = pe.matmul(pair(ps)[:, half, :], C("rot"), A[:, n, half * HT:(half + 1) * HT],
                                       start=True, stop=True)
                    finish(mm, ("rope", n))

                def sumsq_item(item, count, per, mat, slot, name):
                    ps = begin(item)
                    wait(pe, name, L, per, count)
                    for half in range(2):
                        mm = pe.matmul(pair(ps)[:, half, :], C(mat), sq[:, slot, half * HT:(half + 1) * HT],
                                       start=True, stop=True)
                    finish(mm, item)

                for n in (12, 8, 9, 10, 11):
                    rope_item(n)
                sumsq_item(("sumsq", 4), 1, 6, "head_ones", 0, "qk_squares")
                for m, n in enumerate(order):
                    if m < 5:
                        sumsq_item(("sumsq", order[m + 1]), m + 2, 6, "head_ones", (m + 1) % 2, "qk_squares")
                    rope_item(n)

                wait(pe, "roped", L, 11, 11)
                ps = begin("sample_tokens")
                for m, n in enumerate((6, 7, 12)):
                    mm = transpose(ps[0:NB, m * P:(m + 1) * P], A[:, n, TP:T])
                finish(mm, "sample_tokens")
                for j, (r0, n) in enumerate(TILES_ALL):
                    ps = begin(("tokens", j))
                    for m, a in enumerate((4, 5, 6, 7, 12)):
                        mm = transpose(ps[0:n, m * P:(m + 1) * P], A[:, a, r0:r0 + n])
                    finish(mm, ("tokens", j))
                ps = begin("swapped")
                pe.matmul(ps[:, 0:32], C("swap"), A[:, 0:4, TP:T], start=True, stop=True)
                mm = pe.matmul(ps[:, 32:64], C("swap"), A[:, 8:12, TP:T], start=True, stop=True)
                finish(mm, "swapped")
                ps = begin("index_weights")
                wait_drained(pe, L, "sample_tokens")
                mm = pe.matmul(ps[:, 0:8], C("row_page"), s_tok[:, 320:328], start=True, stop=True)
                finish(mm, "index_weights")
                ps = begin("new_key_dots")
                wait(pe, "weights_ready", L, 9, 4)
                hold(pe)
                mm = pe.matmul(ps[0:NB, 0:64], A[0:64, 12, TP:T], q_idx[0:64, 0:64], start=True, stop=True)
                finish(mm, "new_key_dots")

                def key_turn(r):
                    ps = begin(("key_turn", r))
                    q = r // 2
                    pe.wait_ge(S[f"pages_gathered{q % 2}"], L * 32 + 16 * (q // 2) + 16)
                    for m in range(8):
                        lo = (r % 2) * 1024 + m * P
                        mm = transpose(ps[:, m * P:(m + 1) * P], idx_pages[:, q % 2, lo:lo + P])
                    finish(mm, ("key_turn", r))

                def key_dots(r):
                    ps = begin(("key_dots", r))
                    wait_drained(pe, L, ("key_turn", r))
                    for m in range(8):
                        mm = pe.matmul(ps[:, m * P:(m + 1) * P], idx_turned[:, r % 2, m * P:(m + 1) * P], q_idx[:, :],
                                       start=True, stop=True)
                    finish(mm, ("key_dots", r))

                key_turn(0)
                for r in range(8):
                    if r < 7:
                        key_turn(r + 1)
                    key_dots(r)
                pe.wait_ge(S["ki_dup_landed"], L * 16 + 16)
                for j in range(1, 5):
                    r0, n = TILES[j]
                    for h in range(8):
                        ps = begin(("dots", j, h))
                        hold(pe)
                        p0 = 64 * (h % 2)
                        key = A[0:64, 12, :] if p0 == 0 else ki_dup[64:128, :]
                        for c in range(0, WIDTH[j], 512):
                            w = min(512, WIDTH[j] - c)
                            mm = pe.matmul(ps[0:n, c:c + w], A[p0:p0 + 64, 8 + h // 2, r0:r0 + n], key[:, c:c + w],
                                           start=True, stop=True)
                        finish(mm, ("dots", j, h))
                with pe.Fori(0, 8) as g:
                    for i in range(2):
                        unit(UB + g * 2 + i, i, KT, normed, 0, i, OB // 2 + g)

                pe.wait_ge(S["dup_landed"], L * 64 + 64)
                count = 0

                def qk(h, j):
                    r0, n = TILES[j]
                    ps = begin(("qk", h, j))
                    hold(pe)
                    kv, p0 = h // 2, 64 * (h % 2)
                    key = A[p0:p0 + 64, 4 + kv // 2, :] if 64 * (kv % 2) == p0 else k_dup[p0:p0 + 64, kv // 2, :]
                    for c in range(0, WIDTH[j], 512):
                        w = min(512, WIDTH[j] - c)
                        mm = pe.matmul(ps[0:n, c:c + w], A[p0:p0 + 64, h // 2, r0:r0 + n], key[:, c:c + w],
                                       start=True, stop=True)
                    finish(mm, ("qk", h, j))

                def turn(h, j):
                    r0, n = TILES[j]
                    e = (h // 2) * 10 + j * 2 + h % 2
                    ps = begin(("turn", h, j))
                    wait(pe, "probs", L, 40, e + 1)
                    hold(pe)
                    for c in range(j + 1):
                        w = min(P, WIDTH[j] - c * P)
                        mm = transpose(ps[0:w, c * P:c * P + n], E[0:n, h % 2, c * P:c * P + w])
                    finish(mm, ("turn", h, j))

                def pv(n2, j):
                    r0, n = TILES[j]
                    ps = begin(("pv", n2, j))
                    for s in range(2):
                        h = 2 * n2 + s
                        wait_drained(pe, L, ("turn", h, j))
                        for c in range(j + 1):
                            w = min(P, WIDTH[j] - c * P)
                            mm = pe.matmul(ps[64 * s:64 * s + 64, 0:n], tok[0:w, c, 256 + n2 * 64:320 + n2 * 64],
                                           pT[0:w, s, c, 0:n], start=c == 0, stop=c == j)
                    finish(mm, ("pv", n2, j))

                for n2 in range(4):
                    for j in range(5):
                        qk(2 * n2, j)
                        qk(2 * n2 + 1, j)
                        turn(2 * n2, j)
                        turn(2 * n2 + 1, j)
                        pv(n2, j)

                ps = begin("rows_turn")
                wait(pe, "picks_ready", L, 2, 2)
                hold(pe)
                for m, what in enumerate((2, 3)):
                    for half in range(2):
                        mm = transpose(ps[:, m * 16 + half * 8:m * 16 + half * 8 + 8],
                                       pick_f[:, what, half * P:(half + 1) * P])
                finish(mm, "rows_turn")
                pe.wait_ge(S["k_gathered"], L * 256 + 256)

                def sel_turn(r):
                    ps = begin(("sel_turn", r))
                    for m in range(8):
                        mm = transpose(ps[:, m * P:(m + 1) * P], k_sel[:, r * 4 + m // 2, (m % 2) * P:(m % 2) * P + P])
                    finish(mm, ("sel_turn", r))

                def sel_dots(r):
                    ps = begin(("sel_dots", r))
                    wait_drained(pe, L, ("sel_turn", r))
                    wait(pe, "q_sel_ready", L, 4, 4)
                    for m in range(8):
                        i, pr = r * 4 + m // 2, m % 2
                        mm = pe.matmul(ps[:, m * 4:m * 4 + 4], sel_turned[:, r % 2, m * P:(m + 1) * P],
                                       q_sel[:, pr, i % 8, 4 * pr:4 * pr + 4], start=True, stop=True)
                    finish(mm, ("sel_dots", r))

                sel_turn(0)
                sel_turn(1)
                sel_dots(0)
                sel_turn(2)
                sel_dots(1)
                sel_turn(3)
                sel_dots(2)
                sel_dots(3)
                ps = begin("sel_rows")
                wait(pe, "sel_scores", L, 1, 1)
                hold(pe)
                for half in range(2):
                    transpose(ps[0:64, half * P:(half + 1) * P], sel_s[:, half, :])
                for pr in range(2):
                    pe.matmul(ps[0:64, 512:520], q_sel[:, pr, :, :], A[:, 4 + pr, TP:T], start=pr == 0, stop=pr == 1)
                mm = pe.matmul(ps[0:64, 520:521], C("row_head"), flag[:, :], start=True, stop=True)
                finish(mm, "sel_rows")
                ps = begin("sel_probs")
                wait(pe, "sel_probs_ready", L, 2, 2)
                hold(pe)
                for half in range(2):
                    transpose(ps[:, half * 64:half * 64 + 64], sel_p[:, half * P:(half + 1) * P])
                mm = transpose(ps[0:NB, 128:192], sel_new[:, :])
                finish(mm, "sel_probs")
                ps = begin("sel_pv")
                wait_drained(pe, L, "sel_probs")
                pe.wait_ge(S["v_gathered"], L * 256 + 256)
                for pr in range(2):
                    pe.matmul(ps[:, pr * 32:pr * 32 + 32], s_tok[:, pr * P:pr * P + P],
                              sel_pT[0:NB, 128:192].rearrange("p (b h) -> p b h", h=8)[:, :, 4 * pr:4 * pr + 4],
                              start=pr == 0, stop=False, skip_group_check=True)
                for i in range(16):
                    half, b = i // 8, i % 8
                    for pr in range(2):
                        mm = pe.matmul(ps[:, pr * 32 + b * 4:pr * 32 + b * 4 + 4], v_sel[:, i, pr * P:(pr + 1) * P],
                                       sel_pT[:, half * 64 + b * 8 + 4 * pr:half * 64 + b * 8 + 4 * pr + 4],
                                       start=False, stop=i == 15, skip_group_check=True)
                finish(mm, "sel_pv")
                ps = begin("sel_swap")
                wait_drained(pe, L, "sel_pv")
                mm = pe.matmul(ps[:, 0:64], C("swap"), sel_o[:, :, :, :].rearrange("p a b c -> p (a b c)"),
                               start=True, stop=True)
                finish(mm, "sel_swap")

                for lev in range(8):
                    if lev < 7:
                        wait(pe, "lev_ready", L, 14, 2 * lev + 2)
                        left = right = X[lev % 2]
                    else:
                        left, right = K, B
                    for hp in range(2):
                        ps = begin(("level", lev, hp))
                        for m in range(8):
                            h, c = 2 * hp + m // 4, m % 4
                            mm = pe.matmul(ps[:, m * P:(m + 1) * P], left[:, h, c * P:(c + 1) * P],
                                           right[:, h, c * P:(c + 1) * P], start=True, stop=True)
                        finish(mm, ("level", lev, hp))
                    if lev >= 3:
                        ps = begin(("level_tail", lev))
                        for h in range(4):
                            mm = pe.matmul(ps[0:16, h * 16:h * 16 + 16], left[:, h, 512:528], right[:, h, 512:528],
                                           start=True, stop=True)
                        finish(mm, ("level_tail", lev))
                for c in range(5):
                    r0, n = TILES[c]
                    ps = begin(("v_turn", c))
                    for h in range(4):
                        mm = transpose(ps[0:n, h * P:(h + 1) * P], B[:, 8 + h, r0:r0 + n])
                    finish(mm, ("v_turn", c))
                ps = begin("v_sample")
                for h in range(4):
                    mm = transpose(ps[0:NB, h * P:(h + 1) * P], B[:, 8 + h, TP:T])
                finish(mm, "v_sample")
                ps = begin("k_sample")
                for h in range(4):
                    mm = transpose(ps[0:NB, h * P:(h + 1) * P], K[:, h, TP:T])
                finish(mm, "k_sample")
                for c in range(5):
                    r0, n = TILES[c]
                    ps = begin(("decayed", c))
                    wait(pe, "k_decayed", L, 1, 1)
                    for h in range(4):
                        mm = transpose(ps[0:n, h * P:(h + 1) * P], X1[:, h, r0:r0 + n])
                    finish(mm, ("decayed", c))
                    ps = begin(("rec_out", c))
                    wait(pe, "q_decayed", L, 1, 1)
                    wait(pe, "state_ready", L, 20, 4 * c) if c else wait(pe, "forget", L, 9, 9)
                    for h in range(4):
                        a = Asc[:, h, c * P:(c + 1) * P] if c < 4 else Atail[:, h, :]
                        pe.matmul(ps[:, h * P:h * P + n], v_tok[0:n, c, h * P:(h + 1) * P], a, start=True, stop=False)
                        mm = pe.matmul(ps[:, h * P:h * P + n], state[:, h, :], X0[:, h, r0:r0 + n], start=False, stop=True)
                    finish(mm, ("rec_out", c))
                    ps = begin(("state", c))
                    wait_drained(pe, L, ("decayed", c))
                    for h in range(4):
                        mm = pe.matmul(ps[:, h * P:(h + 1) * P], decayed[0:n, c % 2, h * P:(h + 1) * P],
                                       v_tok[0:n, c, h * P:(h + 1) * P], start=True, stop=True)
                    finish(mm, ("state", c))
                wait_drained(pe, L, "k_sample")
                for h in range(4):
                    ps = begin(("rank1", h))
                    wait(pe, "v_blk_ready", L, 4, h + 1)
                    for half in range(2):
                        mm = pe.matmul(ps[:, half * 512:(half + 1) * 512], k_s[:, h * P:(h + 1) * P],
                                       v_blk[:, half * 4:half * 4 + 4, :], start=True, stop=True)
                    finish(mm, ("rank1", h))
                    ps = begin(("rec_sample", h))
                    wait(pe, "s0_ready", L, 32, 8 * h + 8)
                    for b in range(NB):
                        mm = pe.matmul(ps[:, b:b + 1], s0[:, h % 2, b, :], B[:, h, TP + b:TP + b + 1], start=True, stop=True)
                    finish(mm, ("rec_sample", h))
                for h in range(4):
                    sumsq_item(("rec_sumsq", h), h + 1, 4, "ones", h % 2, "rec_squares")

                wait(pe, "att_hi", L, 4, 4)
                wait(pe, "att_lo", L, 4, 4)
                wait(pe, "rec_hi", L, 4, 4)
                wait(pe, "rec_lo", L, 4, 4)
                hold(pe)
                with pe.Fori(0, KT) as g:
                    unit(UM + g * 4, 0, KT, normed, 0, 0, OM // 2 + g * 2)
                    unit(UM + g * 4 + 1, 1, KT, normed, 0, 1, OM // 2 + g * 2)
                    unit(UM + g * 4 + 2, 0, 4, att_hl, 0, 0, OM // 2 + g * 2 + 1)
                    unit(UM + g * 4 + 3, 1, 4, rec_hl, 0, 1, OM // 2 + g * 2 + 1)
                wait(pe, "merged_hi", L, 8, 8)
                wait(pe, "merged_lo", L, 8, 8)
                hold(pe)
                with pe.Fori(0, 4) as g:
                    for i in range(2):
                        unit(UO + g * 2 + i, i, KT, merged, 0, i, OO // 2 + g)
                norm("norm2", 1)
                for part in range(2):
                    with pe.Fori(0, HID[part]) as g:
                        for i in range(2):
                            unit(UG[part] + g * 2 + i, i, KT, normed, 0, i, OG[part] // 2 + g)
                    kt = HID[part] // 2
                    wait(pe, "hid_lo", L, 22, 12 if part == 0 else 22)
                    wait(pe, "hid_hi", L, 22, 12 if part == 0 else 22)
                    hold(pe)
                    with pe.Fori(0, 4) as g:
                        for i in range(4):
                            unit(UD[part] + g * 4 + i, i % 2, kt, hidden, kt * (i % 2), i // 2, OD[part] // 2 + g,
                                 start=i % 2 == 0, stop=i % 2 == 1)
                if ITEM.get("none") is not None:
                    pe.wait_ge(drained[1], L * (ITEMS // 2) + ITEMS // 2)
                    pe.drain().then_inc(filled[1], 1)
            pe.wait_ge(S["x_updated"], 24 * DEPTH + 1)
            for j, (r0, n) in enumerate(TILES_ALL):
                pe.wait_ge(drained[j % 2], DEPTH * (ITEMS // 2) + j // 2 + 1)
                for k in range(KT):
                    mm = transpose(work[j % 2][0:n, k * P:(k + 1) * P], x[:, k, r0:r0 + n])
                mm.then_inc(filled[j % 2], 1)

        @block.scalar
        def _(act):
            for k in range(KT):
                act.wait_ge(S["x_turned"], k + 1)
                act.activation(x[:, k, :], acc[k % 2][:, :, :].rearrange("p a b -> p (a b)")[:, 0:T], ACT.Copy)\
                    .then_inc(S["x_ready"], 1)
            act.wait_ge(S["setup"], 1)
            act.wait_ge(S["loads_ready"], 320)
            act.wait_ge(S["masks_ready"], 2)
            act.wait_ge(S["x_ready"], KT)
            act.activation(lb_tmp[:, 2:4, :], lb_tmp[:, 0:2, :], ACT.Exp).then_inc(S["bounds_exp"], 1)
            with act.Fori(0, DEPTH) as L:
                so = Order(act, S["scalar_order"], L, SCA)

                def drain_to(dst, item, func=ACT.Copy, src=None, **kw):
                    ps = wait_filled(act, L, item)
                    act.activation(dst, ps if src is None else src, func, **kw).then_inc(drained[slot_of(item)], 1)

                def norm(item, w):
                    if w == 0:
                        act.wait_ge(S["x_updated"], L * 24 + 1)
                    for k in range(KT):
                        if w == 1:
                            wait(act, "x_updated", L, 24, k + 2)
                        else:
                            act.wait_ge(S["rope_landed"], L * 16 + 16)
                        if k >= 2:
                            act.wait_ge(S["squares_used"], L * (2 * (KT - 1)) + w * (KT - 1) + k - 1)
                        act.activation(sq[:, k % 2, :], x[:, k, :], ACT.Square).then_inc(S["squares"], 1)
                    drain_to(halves(std[:, :]), item, ACT.Sqrt, pair(work[slot_of(item)]), scale=1.0 / DM, bias=eps[:, 0:1])
                    for k in range(KT):
                        wait(act, "normed_f", L, NORMS * KT, w * KT + k + 1)
                        act.activation(normed[:, 0, k, :], tmp[:, k % 2, :], ACT.Copy).then_inc(S["normed_hi"], 1)

                norm("norm1", 0)
                for n, tile in enumerate(A_TILES):
                    wait_unit(act, L, n)
                    take(act.activation(halves(A[:, tile, :]), acc[n % 2][:, :, 0:HT], ACT.Copy), n)
                act.drain().then_inc(taken[1], 1)
                def qk_square(m):
                    if m == 0:
                        act.wait_ge(taken[0], L * (OUTS // 2) + 8)
                        act.wait_ge(taken[1], L * (OUTS // 2) + 8)
                    else:
                        pass
                    if m >= 2:
                        wait_filled(act, L, ("sumsq", order[m - 2]))
                    act.activation(sq[:, m % 2, :], A[:, order[m], :], ACT.Square).then_inc(S["qk_squares"], 1)

                qk_square(0)
                qk_square(1)
                for m, n in enumerate(order):
                    if m >= 1:
                        wait(act, "qk_normed", L, 6, m)
                    drain_to(halves(std[:, :]), ("sumsq", n), ACT.Sqrt, pair(work[slot_of(("sumsq", n))]),
                             scale=1.0 / 64, bias=eps[:, 0:1])
                    if m + 2 < 6:
                        qk_square(m + 2)
                wait(act, "roped", L, 11, 11)
                act.dma_start(ki_dup[64:128, :], A[0:64, 12, :]).then_inc(S["ki_dup_landed"], 16)
                for m in range(2):
                    act.dma_start(k_dup[0:64, m, :], A[64:128, 4 + m, :]).then_inc(S["dup_landed"], 16)
                    act.dma_start(k_dup[64:128, m, :], A[0:64, 4 + m, :]).then_inc(S["dup_landed"], 16)
                drain_to(s_tok[:, :], "sample_tokens", src=work[slot_of("sample_tokens")][0:NB, 0:328])
                for j, (r0, n) in enumerate(TILES_ALL):
                    drain_to(tok[0:n, j, :], ("tokens", j), src=work[slot_of(("tokens", j))][0:n, 0:584])
                drain_to(swapped[:, :, :].rearrange("p a b -> p (a b)"), "swapped", src=work[slot_of("swapped")][:, 0:64])
                drain_to(new_tmp[:, :], "new_key_dots", ACT.Relu, work[slot_of("new_key_dots")][0:NB, 0:64])

                def key_turn(r):
                    if r >= 2:
                        wait_filled(act, L, ("key_dots", r - 2))
                    drain_to(idx_turned[:, r % 2, :], ("key_turn", r))

                def key_dots(r):
                    if r >= 2:
                        wait(act, "index_done", L, 9, r)
                    drain_to(idx_relu[:, r % 2, :], ("key_dots", r), ACT.Relu)

                key_turn(0)
                for r in range(8):
                    if r < 7:
                        key_turn(r + 1)
                    key_dots(r)
                wait(act, "index_done", L, 9, 9)
                act.dma_start(ss[:, 0:PAST].rearrange("b (g k) -> b g k", g=PAGES), sc_page[:, :])\
                    .then_inc(S["scores_landed"], 16)
                for j in range(1, 5):
                    n = TILES[j][1]
                    for h in range(8):
                        m = (j - 1) * 8 + h
                        if m >= 2:
                            wait(act, "dots_done", L, 32, m - 1)
                        w = WIDTH[j]
                        drain_to(relu_buf(m, n, w), ("dots", j, h), ACT.Relu, work[slot_of(("dots", j, h))][0:n, 0:w])
                wait(act, "index_done", L, 9, 9)
                for kind, func in enumerate((ACT.Silu, ACT.Sigmoid, ACT.Copy, ACT.Silu)):
                    for i in range(4):
                        n = kind * 4 + i
                        wait_unit(act, L, UB + n)
                        take(act.activation(halves(B[:, n, :]), acc[n % 2][:, :, 0:HT], func), OB + n)
                for n2 in range(4):
                    for j in range(5):
                        n, w = TILES[j][1], WIDTH[j]
                        for s in range(2):
                            e = n2 * 10 + j * 2 + s
                            wait(act, "row_mask", L, 40, e + 1)
                            act.activation(E[0:n, s, 0:w], E[0:n, s, 0:w], ACT.Exp, bias=row_st[0:n, s, 1:2],
                                           accum_out=row_st[0:n, s, 2:3]).then_inc(S["exps"], 1)
                        for s in range(2):
                            h = 2 * n2 + s
                            ps = wait_filled(act, L, ("turn", h, j))
                            if j < 4:
                                act.activation(pT[:, s, 0:j + 1, 0:n], ps[:, 0:(j + 1) * P].rearrange("p (c t) -> p c t", t=P),
                                               ACT.Copy).then_inc(drained[slot_of(("turn", h, j))], 1)
                            else:
                                so(act.activation(pT[:, s, 0:4, 0:n], ps[:, 0:512].rearrange("p (c t) -> p c t", t=P)[:, :, 0:n],
                                                  ACT.Copy))
                                act.activation(pT[0:16, s, 4, 0:n], ps[0:16, 512:512 + n], ACT.Copy)\
                                    .then_inc(drained[slot_of(("turn", h, j))], 1)
                        r0 = TILES[j][0]
                        drain_to(A[:, n2, r0:r0 + n], ("pv", n2, j), src=work[slot_of(("pv", n2, j))][:, 0:n])
                for r in range(4):
                    if r == 2:
                        wait_filled(act, L, ("sel_dots", 0))
                    if r == 3:
                        wait_filled(act, L, ("sel_dots", 1))
                    drain_to(sel_turned[:, r % 2, :], ("sel_turn", r))
                wait(act, "sel_exp", L, 1, 1)
                act.activation(sel_p[:, 0:257], sel_p[:, 0:257], ACT.Exp, bias=sel_c[:, 1:2], scale=ATT_SCALE,
                               accum_out=sel_c[:, 2:3]).then_inc(S["sel_out"], 1)
                for n in range(4):
                    wait(act, "att_ready", L, 4, 4)
                    act.wait_ge(S["tok_stored"], L * 144 + 144)
                    act.activation(att_hl[:, 0, n, :], A[:, n, :], ACT.Copy).then_inc(S["att_hi"], 1)
                for h in range(4):
                    wait(act, "forget", L, 9, 8)
                    act.activation(B[:, 4 + h, 0:TP], B[:, 4 + h, 0:TP], ACT.Ln).then_inc(S["log_forget"], 1)
                for lev, hs in enumerate(HALVES):
                    w = 512 if hs >= 16 else TP
                    wait(act, "lev_diff", L, 14, 2 * lev + 2)
                    act.activation(X[lev % 2][:, :, 0:w], X[lev % 2][:, :, 0:w], ACT.Exp).then_inc(S["lev_exp"], 1)
                for c in range(5):
                    n = TILES[c][1]
                    drain_to(v_tok[0:n, c, :], ("v_turn", c), src=work[slot_of(("v_turn", c))][0:n, 0:512])
                drain_to(v_s[:, :], "v_sample", src=work[slot_of("v_sample")][0:NB, 0:512])
                drain_to(k_s[:, :], "k_sample", src=work[slot_of("k_sample")][0:NB, 0:512])
                wait(act, "decay_sum", L, 20, 20)
                wait_filled(act, L, ("level_tail", 6))
                wait_filled(act, L, ("level", 6, 1))
                so(act.activation(last_decay[:, :, 0:4], B[:, 4:8, 0:512].rearrange("p h (c t) -> p h c t", t=P)[:, :, :, P - 1],
                                  ACT.Exp))
                so(act.activation(last_decay[:, :, 4:5], B[:, 4:8, TP - 1:TP], ACT.Exp))
                act.activation(X1[:, :, :], B[:, 4:8, 0:TP], ACT.Exp).then_inc(S["decay_last"], 1)
                wait(act, "q_decayed", L, 1, 1)
                for c, (r0, n) in enumerate(TILES):
                    for h in range(4):
                        act.activation(X1[:, h, r0:r0 + n], B[:, 4 + h, r0:r0 + n], ACT.Exp, scale=-1.0,
                                       bias=B[:, 4 + h, r0 + n - 1:r0 + n]).then_inc(S["k_exp"], 1)
                for c, (r0, n) in enumerate(TILES):
                    if c >= 2:
                        wait_filled(act, L, ("state", c - 2))
                    drain_to(decayed[0:n, c % 2, :], ("decayed", c), src=work[slot_of(("decayed", c))][0:n, 0:512])
                    ps = work[slot_of(("rec_out", c))][:, 0:512].rearrange("p (h t) -> p h t", t=P)[:, :, 0:n]
                    drain_to(B[:, 8:12, r0:r0 + n], ("rec_out", c), src=ps)
                for h in range(4):
                    drain_to(B[:, 8 + h, TP:T], ("rec_sample", h), src=work[slot_of(("rec_sample", h))][:, 0:NB])
                wait_drained(act, L, ("rec_sample", 3))
                wait_drained(act, L, ("rec_sample", 2))
                wait_drained(act, L, ("rec_out", 4))

                def rec_square(h):
                    if h >= 2:
                        wait_filled(act, L, ("rec_sumsq", h - 2))
                    act.activation(sq[:, h % 2, :], B[:, 8 + h, :], ACT.Square).then_inc(S["rec_squares"], 1)

                rec_square(0)
                rec_square(1)
                for h in range(4):
                    if h >= 1:
                        wait(act, "rec_f", L, 4, h)
                    drain_to(halves(std[:, :]), ("rec_sumsq", h), ACT.Sqrt, pair(work[slot_of(("rec_sumsq", h))]),
                             scale=1.0 / P, bias=eps[:, 0:1])
                    if h < 2:
                        rec_square(h + 2)
                for h in range(4):
                    wait(act, "rec_f", L, 4, 4)
                    act.activation(rec_hl[:, 0, h, :], B[:, 8 + h, :], ACT.Copy).then_inc(S["rec_hi"], 1)
                wait(act, "rec_lo", L, 4, 4)
                act.wait_ge(S["s0_stored"], L * 64 + 64)
                with act.Fori(0, KT) as g:
                    for i in range(2):
                        wait_unit(act, L, UM + g * 4 + i)
                        act.activation(halves(gate_s[:, i, :]), acc[i][:, :, 0:HT], ACT.Sigmoid).then_inc(taken[i], 1)
                    act.wait_ge(S["mixed"], L * 8 + g + 1)
                    act.activation(merged[:, 0, ds(g, 1), :].rearrange("p a t -> p (a t)"), mix[:, 0, :], ACT.Copy)\
                        .then_inc(S["merged_hi"], 1)
                norm("norm2", 1)
                for part in range(2):
                    with act.Fori(0, HID[part]) as g:
                        wait_unit(act, L, UG[part] + g * 2)
                        act.activation(halves(silu[:, :]), acc[0][:, :, 0:HT], ACT.Silu).then_inc(taken[0], 1)
                        act.wait_ge(S["act_done"], L * 22 + 12 * part + g + 1)
                        act.activation(hidden[:, 0, ds(g, 1), :].rearrange("p a t -> p (a t)"), act_f[:, :], ACT.Copy)\
                            .then_inc(S["hid_hi"], 1)
                so.end()
                act.wait_ge(S["act_done"], L * 22 + 22)

            for j, (r0, n) in enumerate(TILES_ALL):
                act.wait_ge(filled[j % 2], DEPTH * (ITEMS // 2) + j // 2 + 1)
                if j >= 2:
                    act.wait_ge(S[f"y_stored{j % 2}"], 16 * (j // 2))
                else:
                    act.wait_ge(unit_done, DEPTH * UNITS + 2)
                act.activation(y_rows[0:n, j % 2, :], work[j % 2][0:n, :], ACT.Copy).then_inc(S["y_ready"], 1)
                act.wait_ge(S["y_ready"], j + 1)
                act.sem_inc(drained[j % 2], 1)

        @block.vector
        def _(vec):
            TT, TS, STT = vec.tensor_tensor, vec.tensor_scalar, vec.scalar_tensor_tensor
            vec.memset(eps[:, :], EPS).then_inc(S["setup"], 1)
            vec.memset(q_idx[:, :], 0.0).then_inc(S["setup"], 1)
            vec.memset(q_sel[:, :, :, :], 0.0).then_inc(S["setup"], 1)
            vec.memset(row_base[:, :], 0.0)
            vec.wait_ge(S["loads_ready"], 320)
            vec.tensor_copy(level_mask[:, :, :], level_f[:, :, :])
            vec.tensor_copy(pages_f[:, :], pages_i[:, :]).then_inc(S["par_ready"], 1)
            vec.tensor_copy(table_f[:, :], table_i[:, :]).then_inc(S["masks_ready"], 1)
            raws = params[:, :, 19:23]
            TT(lb_tmp[:, 4, :], raws[:, 0, :], raws[:, 1, :], ALU.max).then_inc(S["setup"], 1)
            vec.wait_ge(S["setup"], 4)
            for l in range(2):
                TT(lb_tmp[:, l, :], raws[:, l, :], lb_tmp[:, 4, :], ALU.subtract).then_inc(S["setup"], 1)
            vec.wait_ge(S["setup"], 6)
            vec.drain().then_inc(S["masks_ready"], 1)
            vec.wait_ge(S["bounds_exp"], 1)
            TT(lb_tmp[:, 4, :], lb_tmp[:, 2, :], lb_tmp[:, 3, :], ALU.add).then_inc(S["setup"], 1)
            vec.wait_ge(S["setup"], 7)
            vec.reciprocal(lb_tmp[:, 5, :], lb_tmp[:, 4, :]).then_inc(S["setup"], 1)
            vec.wait_ge(S["setup"], 8)
            for l in range(2):
                TT(lb_tmp[:, l, :], lb_tmp[:, 2 + l, :], lb_tmp[:, 5, :], ALU.mult).then_inc(S["setup"], 1)
            vec.wait_ge(S["setup"], 10)
            TT(params[:, 0, 19:23], lb_tmp[:, 0, :], lb_tmp[:, 0, :], ALU.subtract).then_inc(S["setup"], 1)
            TT(lb_tmp[:, 4, :], lb_tmp[:, 0, :], lb_tmp[:, 1, :], ALU.add).then_inc(S["setup"], 1)
            vec.wait_ge(S["setup"], 12)
            TT(params[:, 1, 19:23], lb_tmp[:, 4, :], lb_tmp[:, 0, :], ALU.subtract).then_inc(S["setup"], 1)
            vec.wait_ge(S["setup"], 13)
            TS(params[:, :, 23:27], params[:, :, 19:23], -1.0, 1.0, ALU.mult, ALU.add).then_inc(S["setup"], 1)
            vec.wait_ge(S["setup"], 14)
            vec.wait_ge(S["par_ready"], 1)
            TS(page_rows_f[:, :], C("iota16", P)[:, 0:4], 0.0, None, ALU.mult).then_inc(S["setup"], 1)
            vec.wait_ge(S["setup"], 15)
            for q in range(4):
                TS(page_rows_f[:, q:q + 1], pages_f[:, :], 4.0, float(q), ALU.mult, ALU.add).then_inc(S["setup"], 1)
            vec.wait_ge(S["setup"], 19)
            vec.wait_ge(S["x_ready"], KT)

            with vec.Fori(0, DEPTH) as L:
                vo = Order(vec, S["vector_order"], L, VEC)

                def drain_ins(ins, item):
                    ins.then_inc(drained[slot_of(item)], 1)

                vo(vec.tensor_copy(par[:, :], params[:, ds(L, 1), :].rearrange("p a n -> p (a n)")))
                for q in range(4):
                    vec.tensor_copy(page_rows[:, q:q + 1], page_rows_f[:, q:q + 1]).then_inc(S["page_rows_ready"], 1)
                vec.wait_ge(S["page_rows_ready"], L * 8 + 4)
                for q in range(4):
                    TS(page_rows_f[:, q:q + 1], page_rows_f[:, q:q + 1], float(NPOOL * 4), None, ALU.add)\
                        .then_inc(S["page_rows_ready"], 1)
                vec.drain().then_inc(S["layer_begun"], 1)
                vo.settle()

                def norm(item, w):
                    wait_drained(vec, L, item)
                    vo(vec.reciprocal(std[:, :], std[:, :]))
                    vo.settle()

                    def rest(k):
                        wait(vec, "normed_hi", L, NORMS * KT, w * KT + k + 1)
                        TT(normed[:, 1, k, :], tmp[:, k % 2, :], normed[:, 0, k, :].bitcast(f32), ALU.subtract)\
                            .then_inc(S["normed_lo"], 1)

                    for k in range(KT):
                        if k >= 2:
                            wait(vec, "normed_lo", L, NORMS * KT, w * KT + k - 1)
                        STT(tmp[:, k % 2, :], x[:, k, :], par[:, 8 * w + k:8 * w + k + 1], std[:, :], ALU.mult, ALU.mult)\
                            .then_inc(S["normed_f"], 1)
                        if k >= 1:
                            rest(k - 1)
                    rest(KT - 1)

                norm("norm1", 0)

                def rope_tile(n, m):
                    ps = wait_filled(vec, L, ("rope", n))
                    rows = 64 if n == 12 else P
                    drain_ins(TT(halves(tmp[0:rows, m % 2, :]), pair(ps)[0:rows], halves(rope[0:rows, 1, :]), ALU.mult),
                              ("rope", n))
                    vo(TT(A[0:rows, n, :], A[0:rows, n, :], rope[0:rows, 0, :], ALU.mult))
                    vo.settle()
                    wait_drained(vec, L, ("rope", n))
                    TT(A[0:rows, n, :], A[0:rows, n, :], tmp[0:rows, m % 2, :], ALU.add).then_inc(S["roped"], 1)

                vec.wait_ge(S["rope_landed"], L * 16 + 16)
                for m, n in enumerate((12, 8, 9, 10, 11)):
                    rope_tile(n, m)

                def qk_norm(m):
                    n = order[m]
                    wait_drained(vec, L, ("sumsq", n))
                    vo(vec.reciprocal(std[:, :], std[:, :]))
                    vo.settle()
                    gain = par[:, 17:18] if n >= 4 else par[:, 16:17]
                    STT(A[:, n, :], A[:, n, :], gain, std[:, :], ALU.mult, ALU.mult).then_inc(S["qk_normed"], 1)

                qk_norm(0)
                for m, n in enumerate(order):
                    if m < 5:
                        qk_norm(m + 1)
                    wait(vec, "qk_normed", L, 6, m + 1)
                    rope_tile(n, m)
                wait(vec, "roped", L, 11, 11)

                wait_drained(vec, L, "swapped")
                qi = A[:, 8:12, TP:T].rearrange("p i b -> p b i")
                sw = swapped[:, 4:8, :].rearrange("p i b -> p b i")
                for p0 in (0, 64):
                    dst = q_idx[p0:p0 + 64, p0:p0 + 64].rearrange("p (b i s) -> p b i s", i=4, s=2)
                    s = p0 // 64
                    vec.tensor_copy(dst[:, :, :, s], qi[p0:p0 + 64]).then_inc(S["weights_ready"], 1)
                    vec.tensor_copy(dst[:, :, :, 1 - s], sw[p0:p0 + 64]).then_inc(S["weights_ready"], 1)
                ps = wait_filled(vec, L, "index_weights")
                drain_ins(STT(w_page[:, :, :], ps[:, 0:8].unsqueeze(1).broadcast_to((P, 8, 8)), IDX_SCALE,
                              C("page_row").unsqueeze(2).broadcast_to((P, 8, 8)), ALU.mult, ALU.mult), "index_weights")
                wait_drained(vec, L, "sample_tokens")
                STT(w_new[:, :, :], s_tok[:, 320:328].unsqueeze(1).broadcast_to((NB, 8, 8)), IDX_SCALE,
                    C("ident")[0:8, 0:8].unsqueeze(2).broadcast_to((NB, 8, 8)), ALU.mult, ALU.mult)\
                    .then_inc(S["weights_ready"], 1)
                for p0 in (0, 64):
                    s = p0 // 64
                    for side in range(2):
                        src = (A if side == s else swapped)[p0:p0 + 64]
                        src = src[:, s:4:2, TP:T] if side == s else src[:, s:4:2, :]
                        for pr in range(2):
                            ins = vec.tensor_copy(q_sel[p0:p0 + 64, pr, :, 4 * pr + 2 * s + side], src[:, pr, :])
                            if pr == 0:
                                vo(ins)
                            else:
                                ins.then_inc(S["q_sel_ready"], 1)
                for j, (r0, n) in enumerate(TILES_ALL):
                    wait_drained(vec, L, ("tokens", j))
                    ins = TS(w_tok[0:n, j, :], tok[0:n, j, 576:584], IDX_SCALE, None, ALU.mult)
                    if j < 4:
                        ins.then_inc(S["weights_ready"], 1)
                    else:
                        vo(ins)
                wait_drained(vec, L, "new_key_dots")
                wait(vec, "weights_ready", L, 9, 9)
                vo.settle()
                vo(TT(new_tmp[:, :], new_tmp[:, :], w_new[:, :, :].rearrange("p a b -> p (a b)"), ALU.mult))
                vo.settle()
                vec.tensor_reduce(ss[:, PAST:PAST + 1], new_tmp[:, :], AX.X, ALU.add).then_inc(S["index_done"], 1)
                wait_drained(vec, L, "index_weights")
                for r in range(8):
                    wait_drained(vec, L, ("key_dots", r))
                    if r % 2 == 1:
                        pass
                    buf = idx_relu[:, r % 2, :].rearrange("p (k c) -> p k c", c=64)
                    vo(TT(buf, buf, w_page[:, :, :].rearrange("p a b -> p (a b)").unsqueeze(1).broadcast_to((P, 16, 64)),
                          ALU.mult))
                    vo.settle()
                    vec.tensor_reduce(sc_page[:, r * 16:r * 16 + 16], buf, AX.X, ALU.add).then_inc(S["index_done"], 1)
                    if r % 2 == 1 and r < 7:
                        vec.drain().then_inc(S["pages_used"], 1)
                vec.drain().then_inc(S["pages_used"], 1)

                for j in range(1, 5):
                    n, w = TILES[j][1], WIDTH[j]
                    dst = sc[0:n, SC_AT[j]:SC_AT[j] + w]
                    for h in range(8):
                        m = (j - 1) * 8 + h
                        wait_drained(vec, L, ("dots", j, h))
                        wh = w_tok[0:n, j, h:h + 1]
                        if h == 0:
                            ins = TS(dst, relu_buf(m, n, w), wh, None, ALU.mult)
                        else:
                            wait(vec, "dots_done", L, 32, m)
                            ins = STT(dst, relu_buf(m, n, w), wh, dst, ALU.mult, ALU.add)
                        ins.then_inc(S["dots_done"], 1)
                    wait(vec, "dots_done", L, 32, m + 1)
                    r0 = TILES[j][0]
                    tail = sc[0:n, SC_AT[j] + r0:SC_AT[j] + w]
                    vo(TT(tail, tail, C("causal")[0:n, 0:w - r0], ALU.add))
                vo.settle()
                hold(vec)
                for j in range(1, 5):
                    n, w = TILES[j][1], WIDTH[j]
                    dst = sc[0:n, SC_AT[j]:SC_AT[j] + w]
                    with vec.Fori(0, TOPK_P // 8) as r:
                        vec.max(top8[0:n, :], dst).then_inc(S["topk"], 1)
                        vec.wait_ge(S["topk"], (L * 4 + (j - 1)) * (TOPK_P // 4) + r * 2 + 1)
                        hold(vec)
                        vec.match_replace(dst, top8[0:n, :], dst, PICKED).then_inc(S["topk"], 1)
                        vec.wait_ge(S["topk"], (L * 4 + (j - 1)) * (TOPK_P // 4) + r * 2 + 2)
                        hold(vec)
                    vo(TS(dst, dst, PICKED, NEG, ALU.is_gt, ALU.mult))
                vec.wait_ge(S["scores_landed"], L * 16 + 16)
                wait(vec, "index_done", L, 9, 9)
                hold(vec)
                with vec.Fori(0, TOPK_S // 32) as r:
                    for i in range(4):
                        base_n = L * (TOPK_S // 8 * 3) + r * 12 + i * 3
                        vec.max(top8s[:, :], ss[:, :]).then_inc(S["sample_topk"], 1)
                        vec.wait_ge(S["sample_topk"], base_n + 1)
                        hold(vec)
                        vec.max_index(pick_i[:, 0, 8 * i:8 * i + 8], top8s[:, :], ss[:, :]).then_inc(S["sample_topk"], 1)
                        vec.match_replace(ss[:, :], top8s[:, :], ss[:, :], PICKED).then_inc(S["sample_topk"], 1)
                        vec.wait_ge(S["sample_topk"], base_n + 3)
                        hold(vec)
                    vec.tensor_copy(found[:, ds(r * 32, 32)], pick_i[:, 0, 0:32]).then_inc(S["found_part"], 1)
                    vec.wait_ge(S["found_part"], L * 8 + r + 1)
                    hold(vec)
                vo(TS(flag[:, :], ss[:, PAST:PAST + 1], PICKED, NEG, ALU.is_gt, ALU.mult))
                vo(TS(pick_i[:, 0, :], found[:, :], 7, None, ALU.logical_shift_right))
                vo(TS(pick_i[:, 1, :], found[:, :], 127, None, ALU.bitwise_and))
                vo.settle()
                vo(vec.tensor_copy(pick_f[:, 0:2, :], pick_i[:, :, :]))
                vo.settle()
                vo(TT(page_eq[:, :, :], pick_f[:, 0, :].unsqueeze(2).broadcast_to((NB, TOPK_S, PAGES)),
                      C("iota16", NB).unsqueeze(1).broadcast_to((NB, TOPK_S, PAGES)), ALU.is_equal))
                vo.settle()
                vo(TT(page_eq[:, :, :], page_eq[:, :, :], table_f[:, :].unsqueeze(1).broadcast_to((NB, TOPK_S, PAGES)),
                      ALU.mult))
                vo.settle()
                vo(vec.tensor_reduce(pick_f[:, 2, :], page_eq[:, :, :], AX.X, ALU.add))
                vo(TS(pick_f[:, 3, :], pick_f[:, 0, :], float(PAGES), NEG, ALU.is_ge, ALU.mult))
                vo.settle()
                STT(pick_f[:, 2, :], pick_f[:, 2, :], float(PAGE), pick_f[:, 1, :], ALU.mult, ALU.add)\
                    .then_inc(S["picks_ready"], 1)
                vec.drain().then_inc(S["picks_ready"], 1)

                for n2 in range(4):
                    for j in range(5):
                        n, w = TILES[j][1], WIDTH[j]
                        mask = sc[0:n, SC_AT[j]:SC_AT[j] + w] if j else C("causal")
                        for s in range(2):
                            h = 2 * n2 + s
                            e = n2 * 10 + j * 2 + s
                            ps = wait_filled(vec, L, ("qk", h, j))
                            if e >= 2:
                                pj, pn = (j - 1, n2) if j else (4, n2 - 1)
                                wait_filled(vec, L, ("turn", 2 * pn + s, pj))
                            hold(vec)
                            drain_ins(vec.tensor_tensor_reduce(E[0:n, s, 0:w], ps[0:n, 0:w], mask, ATT_SCALE, -3e38,
                                                               ALU.add, ALU.max, row_st[0:n, s, 0:1]), ("qk", h, j))
                            wait_drained(vec, L, ("qk", h, j))
                            TS(row_st[0:n, s, 1:2], row_st[0:n, s, 0:1], -1.0, None, ALU.mult).then_inc(S["row_mask"], 1)
                        for s in range(2):
                            e = n2 * 10 + j * 2 + s
                            wait(vec, "exps", L, 40, e + 1)
                            vo(vec.reciprocal(row_st[0:n, s, 3:4], row_st[0:n, s, 2:3]))
                            vo.settle()
                            TS(E[0:n, s, 0:w], E[0:n, s, 0:w], row_st[0:n, s, 3:4], None, ALU.mult).then_inc(S["probs"], 1)

                ps = wait_filled(vec, L, "rows_turn")
                vo(vec.tensor_copy(new_mask[:, :], ps[:, 16:32]))
                drain_ins(TT(row_idx[:, :], ps[:, 0:16], row_base[:, 0:1].broadcast_to((P, 16)), ALU.add), "rows_turn")
                wait_drained(vec, L, "rows_turn")
                TS(row_base[:, :], row_base[:, :], float(NPOOL * PAGE), None, ALU.add).then_inc(S["rows_ready"], 1)
                vec.drain().then_inc(S["rows_ready"], 1)
                vo.settle()
                for r in range(4):
                    ps = wait_filled(vec, L, ("sel_dots", r))
                    dst = sel_s[:, :, :].rearrange("p a (b c) -> p (a b) c", c=8)[:, 4 * r:4 * r + 4, :]
                    drain_ins(TT(dst, ps[:, 0:32].rearrange("p (a c) -> p a c", c=8),
                                 new_mask[:, 4 * r:4 * r + 4].unsqueeze(2).broadcast_to((P, 4, 8)), ALU.add),
                              ("sel_dots", r))
                for r in range(4):
                    wait_drained(vec, L, ("sel_dots", r))
                hold(vec)
                vec.drain().then_inc(S["sel_scores"], 1)
                ps = wait_filled(vec, L, "sel_rows")
                vo(TT(sel_new[:, :], ps[0:64, 512:520], C("head_row"), ALU.mult))
                vo(vec.tensor_copy(sel_c[:, 3:4], ps[0:64, 520:521]))
                drain_ins(vec.tensor_copy(sel_p[:, 0:256], ps[0:64, 0:256]), "sel_rows")
                vo.settle()
                vo(vec.tensor_reduce(sel_p[:, 256:257], sel_new[:, :], AX.X, ALU.add))
                vo.settle()
                vo(TT(sel_p[:, 256:257], sel_p[:, 256:257], sel_c[:, 3:4], ALU.add))
                vo.settle()
                wait_drained(vec, L, "sel_rows")
                vo(vec.tensor_reduce(sel_c[:, 0:1], sel_p[:, 0:257], AX.X, ALU.max))
                vo.settle()
                TS(sel_c[:, 1:2], sel_c[:, 0:1], -ATT_SCALE, None, ALU.mult).then_inc(S["sel_exp"], 1)
                wait(vec, "sel_out", L, 1, 1)
                vo(vec.reciprocal(sel_c[:, 3:4], sel_c[:, 2:3]))
                vo.settle()
                vo(TS(sel_p[:, 0:257], sel_p[:, 0:257], sel_c[:, 3:4], None, ALU.mult))
                vo.settle()
                TS(sel_new[:, :], C("head_row"), sel_p[:, 256:257], None, ALU.mult).then_inc(S["sel_probs_ready"], 1)
                vec.drain().then_inc(S["sel_probs_ready"], 1)
                ps = wait_filled(vec, L, "sel_probs")
                vo(vec.tensor_copy(sel_pT[:, 0:128], ps[:, 0:128]))
                drain_ins(vec.tensor_copy(sel_pT[0:NB, 128:192], ps[0:NB, 128:192]), "sel_probs")
                ps = wait_filled(vec, L, "sel_pv")
                drain_ins(vec.tensor_copy(sel_o[:, :, :, :].rearrange("p a b c -> p (a b c)"), ps[:, 0:64]), "sel_pv")
                wait_drained(vec, L, "sel_pv")
                ps = wait_filled(vec, L, "sel_swap")
                pso = ps[:, 0:64].rearrange("p (a b c) -> p a b c", a=2, b=NB)
                for s in range(2):
                    for side in range(2):
                        src = (sel_o[:, :, :, :] if side == s else pso)[64 * side:64 * side + 64, :, :, 2 * s + side]
                        vec.tensor_copy(A[64 * side:64 * side + 64, s:4:2, TP:T], src).then_inc(S["att_ready"], 1)
                vec.drain().then_inc(drained[slot_of("sel_swap")], 1)
                wait(vec, "att_ready", L, 4, 4)
                wait_filled(vec, L, "sel_swap")
                for n in range(4):
                    wait(vec, "att_hi", L, 4, n + 1)
                    TT(att_hl[:, 1, n, :], A[:, n, :], att_hl[:, 0, n, :].bitcast(f32), ALU.subtract)\
                        .then_inc(S["att_lo"], 1)

                for h in range(4):
                    TS(B[:, 4 + h, :], B[:, 4 + h, :], par[:, 23 + h:24 + h], par[:, 19 + h:20 + h], ALU.mult, ALU.add)\
                        .then_inc(S["forget"], 1)
                    wait(vec, "forget", L, 9, 2 * h + 1)
                    TS(K[:, h, :], B[:, 4 + h, :], -1.0, 1.0, ALU.mult, ALU.add).then_inc(S["forget"], 1)
                vec.wait_ge(S["state_stored"], L * 16 + 16)
                vec.memset(state[:, :, :], 0.0).then_inc(S["forget"], 1)
                vo(vec.memset(Asc[:, :, :], 0.0))
                vo(vec.memset(Atail[:, :, :], 0.0))
                for h in range(4):
                    wait(vec, "log_forget", L, 4, h + 1)
                    for r0, n in TILES:
                        lf = B[:, 4 + h, r0:r0 + n]
                        vec.tensor_tensor_scan(lf, C("ones")[:, 0:n], lf, 0.0, ALU.mult, ALU.add)\
                            .then_inc(S["decay_sum"], 1)
                wait(vec, "decay_sum", L, 20, 20)
                vo.settle()

                def level_scores(lev):
                    for hp in range(2):
                        ps = wait_filled(vec, L, ("level", lev, hp))
                        hold(vec)
                        drain_ins(vec.copy_predicated(
                            Asc[:, 2 * hp:2 * hp + 2, :].rearrange("p h (c t) -> p (h c) t", t=P),
                            level_mask[:, lev:lev + 1, :].broadcast_to((P, 8, P)),
                            ps[:, :].rearrange("p (c t) -> p c t", t=P)), ("level", lev, hp))
                    if lev >= 3:
                        ps = wait_filled(vec, L, ("level_tail", lev))
                        hold(vec)
                        drain_ins(vec.copy_predicated(Atail[:, :, :], level_mask[0:16, lev:lev + 1, 0:16].broadcast_to((16, 4, 16)),
                                                      ps[0:16, 0:64].rearrange("p (h t) -> p h t", t=16)),
                                  ("level_tail", lev))

                for lev, hs in enumerate(HALVES):
                    w = 512 if hs >= 16 else TP
                    xv = X[lev % 2][:, :, 0:w].rearrange("p h (b c) -> p h b c", c=2 * hs)
                    bv = B[:, 4:8, 0:w].rearrange("p h (b c) -> p h b c", c=2 * hs)
                    qv = B[:, 0:4, 0:w].rearrange("p h (b c) -> p h b c", c=2 * hs)
                    kv = K[:, :, 0:w].rearrange("p h (b c) -> p h b c", c=2 * hs)
                    mid = bv[:, :, :, hs - 1:hs].broadcast_to((P, 4, w // (2 * hs), hs))
                    TT(xv[:, :, :, hs:], bv[:, :, :, hs:], mid, ALU.subtract).then_inc(S["lev_diff"], 1)
                    TT(xv[:, :, :, 0:hs], mid, bv[:, :, :, 0:hs], ALU.subtract).then_inc(S["lev_diff"], 1)
                    if lev >= 1:
                        level_scores(lev - 1)
                    wait(vec, "lev_exp", L, 7, lev + 1)
                    TT(xv[:, :, :, hs:], xv[:, :, :, hs:], qv[:, :, :, hs:], ALU.mult).then_inc(S["lev_ready"], 1)
                    TT(xv[:, :, :, 0:hs], xv[:, :, :, 0:hs], kv[:, :, :, 0:hs], ALU.mult).then_inc(S["lev_ready"], 1)
                level_scores(6)
                level_scores(7)
                wait(vec, "decay_last", L, 1, 1)
                TT(X0[:, :, :], X1[:, :, :], B[:, 0:4, 0:TP], ALU.mult).then_inc(S["q_decayed"], 1)
                wait(vec, "k_exp", L, 20, 20)
                TT(X1[:, :, :], X1[:, :, :], K[:, :, 0:TP], ALU.mult).then_inc(S["k_decayed"], 1)
                for c in range(5):
                    ps = wait_filled(vec, L, ("state", c))
                    for h in range(4):
                        if c:
                            wait(vec, "state_ready", L, 20, 4 * c - 3 + h)
                        STT(state[:, h, :], state[:, h, :], last_decay[:, h, c:c + 1], ps[:, h * P:(h + 1) * P],
                            ALU.mult, ALU.add).then_inc(S["state_ready"], 1)
                    vec.drain().then_inc(drained[slot_of(("state", c))], 1)
                wait_drained(vec, L, "v_sample")
                for h in range(4):
                    if h:
                        wait_filled(vec, L, ("rank1", h - 1))
                    TT(v_blk[:, :, :], v_s[:, h * P:(h + 1) * P].unsqueeze(1).broadcast_to((NB, NB, P)),
                       C("ident")[0:8, 0:8].unsqueeze(2).broadcast_to((NB, NB, P)), ALU.mult)\
                        .then_inc(S["v_blk_ready"], 1)
                    ps = wait_filled(vec, L, ("rank1", h))
                    vec.wait_ge(S[f"s0_landed{h % 2}"], L * 32 + 16 * (h // 2) + 16)
                    for b in range(NB):
                        STT(s0[:, h % 2, b, :], s0[:, h % 2, b, :], B[:, 4 + h, TP + b:TP + b + 1], ps[:, b * P:(b + 1) * P],
                            ALU.mult, ALU.add).then_inc(S["s0_ready"], 1)
                    vec.drain().then_inc(drained[slot_of(("rank1", h))], 1)
                for h in range(4):
                    wait_drained(vec, L, ("rec_sumsq", h))
                    vo(vec.reciprocal(std[:, :], std[:, :]))
                    vo(TT(B[:, 12 + h, :], B[:, 12 + h, :], B[:, 8 + h, :], ALU.mult))
                    vo.settle()
                    STT(B[:, 8 + h, :], B[:, 12 + h, :], par[:, 18:19], std[:, :], ALU.mult, ALU.mult)\
                        .then_inc(S["rec_f"], 1)
                for h in range(4):
                    wait(vec, "rec_hi", L, 4, h + 1)
                    TT(rec_hl[:, 1, h, :], B[:, 8 + h, :], rec_hl[:, 0, h, :].bitcast(f32), ALU.subtract)\
                        .then_inc(S["rec_lo"], 1)

                with vec.Fori(0, KT) as g:
                    wait_unit(vec, L, UM + g * 4 + 2)
                    vec.wait_ge(taken[0], L * (OUTS // 2) + OM // 2 + g * 2 + 2)
                    TT(halves(mix[:, 0, :]), acc[0][:, :, 0:HT], halves(gate_s[:, 0, :]), ALU.mult).then_inc(taken[0], 1)
                    wait_unit(vec, L, UM + g * 4 + 3)
                    vec.wait_ge(taken[1], L * (OUTS // 2) + OM // 2 + g * 2 + 2)
                    TT(halves(mix[:, 1, :]), acc[1][:, :, 0:HT], halves(gate_s[:, 1, :]), ALU.mult).then_inc(taken[1], 1)
                    vec.wait_ge(taken[0], L * (OUTS // 2) + OM // 2 + g * 2 + 3)
                    vec.wait_ge(taken[1], L * (OUTS // 2) + OM // 2 + g * 2 + 3)
                    TT(mix[:, 0, :], mix[:, 0, :], mix[:, 1, :], ALU.add).then_inc(S["mixed"], 1)
                    vec.wait_ge(S["merged_hi"], L * 8 + g + 1)
                    TT(merged[:, 1, ds(g, 1), :].rearrange("p a t -> p (a t)"), mix[:, 0, :],
                       merged[:, 0, ds(g, 1), :].rearrange("p a t -> p (a t)").bitcast(f32), ALU.subtract)\
                        .then_inc(S["merged_lo"], 1)
                    vec.wait_ge(S["merged_lo"], L * 8 + g + 1)
                    hold(vec)
                with vec.Fori(0, 4) as g:
                    for i in range(2):
                        wait_unit(vec, L, UO + g * 2 + i)
                        xk = x[:, ds(g * 2 + i, 1), :].rearrange("p a (b c) -> p (a b) c", b=2)
                        TT(xk, acc[i][:, :, 0:HT], xk, ALU.add).then_inc(taken[i], 1)
                        vec.drain().then_inc(S["x_updated"], 1)
                norm("norm2", 1)
                for part in range(2):
                    with vec.Fori(0, HID[part]) as g:
                        wait_unit(vec, L, UG[part] + g * 2 + 1)
                        vec.wait_ge(taken[0], L * (OUTS // 2) + OG[part] // 2 + g + 2)
                        TT(halves(act_f[:, :]), acc[1][:, :, 0:HT], halves(silu[:, :]), ALU.mult).then_inc(taken[1], 1)
                        vec.drain().then_inc(S["act_done"], 1)
                        vec.wait_ge(S["hid_hi"], L * 22 + 12 * part + g + 1)
                        vec.wait_ge(taken[1], L * (OUTS // 2) + OG[part] // 2 + g + 2)
                        TT(hidden[:, 1, ds(g, 1), :].rearrange("p a t -> p (a t)"), act_f[:, :],
                           hidden[:, 0, ds(g, 1), :].rearrange("p a t -> p (a t)").bitcast(f32), ALU.subtract)\
                            .then_inc(S["hid_lo"], 1)
                        vec.wait_ge(S["hid_lo"], L * 22 + 12 * part + g + 1)
                        hold(vec)
                    with vec.Fori(0, 4) as g:
                        for i in range(2):
                            wait_unit(vec, L, UD[part] + g * 4 + 2 * i + 1)
                            xk = x[:, ds(g * 2 + i, 1), :].rearrange("p a (b c) -> p (a b) c", b=2)
                            TT(xk, acc[i][:, :, 0:HT], xk, ALU.add).then_inc(taken[i], 1)
                            vec.drain().then_inc(S["x_updated"], 1)
                if ITEM.get("none") is not None:
                    wait_filled(vec, L, "none")
                    vec.drain().then_inc(drained[1], 1)
                vo.end()


_STEPS = (109, 10)
_INS = ["x_prompt", "x_sample", "cache_k", "cache_v", "cache_idx_k", "state_rec", "page_table", "meta_tokens", "w_in",
        "norm_mix", "q_norm", "k_norm", "lb_raw", "rec_norm", "w_pa", "w_pb", "w_o", "norm_ffn", "w_gu", "w_down"]
_OUTS = [(1, 512, 1024), (8, 1, 1024), (2, 1, 528, 256), (2, 1, 528, 256), (2, 1, 528, 64), (2, 1, 4, 128, 128),
         (2, 8, 1, 256), (2, 8, 1, 256), (2, 8, 1, 64), (2, 8, 4, 128, 128)]
_SHAPES = [(1, 512, 1024), (8, 1, 1024), (2, 1, 528, 4, 64), (2, 1, 528, 4, 64), (2, 1, 528, 64), (2, 1, 4, 128, 128),
           (2, 8, 1, 4, 64), (2, 8, 1, 4, 64), (2, 8, 1, 64), (2, 8, 4, 128, 128)]


def kernel(**inputs):
    import numpy as np
    import concourse.bacc as bacc
    from concourse import mybir
    from concourse.bass_utils import run_bass_kernel_spmd

    nc = bacc.Bacc("TRN2", target_bir_lowering=False, num_devices=1)
    arrays, t = {}, {}

    def feed(name, a):
        arrays[f"in_{name}_dram"] = a
        t[name] = nc.dram_tensor(f"in_{name}_dram", a.shape, mybir.dt.from_np(a.dtype), kind="ExternalInput").ap()

    for name in _INS:
        feed(name, np.ascontiguousarray(inputs[name]))
    table, levels, where, resident = constants()
    feed("constants", table)
    feed("levels", levels)
    t["where"], t["resident"], t["steps"] = where, resident, _STEPS
    outs = [nc.dram_tensor(f"out_{i}_dram", shape, mybir.dt.float32, kind="ExternalOutput").ap()
            for i, shape in enumerate(_OUTS)]
    build(nc, t, outs)
    r = run_bass_kernel_spmd(nc, [arrays], core_ids=[0])
    return tuple(np.asarray(r.results[0][f"out_{i}_dram"]).reshape(s) for i, s in enumerate(_SHAPES))
```

```python
def constants():
    import numpy as np

    P, T, TP = 128, 536, 528
    parts, where, at = [], {}, 0

    def add(name, a):
        nonlocal at
        full = np.zeros((P, a.shape[1]), np.float32)
        full[: a.shape[0]] = a
        where[name] = (at, a.shape[0], a.shape[1])
        parts.append(full)
        at += a.shape[1]

    i = np.arange(P)
    add("ident", np.eye(P))
    add("ones", np.ones((P, P)))
    add("head_ones", (i[:, None] // 64 == i[None, :] // 64).astype(np.float32))
    rot = np.zeros((P, P), np.float32)
    for base in (0, 64):
        for d in range(8):
            rot[base + d, base + d + 8] = -1.0
            rot[base + d + 8, base + d] = 1.0
    add("rot", rot.T)
    swap = np.zeros((P, P), np.float32)
    swap[i, (i + 64) % P] = 1.0
    add("swap", swap)
    add("causal", np.where(i[None, :] <= i[:, None], 0.0, -1e30))
    b8 = np.arange(8)
    add("page_row", (i[:, None] // 16 == b8[None, :]).astype(np.float32))
    same_row = i[:, None] // 16 == i[None, :] // 16
    add("page_ones", same_row.astype(np.float32))
    add("page_before", (same_row & (i[:, None] < i[None, :])).astype(np.float32))
    add("row_page", (b8[:, None] == i[None, :] // 16).astype(np.float32))
    add("row_head", (b8[:, None] == np.arange(64)[None, :] // 8).astype(np.float32))
    add("head_row", (np.arange(64)[:, None] // 8 == b8[None, :]).astype(np.float32))
    add("iota", np.tile(np.arange(136, dtype=np.float32), (P, 1)))
    add("row_number", np.stack([i, i + P], 1).astype(np.float32))
    add("last_page", (i[:, None] % 16 == 15).astype(np.float32))
    add("not_last", np.where(i[:, None] % 16 == 15, 0.0, -3.4028235e38))
    resident = at
    pos = np.concatenate([np.arange(TP), np.full(T - TP, 2048)]).astype(np.float32)
    inv = np.power(np.float32(500000.0), np.float32(-2.0) * np.arange(8, dtype=np.float32) / np.float32(16))
    cos, sin = np.ones((P, T), np.float32), np.zeros((P, T), np.float32)
    for p in range(P):
        if p % 64 < 16:
            ang = (pos * inv[p % 8].astype(np.float32)).astype(np.float32)
            cos[p], sin[p] = np.cos(ang), np.sin(ang)
    add("cos", cos)
    add("sin", sin)
    levels = np.zeros((P, 8, P), np.float32)
    for lev in range(7):
        half = 64 >> lev
        same = i[:, None] // (2 * half) == i[None, :] // (2 * half)
        levels[:, lev] = same & (i[:, None] % (2 * half) < half) & (i[None, :] % (2 * half) >= half)
    levels[:, 7] = np.eye(P)
    return np.concatenate(parts, 1), levels, where, resident


def build(nc, t, out):
    from contextlib import ExitStack

    import concourse.bass as bass
    from concourse import mybir

    f32, f32r, i32, u32, u8 = (mybir.dt.float32, mybir.dt.float32r, mybir.dt.int32, mybir.dt.uint32, mybir.dt.uint8)
    ACT, ALU, AX = mybir.ActivationFunctionType, mybir.AluOpType, mybir.AxisListType
    ds = bass.ds

    P = 128
    DEPTH, DM, DFF = 2, 1024, 2816
    NP, NB = 512, 8
    META = 16
    TP = NP + META
    T = TP + NB
    HT = T // 2
    KT = DM // P
    NPOOL, PAGE, PAGES, PAST = 160, 128, 16, 2048
    TOPK_P, TOPK_S = 128, 256
    EPS, NEG, PICKED = 1e-6, -1e30, -3e38
    IDX_SCALE = (8 * 64) ** -0.5
    ATT_SCALE = 64 ** -0.5
    TILES = [(128 * j, min(128, TP - 128 * j)) for j in range(5)]
    TILES_ALL = TILES[:4] + [(512, 24)]
    WIDTH = [128, 256, 384, 512, 528]
    SC_AT = [0, 0, 256, 640, 1152]
    HALVES = [64, 32, 16, 8, 4, 2, 1]

    A_TILES = [12, 8, 9, 10, 11, 4, 5, 6, 7, 0, 1, 2, 3]
    UA, UB, UM, UO = 0, 16, 32, 64
    HID = [12, 10]
    UG = [72, 112]
    UD = [96, 132]
    UNITS = 148
    OA, OB, OM, OO = 0, 14, 30, 62
    OG = [70, 102]
    OD = [94, 122]
    OUTS = 130

    items = ["norm1", ("rope", 12)]
    items += [("rope", n) for n in (8, 9, 10, 11)]
    order = [4, 5, 0, 1, 2, 3]
    items += [("sumsq", 4)]
    for n, nxt in zip(order, order[1:] + [None]):
        if nxt is not None:
            items.append(("sumsq", nxt))
        items.append(("rope", n))
    items += ["sample_tokens"] + [("tokens", j) for j in range(5)]
    items += ["swapped", "index_weights", "new_key_dots"]
    items += [("key_turn", 0)]
    for r in range(8):
        if r < 7:
            items.append(("key_turn", r + 1))
        items.append(("key_dots", r))
    items += ["new_score"]
    items += [("dots", j, h) for j in range(1, 5) for h in range(8)]
    items += ["ties", "starts"]
    for n in range(4):
        for j in range(5):
            items += [("turn", 2 * n, j), ("turn", 2 * n + 1, j), ("pv", n, j)]
        if n == 0:
            items += ["new_flag"] + [("slots", r) for r in range(4)]
    items += [("sel_turn", 0), ("sel_turn", 1), ("sel_dots", 0), ("sel_turn", 2), ("sel_dots", 1), ("sel_turn", 3),
              ("sel_dots", 2), ("sel_dots", 3)]
    items += ["sel_rows", "sel_probs", "sel_pv", "sel_swap"]
    LEVELS = [7, 0, 1, 2, 3, 4, 5, 6]
    turns = [("v_turn", c) for c in range(5)] + ["v_sample", "k_sample"]
    for n, lev in enumerate(LEVELS):
        items += [("level", lev, 0), ("level", lev, 1)] + ([("level_tail", lev)] if lev >= 3 else []) + turns[n:n + 1]
    for c in range(5):
        items += [("decayed", c), ("rec_out", c), ("state", c)]
        items += ([("rank1", c)] if c < 4 else []) + ([("rec_sample", c - 1)] if c else [])
    items += [("rec_sumsq", h) for h in range(4)]
    items += ["norm2"]
    if len(items) % 2:
        items.append("none")
    ITEM = {name: n for n, name in enumerate(items)}
    ITEMS = len(items)

    csts, where = t["constants"], t["where"]
    ctx = ExitStack()
    with ctx:
        def sb(name, shape, dt=f32):
            return ctx.enter_context(nc.sbuf_tensor(name, shape, dt))

        def sem(name):
            return ctx.enter_context(nc.semaphore(name))

        x = sb("x", [P, KT, T])
        normed = sb("normed", [P, 2, KT, T], f32r)
        raw = [sb(f"raw{i}", [P, 8, P]) for i in range(4)]
        w_hi = [sb(f"w_hi{i}", [P, 8, P], f32r) for i in range(2)]
        w_lo = [sb(f"w_lo{i}", [P, 8, P], f32r) for i in range(2)]
        cst = sb("cst", [P, t["resident"]])
        level_mask = sb("level_mask", [P, 8, P], u8)
        params = sb("params", [P, DEPTH, 27])
        par = sb("par", [P, 27])
        lb_tmp = sb("lb_tmp", [P, 6, 4])
        eps = sb("eps", [P, 1])
        state = sb("state", [P, 4, P])
        last_decay = sb("last_decay", [P, 4, 5])
        pages_i = sb("pages_i", [P, 1], i32)
        pages_f = sb("pages_f", [P, 1])
        page_rows = sb("page_rows", [P, 4], i32)
        page_rows_f = sb("page_rows_f", [P, 4])
        pick_cols = sb("pick_cols", [P, 8])
        page_base = pick_cols[:, 0:1]
        top8_pair = sb("top8_pair", [P, 2, 8])
        top8, top8b = top8_pair[:, 0, :], top8_pair[:, 1, :]
        limit = sb("limit", [P, 1], u32)
        trial = sb("trial", [P, 1], u32)
        enough = sb("enough", [P, 1], u8)
        counts = pick_cols[:, 1:3]
        first_slot, ties_left, unpicked = (pick_cols[:, i:i + 1] for i in (3, 4, 5))
        new_score = sb("new_score", [NB, 1])
        picks = sb("picks", [P, 20])
        slot_l, picks = picks[:, 16:20], picks[:, 0:16]
        row_idx = sb("row_idx", [P, 16], i32)
        new_mask = sb("new_mask", [P, 16])
        flag = sb("flag", [NB, 1])
        row_base = sb("row_base", [P, 1])
        s_tok = sb("s_tok", [NB, 328])
        w_tok = sb("w_tok", [P, 5, 8])
        w_page = sb("w_page", [P, 8, 8])
        w_new = sb("w_new", [NB, 8, 8])
        swapped = sb("swapped", [P, 8, NB])
        q_idx = sb("q_idx", [P, P])
        q_sel = sb("q_sel", [P, 2, NB, 8])
        sc_page = sb("sc_page", [P, P + 1])
        new_tmp = sb("new_tmp", [NB, 64])
        sel_s = sb("sel_s", [P, 2, 64])
        sel_p = sb("sel_p", [64, 260])
        sel_c = sb("sel_c", [64, 4])
        sel_new = sb("sel_new", [64, 8])
        sel_pT = sb("sel_pT", [P, 192])
        sel_o = sb("sel_o", [P, 2, NB, 4])
        row_st = sb("row_st", [P, 2, 4])

        base = (nc.sbuf_base + 63) // 64 * 64
        size = nc.sbuf_usable_end - base

        def place(name, shape, offset, dt=f32):
            n = 1
            for d in shape[1:]:
                n *= d
            n *= 1 if dt == u8 else 4
            assert offset + n <= size, (name, offset + n, size)
            return nc.alloc_sbuf_tensor_at(name, shape, dt, offset=base + offset)

        TB = T * 4
        A = place("proj_att", [P, 13, T], 0)
        PB0 = 29248
        B = place("proj_rec", [P, 16, T], PB0)
        idx_pages = place("idx_pages", [P, 2, 2048], PB0)
        idx_turned = place("idx_turned", [P, 2, 1024], PB0 + 16384)
        idx_relu = place("idx_relu", [P, 2, 1024], PB0 + 24576)
        o = PB0 + 16 * TB
        tok = place("tok", [P, 5, 584], o); o_tok = o; o += 5 * 584 * 4
        k_dup = place("k_dup", [P, 2, T], o); o += 2 * TB
        sc = place("sc", [P, 1680], o); o_sc = o; o += 1680 * 4
        ki_dup = place("ki_dup", [P, T], o); o_ss = o; o += TB
        o += 7200
        o_v = o
        k_sel = place("k_sel", [P, 16, 256], 6 * TB)
        v_sel = place("v_sel", [P, 16, 256], o_v)
        o_p = 6 * TB
        code = place("code", [P, 129], o_p)
        above = place("above", [P, 129], o_p + 544)
        equal = place("equal", [P, 129], o_p + 2 * 544)
        rank = place("rank", [P, 129], o_p + 3 * 544)
        lists = place("lists", [P, 137], o_p + 4 * 544)
        slot_d = place("slot_d", [P, 2, P], o_p + 6 * 544)
        slot_o = place("slot_o", [P, 2, P], o_p + 6 * 544 + 1024)
        slot_b = place("slot_b", [P, NB, 2, P], o_p + 6 * 544 + 2048)
        slot_x = place("slot_x", [P, 2, 2, 136], o_v)
        E = place("E", [P, 2, TP], o_ss)
        pT = place("pT", [P, 2, 5, P], o_ss + 2 * TP * 4)
        sel_turned = place("sel_turned", [P, 2, 1024], o_sc - 2048)
        sq = place("sq", [P, 2, T], o_v)
        std = place("std", [P, T], o_v + 2 * TB)
        tmp = place("tmp", [P, 2, T], o_v + 3 * TB)
        rec_std = [std[:, :], tmp[:, 0, :]]
        rope = place("rope", [P, 2, T], o_v + 5 * TB)
        relu = place("relu", [P, 2, TP], o_v + 5 * TB)
        X1 = place("X1", [P, 4, TP], 0)
        K = place("K", [P, 4, T], 4 * TB)
        X0 = place("X0", [P, 4, TP], 8 * TB)
        X = [X0, X1]
        s0 = place("s0", [P, 2, NB, P], 4 * TB)
        att_hl = place("att_hl", [P, 2, 4, T], o_tok, f32r)
        rec_hl = place("rec_hl", [P, 2, 4, T], o_tok + 8 * TB, f32r)
        v_tok = place("v_tok", [P, 5, 512], o_tok + 8 * TB)
        decayed = place("decayed", [P, 2, 512], o_tok + 8 * TB + 10240)
        v_s = place("v_s", [NB, 512], o_tok + 8 * TB + 14336)
        k_s = place("k_s", [NB, 512], 8 * TB + 4 * TP * 4)
        o_A = o_tok + 16 * TB
        Asc = place("Asc", [P, 4, 512], o_A)
        Atail = place("Atail", [16, 4, 16], o_A + 8192)
        v_blk = place("v_blk", [NB, NB, P], o_A + 8448)
        merged = place("merged", [P, 2, KT, T], 0, f32r)
        gate_s = place("gate_s", [P, 2, T], 16 * TB)
        mix = place("mix", [P, 2, T], 18 * TB)
        hidden = place("hidden", [P, 2, 12, T], 0, f32r)
        silu = place("silu", [P, T], 24 * TB)
        act_f = place("act_f", [P, T], 25 * TB)
        x_rows = place("x_rows", [P, 5, DM], 0)
        y_rows = place("y_rows", [P, 2, DM], 12 * TB)
        level_f = place("level_f", [P, 8, P], 12 * TB)

        acc = [ctx.enter_context(nc.psum_tensor(f"acc{i}", [P, 2, 512], f32)) for i in range(2)]
        work = [ctx.enter_context(nc.psum_tensor(f"work{i}", [P, 1024], f32)) for i in range(2)]

        def pair(w):
            return w[:, :].rearrange("p (a b) -> p a b", a=2)[:, :, 0:HT]

        def halves(ap):
            return ap.rearrange("p (a b) -> p a b", a=2)

        def C(name, rows=None):
            at, r, c = where[name]
            return cst[0:(rows or r), at:at + c]

        raw_ready = [sem(f"raw_ready{i}") for i in range(4)]
        hi_done, lo_done = sem("hi_done"), sem("lo_done")
        unit_done = sem("unit_done")
        taken = [sem(f"taken{i}") for i in range(2)]
        filled = [sem(f"filled{i}") for i in range(2)]
        drained = [sem(f"drained{i}") for i in range(2)]
        qk_filled = [sem(f"qk_filled{i}") for i in range(2)]
        qk_drained = [sem(f"qk_drained{i}") for i in range(2)]
        S = {n: sem(n) for n in (
            "vector_order scalar_order gpsimd_order loads_ready x_landed x_ready par_ready squares squares_used "
            "normed_f normed_hi normed_lo qk_squares qk_normed roped dup_landed ki_dup_landed rope_landed "
            "page_rows_ready pages_gathered0 pages_gathered1 index_done dots_done topk bounds_exp x_turned "
            "weights_ready count_ready count_done list_part mask_counts slots_ready flag_ready "
            "masks_ready setup rows_ready k_gathered v_gathered row_mask exps probs att_hi att_lo q_sel_ready "
            "sel_scores sel_exp sel_probs_ready sel_out att_ready tok_stored "
            "forget scores_cleared log_forget decay_sum lev_diff lev_exp lev_ready q_decayed decay_last k_exp k_decayed state_ready state_stored "
            "v_blk_ready s0_landed0 s0_landed1 s0_ready s0_stored rec_squares rec_f rec_hi rec_lo mixed merged_hi merged_lo "
            "x_updated act_done hid_hi hid_lo layer_begun held y_ready y_stored0 y_stored1").split()}

        NORMS = 2

        def wait(eng, name, L, per, n):
            eng.wait_ge(S[name], L * per + n)

        def hold(eng):
            eng.sem_inc(S["held"], 1)

        def slot_of(item):
            return ITEM[item] % 2

        def wait_filled(eng, L, item):
            eng.wait_ge(filled[ITEM[item] % 2], L * (ITEMS // 2) + ITEM[item] // 2 + 1)
            return work[ITEM[item] % 2][:, :]

        def wait_drained(eng, L, item):
            eng.wait_ge(drained[ITEM[item] % 2], L * (ITEMS // 2) + ITEM[item] // 2 + 2)

        class Order:

            def __init__(self, eng, s, L, per):
                self.eng, self.s, self.L, self.per, self.n = eng, s, L, per, 0

            def __call__(self, ins):
                ins.then_inc(self.s, 1)
                self.n += 1

            def settle(self):
                self.eng.wait_ge(self.s, self.L * self.per + self.n)

            def end(self, start=0):
                assert self.n == self.per, ("signals a layer", self.n, "declared", self.per)

        VEC, SCA = t["steps"]

        def wait_unit(eng, L, u):
            eng.wait_ge(unit_done, L * UNITS + u + 3)

        def take(ins, o):
            ins.then_inc(taken[o % 2], 1)

        def store_state(sync, L, h):
            wait(sync, "s0_ready", L, 32, 8 * h + 8)
            sync.dma_start(out[9][ds(L, 1), :, h, :, :].rearrange("l b k v -> k (l b) v"), s0[:, h % 2, :, :])\
                .then_inc(S["s0_stored"], 16)

        def relu_buf(m, n, w):
            return relu[0:n, m % 2, 0:w]

        block = ctx.enter_context(nc.Block())

        @block.sync
        def _(sync):
            sync.sem_inc(hi_done, 4)
            sync.sem_inc(lo_done, 4)
            sync.sem_inc(unit_done, 2)
            for i in range(2):
                sync.sem_inc(qk_drained[i], 1)
            sync.sem_inc(S["x_updated"], 1)
            sync.sem_inc(S["state_stored"], 16)
            for i in range(2):
                sync.sem_inc(taken[i], 1)
                sync.sem_inc(drained[i], 1)
            sync.dma_start(x_rows[0:META, 0, :], t["meta_tokens"]).then_inc(S["x_landed"], 16)
            xp = t["x_prompt"][0]
            sync.dma_start(x_rows[META:P, 0, :], xp[0:P - META, :]).then_inc(S["x_landed"], 16)
            sync.dma_start(x_rows[:, 1:4, :], xp[112:496, :].rearrange("(j p) d -> p j d", p=P)).then_inc(S["x_landed"], 16)
            sync.dma_start(x_rows[0:16, 4, :], xp[496:512, :]).then_inc(S["x_landed"], 16)
            sync.dma_start(x_rows[16:24, 4, :], t["x_sample"][:, 0, :]).then_inc(S["x_landed"], 16)
            sync.dma_start(cst[:, :], csts[:, 0:t["resident"]]).then_inc(S["loads_ready"], 16)
            sync.dma_start(level_f[:, :, :], t["levels"]).then_inc(S["loads_ready"], 16)
            pt = t["page_table"]
            sync.dma_start(pages_i[:, :], pt.rearrange("b (g o) -> (b g) o", o=1)).then_inc(S["loads_ready"], 16)
            for l in range(DEPTH):
                for at, src, n in ((0, t["norm_mix"][l], KT), (8, t["norm_ffn"][l], KT), (18, t["rec_norm"][l], 1),
                                   (19, t["lb_raw"][l], 4)):
                    sync.dma_start(params[:, l, at:at + n], src.rearrange("(k p) -> p k", p=P),
                                   allow_slow_non_contiguous=True).then_inc(S["loads_ready"], 16)
                for at, src in ((16, t["q_norm"][l]), (17, t["k_norm"][l])):
                    for half in range(2):
                        sync.dma_start(params[64 * half:64 * half + 64, l, at:at + 1],
                                       src.rearrange("(p o) -> p o", o=1)).then_inc(S["loads_ready"], 16)

            with sync.Fori(0, DEPTH) as L:
                def load(u, q, slot, src, kt):
                    sync.wait_ge(hi_done, L * UNITS + u + 1)
                    sync.wait_ge(lo_done, L * UNITS + u + 1)
                    if isinstance(u, int):
                        hold(sync)
                    sync.dma_start(raw[slot][:, 0:kt, :], src).then_inc(raw_ready[slot], 16)

                def cols(w, col, lo=0, kt=KT):
                    return w[ds(L, 1), lo * P:(lo + kt) * P, ds(col, P)].rearrange("l (k p) n -> p (l k) n", p=P)

                first = where["cos"][0]
                sync.wait_ge(S["layer_begun"], L + 1)
                hold(sync)
                sync.dma_start(rope[:, :, :], csts[:, first:first + 2 * T].rearrange("p (a t) -> p a t", a=2))\
                    .then_inc(S["rope_landed"], 16)
                for n, tile in enumerate(A_TILES):
                    load(n, n // 4, n % 4, cols(t["w_in"], tile * P), KT)
                for n in range(13, 16):
                    sync.wait_ge(lo_done, L * UNITS + n + 1)
                    sync.sem_inc(raw_ready[n % 4], 16)
                with sync.Fori(0, 4) as g:
                    for i in range(4):
                        load(UB + g * 4 + i, UB // 4 + g, i, cols(t["w_in"], 1608 + g * 512 + i * P), KT)
                def load_merge(g):
                    load(UM + g * 4, UM // 4 + g, 0, cols(t["w_in"], 3656 + g * P), KT)
                    load(UM + g * 4 + 1, UM // 4 + g, 1, cols(t["w_in"], 4680 + g * P), KT)
                    load(UM + g * 4 + 2, UM // 4 + g, 2, cols(t["w_pa"], g * P, 0, 4), 4)
                    load(UM + g * 4 + 3, UM // 4 + g, 3, cols(t["w_pb"], g * P, 0, 4), 4)

                load_merge(0)
                wait_drained(sync, L, ("tokens", 4))
                wait_drained(sync, L, ("tokens", 3))
                kp, vp, kip, ksm, vsm, kism = out[2], out[3], out[4], out[6], out[7], out[8]
                for dst, lo, n in ((kp, 0, 256), (vp, 256, 256), (kip, 512, 64)):
                    d = dst[ds(L, 1), 0, :, :].rearrange("l t c -> (l t) c")
                    sync.dma_start(d[0:512, :].rearrange("(j p) c -> p j c", p=P), tok[:, 0:4, lo:lo + n])\
                        .then_inc(S["tok_stored"], 16)
                    sync.dma_start(d[512:528, :], tok[0:16, 4, lo:lo + n]).then_inc(S["tok_stored"], 16)
                for dst, lo, n in ((ksm, 0, 256), (vsm, 256, 256), (kism, 512, 64)):
                    sync.dma_start(dst[ds(L, 1), :, 0, :].rearrange("l b c -> (l b) c"), tok[16:24, 4, lo:lo + n])\
                        .then_inc(S["tok_stored"], 16)
                for h in range(4):
                    if h < 2:
                        wait(sync, "k_decayed", L, 1, 1)
                        hold(sync)
                        wait_filled(sync, L, "k_sample")
                        hold(sync)
                    else:
                        sync.wait_ge(S["s0_stored"], L * 64 + 16 * (h - 1))
                        hold(sync)
                        wait_filled(sync, L, ("rec_sample", h - 2))
                        hold(sync)
                    sync.dma_start(s0[:, h % 2, :, :],
                                   t["state_rec"][ds(L, 1), :, h, :, :].rearrange("l b k v -> k (l b) v"))\
                        .then_inc(S[f"s0_landed{h % 2}"], 16)
                    if h >= 1:
                        store_state(sync, L, h - 1)
                store_state(sync, L, 3)
                wait(sync, "state_ready", L, 20, 20)
                sync.dma_start(out[5][ds(L, 1), 0, :, :, :].rearrange("l h k v -> k (l h) v"), state[:, :, :])\
                    .then_inc(S["state_stored"], 16)
                hold(sync)
                with sync.Fori(1, KT) as g:
                    load_merge(g)
                with sync.Fori(0, 2) as g:
                    for i in range(4):
                        load(UO + g * 4 + i, UO // 4 + g, i, cols(t["w_o"], g * 512 + i * P), KT)
                for part in range(2):
                    n0 = 12 * part
                    with sync.Fori(0, HID[part] // 2) as g:
                        for i in range(4):
                            col = (i % 2) * DFF + (n0 + i // 2) * P
                            load(UG[part] + g * 4 + i, UG[part] // 4 + g, i, cols(t["w_gu"], g * 256 + col), KT)
                    kt = HID[part] // 2
                    with sync.Fori(0, 4) as g:
                        for i in range(4):
                            load(UD[part] + g * 4 + i, UD[part] // 4 + g, i,
                                 cols(t["w_down"], g * 256 + (i // 2) * P, n0 + kt * (i % 2), kt), kt)
                sync.wait_ge(S["tok_stored"], L * 144 + 144)
                hold(sync)
            for j, (r0, n) in enumerate(TILES_ALL):
                sync.wait_ge(S["y_ready"], j + 1)
                if j == 0:
                    sync.dma_start(out[0][0, 0:112, :], y_rows[16:128, 0, :]).then_inc(S[f"y_stored{j % 2}"], 16)
                elif j < 4:
                    sync.dma_start(out[0][0, 128 * j - 16:128 * j + 112, :], y_rows[:, j % 2, :])\
                        .then_inc(S[f"y_stored{j % 2}"], 16)
                else:
                    sync.dma_start(out[0][0, 496:512, :], y_rows[0:16, 0, :]).then_inc(S[f"y_stored{j % 2}"], 16)
                    sync.dma_start(out[1][:, 0, :], y_rows[16:24, 0, :]).then_inc(S[f"y_stored{j % 2}"], 16)
            sync.wait_ge(S["y_stored0"], 64)
            sync.wait_ge(S["y_stored1"], 32)
            sync.wait_ge(S["s0_stored"], 64 * DEPTH)
            sync.wait_ge(S["state_stored"], 16 * DEPTH + 16)

        @block.gpsimd
        def _(pool):
            pool.wait_ge(S["par_ready"], 1)
            with pool.Fori(0, DEPTH) as L:
                def rest(u, slot, kt):
                    s = slot % 2
                    pool.wait_ge(hi_done, L * UNITS + u + 5)
                    pool.tensor_tensor(w_lo[s][:, 0:kt, :], raw[slot][:, 0:kt, :], w_hi[s][:, 0:kt, :].bitcast(f32),
                                       ALU.subtract).then_inc(lo_done, 1)

                pool.wait_ge(S["page_rows_ready"], L * 8 + 8)
                pages = t["cache_idx_k"].rearrange("l g (q s) d -> (l g q) (s d)", q=4)

                def gather_pages(q):
                    if q >= 2:
                        wait_filled(pool, L, ("key_turn", 2 * (q - 2) + 1))
                    hold(pool)
                    pool.indirect_dma_start(idx_pages[:, q % 2, :], None, pages,
                                            bass.IndirectOffsetOnAxis(page_rows[:, q:q + 1].bitcast(u32), 0))\
                        .then_inc(S[f"pages_gathered{q % 2}"], 16)

                gather_pages(0)
                gather_pages(1)
                for n in range(13):
                    rest(n, n % 4, KT)
                pool.wait_ge(raw_ready[1], L * (UNITS // 4 * 16) + 3 * 16 + 16)
                pool.wait_ge(raw_ready[2], L * (UNITS // 4 * 16) + 3 * 16 + 16)
                pool.wait_ge(raw_ready[3], L * (UNITS // 4 * 16) + 3 * 16 + 16)
                hold(pool)
                pool.drain().then_inc(lo_done, 3)
                po = Order(pool, S["gpsimd_order"], L, 11)
                pool.wait_ge(S["rope_landed"], L * 16 + 16)
                hold(pool)
                for m, n in enumerate((12, 8, 9, 10, 11, *order)):
                    rows = 64 if n == 12 else P
                    wait_filled(pool, L, ("rope", n))
                    po(pool.tensor_tensor(A[0:rows, n, :], A[0:rows, n, :], rope[0:rows, 0, :], ALU.mult))
                    po.settle()
                    wait_drained(pool, L, ("rope", n))
                    hold(pool)
                    pool.tensor_tensor(A[0:rows, n, :], A[0:rows, n, :], tmp[0:rows, m % 2, :], ALU.add)\
                        .then_inc(S["roped"], 1)
                gather_pages(2)
                gather_pages(3)
                with pool.Fori(0, 4) as g:
                    for i in range(4):
                        rest(UB + g * 4 + i, i, KT)
                wait(pool, "rows_ready", L, 2, 1)
                hold(pool)
                for src, dst, done in ((t["cache_k"], k_sel, "k_gathered"), (t["cache_v"], v_sel, "v_gathered")):
                    rows = src.rearrange("l g s n d -> (l g s) (n d)")
                    for i in range(16):
                        pool.indirect_dma_start(dst[:, i, :], None, rows,
                                                bass.IndirectOffsetOnAxis(row_idx[:, i:i + 1].bitcast(u32), 0))\
                            .then_inc(S[done], 16)
                wait_filled(pool, L, "sel_pv")
                hold(pool)
                pool.memset(Asc[:, :, :], 0.0).then_inc(S["scores_cleared"], 1)
                pool.memset(Atail[:, :, :], 0.0).then_inc(S["scores_cleared"], 1)
                with pool.Fori(0, KT) as g:
                    for i in range(4):
                        rest(UM + g * 4 + i, i, KT if i < 2 else 4)
                with pool.Fori(0, 2) as g:
                    for i in range(4):
                        rest(UO + g * 4 + i, i, KT)
                for part in range(2):
                    with pool.Fori(0, HID[part] // 2) as g:
                        for i in range(4):
                            rest(UG[part] + g * 4 + i, i, KT)
                    with pool.Fori(0, 4) as g:
                        for i in range(4):
                            rest(UD[part] + g * 4 + i, i, HID[part] // 2)

        @block.tensor
        def _(pe):
            ident = C("ident")

            def transpose(dst, src):
                k = src.shape[0]
                return pe.transpose(dst, src, ident[0:k, 0:k])

            pe.wait_ge(S["loads_ready"], 304)
            pe.wait_ge(S["x_landed"], 80)
            for k in range(KT):
                if k >= 2:
                    pe.wait_ge(S["x_ready"], k - 1)
                for j, (r0, n) in enumerate(TILES_ALL):
                    mm = transpose(acc[k % 2][:, :, :].rearrange("p a b -> p (a b)")[:, r0:r0 + n],
                                   x_rows[0:n, j, k * P:(k + 1) * P])
                mm.then_inc(S["x_turned"], 1)
            with pe.Fori(0, DEPTH) as L:
                def begin(item):
                    pe.wait_ge(drained[slot_of(item)], L * (ITEMS // 2) + ITEM[item] // 2 + 1)
                    return work[slot_of(item)][:, :]

                def finish(mm, item):
                    mm.then_inc(filled[slot_of(item)], 1)

                def unit(u, s, kt, mov, k0, o, q, start=True, stop=True, fresh=None):
                    pe.wait_ge(lo_done, L * UNITS + u + 5)
                    if start:
                        pe.wait_ge(taken[o], L * (OUTS // 2) + q + 1)
                    n = 0
                    for k in range(kt):
                        if fresh is not None:
                            wait(pe, "normed_lo", L, NORMS * KT, fresh * KT + k + 1)
                        for w, part in ((w_hi, 0), (w_hi, 1), (w_lo, 0)):
                            for half in range(2):
                                mm = pe.matmul(acc[o][:, half, 0:HT], w[s][:, k, :],
                                               mov[:, part, k0 + k, half * HT:(half + 1) * HT],
                                               start=start and n == 0, stop=stop and n == 3 * kt - 1)
                            n += 1
                    mm.then_inc(unit_done, 1)

                def norm(item, w):
                    ps = begin(item)
                    for k in range(KT):
                        wait(pe, "squares", L, NORMS * KT, w * KT + k + 1)
                        for half in range(2):
                            mm = pe.matmul(pair(ps)[:, half, :], C("ones"), sq[:, k % 2, half * HT:(half + 1) * HT],
                                           start=k == 0, stop=k == KT - 1)
                        if k < KT - 1:
                            mm.then_inc(S["squares_used"], 1)
                    finish(mm, item)

                norm("norm1", 0)
                unit(UA, 0, KT, normed, 0, 0, 0, fresh=0)
                unit(UA + 1, 1, KT, normed, 0, 1, 0)
                with pe.Fori(1, 6) as g:
                    for i in range(2):
                        unit(UA + g * 2 + i, i, KT, normed, 0, i, g)
                unit(12, 0, KT, normed, 0, 0, 6)
                pe.drain().then_inc(unit_done, 3)

                def rope_item(n):
                    ps = begin(("rope", n))
                    if n < 6:
                        wait(pe, "qk_normed", L, 6, order.index(n) + 1)
                    else:
                        pe.wait_ge(taken[0], L * (OUTS // 2) + 8)
                        pe.wait_ge(taken[1], L * (OUTS // 2) + 8)
                    for half in range(2):
                        mm = pe.matmul(pair(ps)[:, half, :], C("rot"), A[:, n, half * HT:(half + 1) * HT],
                                       start=True, stop=True)
                    finish(mm, ("rope", n))

                def sumsq_item(item, count, per, mat, slot, name):
                    ps = begin(item)
                    wait(pe, name, L, per, count)
                    for half in range(2):
                        mm = pe.matmul(pair(ps)[:, half, :], C(mat), sq[:, slot, half * HT:(half + 1) * HT],
                                       start=True, stop=True)
                    finish(mm, item)

                for n in (12, 8, 9, 10, 11):
                    rope_item(n)
                sumsq_item(("sumsq", 4), 1, 6, "head_ones", 0, "qk_squares")
                for m, n in enumerate(order):
                    if m < 5:
                        sumsq_item(("sumsq", order[m + 1]), m + 2, 6, "head_ones", (m + 1) % 2, "qk_squares")
                    rope_item(n)

                wait(pe, "roped", L, 11, 11)
                ps = begin("sample_tokens")
                for m, n in enumerate((6, 7, 12)):
                    mm = transpose(ps[0:NB, m * P:(m + 1) * P], A[:, n, TP:T])
                finish(mm, "sample_tokens")
                for j, (r0, n) in enumerate(TILES_ALL):
                    ps = begin(("tokens", j))
                    for m, a in enumerate((4, 5, 6, 7, 12)):
                        mm = transpose(ps[0:n, m * P:(m + 1) * P], A[:, a, r0:r0 + n])
                    finish(mm, ("tokens", j))
                ps = begin("swapped")
                pe.matmul(ps[:, 0:32], C("swap"), A[:, 0:4, TP:T], start=True, stop=True)
                mm = pe.matmul(ps[:, 32:64], C("swap"), A[:, 8:12, TP:T], start=True, stop=True)
                finish(mm, "swapped")
                ps = begin("index_weights")
                wait_drained(pe, L, "sample_tokens")
                mm = pe.matmul(ps[:, 0:8], C("row_page"), s_tok[:, 320:328], start=True, stop=True)
                finish(mm, "index_weights")
                ps = begin("new_key_dots")
                wait(pe, "weights_ready", L, 9, 4)
                hold(pe)
                mm = pe.matmul(ps[0:NB, 0:64], A[0:64, 12, TP:T], q_idx[0:64, 0:64], start=True, stop=True)
                finish(mm, "new_key_dots")

                def key_turn(r):
                    ps = begin(("key_turn", r))
                    q = r // 2
                    pe.wait_ge(S[f"pages_gathered{q % 2}"], L * 32 + 16 * (q // 2) + 16)
                    for m in range(8):
                        lo = (r % 2) * 1024 + m * P
                        mm = transpose(ps[:, m * P:(m + 1) * P], idx_pages[:, q % 2, lo:lo + P])
                    finish(mm, ("key_turn", r))

                def key_dots(r):
                    ps = begin(("key_dots", r))
                    wait_drained(pe, L, ("key_turn", r))
                    for m in range(8):
                        mm = pe.matmul(ps[:, m * P:(m + 1) * P], idx_turned[:, r % 2, m * P:(m + 1) * P], q_idx[:, :],
                                       start=True, stop=True)
                    finish(mm, ("key_dots", r))

                key_turn(0)
                for r in range(8):
                    if r < 7:
                        key_turn(r + 1)
                    key_dots(r)
                ps = begin("new_score")
                wait(pe, "index_done", L, 9, 1)
                mm = pe.matmul(ps[:, 0:1], C("row_page"), new_score[:, :], start=True, stop=True)
                finish(mm, "new_score")
                pe.wait_ge(S["ki_dup_landed"], L * 16 + 16)
                for j in range(1, 5):
                    r0, n = TILES[j]
                    for h in range(8):
                        ps = begin(("dots", j, h))
                        hold(pe)
                        p0 = 64 * (h % 2)
                        key = A[0:64, 12, :] if p0 == 0 else ki_dup[64:128, :]
                        for c in range(0, WIDTH[j], 512):
                            w = min(512, WIDTH[j] - c)
                            mm = pe.matmul(ps[0:n, c:c + w], A[p0:p0 + 64, 8 + h // 2, r0:r0 + n], key[:, c:c + w],
                                           start=True, stop=True)
                        finish(mm, ("dots", j, h))
                        wait(pe, "count_ready", L, 32, (j - 1) * 8 + h + 1)
                        pe.matmul(acc[0][:, 0, 500:501], C("page_ones"), counts[:, 0:1], start=True, stop=True)\
                            .then_inc(S["count_done"], 1)
                ps = begin("ties")
                wait(pe, "mask_counts", L, 3, 2)
                pe.matmul(ps[:, 0:2], C("page_ones"), counts[:, :], start=True, stop=True)
                mm = pe.matmul(ps[:, 2:4], C("page_before"), counts[:, :], start=True, stop=True)
                finish(mm, "ties")
                ps = begin("starts")
                wait(pe, "mask_counts", L, 3, 3)
                mm = pe.matmul(ps[:, 0:1], C("page_before"), counts[:, 0:1], start=True, stop=True)
                finish(mm, "starts")
                with pe.Fori(0, 8) as g:
                    for i in range(2):
                        unit(UB + g * 2 + i, i, KT, normed, 0, i, OB // 2 + g)

                pe.wait_ge(S["dup_landed"], L * 64 + 64)

                def qk(h, j):
                    r0, n = TILES[j]
                    s, step = h % 2, (h // 2) * 5 + j
                    ps = acc[s][:, :, :].rearrange("p a b -> p (a b)")
                    pe.wait_ge(qk_drained[s], L * 20 + step + 1)
                    hold(pe)
                    kv, p0 = h // 2, 64 * (h % 2)
                    key = A[p0:p0 + 64, 4 + kv // 2, :] if 64 * (kv % 2) == p0 else k_dup[p0:p0 + 64, kv // 2, :]
                    for c in range(0, WIDTH[j], 512):
                        w = min(512, WIDTH[j] - c)
                        mm = pe.matmul(ps[0:n, c:c + w], A[p0:p0 + 64, h // 2, r0:r0 + n], key[:, c:c + w],
                                       start=True, stop=True)
                    mm.then_inc(qk_filled[s], 1)

                def turn(h, j):
                    r0, n = TILES[j]
                    e = (h // 2) * 10 + j * 2 + h % 2
                    ps = begin(("turn", h, j))
                    wait(pe, "probs", L, 40, e + 1)
                    hold(pe)
                    for c in range(j + 1):
                        w = min(P, WIDTH[j] - c * P)
                        mm = transpose(ps[0:w, c * P:c * P + n], E[0:n, h % 2, c * P:c * P + w])
                    finish(mm, ("turn", h, j))

                def pv(n2, j):
                    r0, n = TILES[j]
                    ps = begin(("pv", n2, j))
                    for s in range(2):
                        h = 2 * n2 + s
                        wait_drained(pe, L, ("turn", h, j))
                        for c in range(j + 1):
                            w = min(P, WIDTH[j] - c * P)
                            mm = pe.matmul(ps[64 * s:64 * s + 64, 0:n], tok[0:w, c, 256 + n2 * 64:320 + n2 * 64],
                                           pT[0:w, s, c, 0:n], start=c == 0, stop=c == j)
                    finish(mm, ("pv", n2, j))

                pe.wait_ge(taken[0], L * (OUTS // 2) + OM // 2 + 1)
                pe.wait_ge(taken[1], L * (OUTS // 2) + OM // 2 + 1)
                hold(pe)
                qk(0, 0)
                qk(1, 0)
                for n2 in range(4):
                    for j in range(5):
                        if n2 * 5 + j < 19:
                            nn, nj = (n2, j + 1) if j < 4 else (n2 + 1, 0)
                            qk(2 * nn, nj)
                            qk(2 * nn + 1, nj)
                        turn(2 * n2, j)
                        turn(2 * n2 + 1, j)
                        pv(n2, j)
                    if n2 == 0:
                        ps = begin("new_flag")
                        wait(pe, "flag_ready", L, 1, 1)
                        mm = pe.matmul(ps[0:NB, 0:1], C("page_row"), unpicked[:, :], start=True, stop=True)
                        finish(mm, "new_flag")
                        wait(pe, "slots_ready", L, 2, 2)
                        for r in range(4):
                            ps = begin(("slots", r))
                            for m in range(4):
                                half, b = r // 2, 4 * (r % 2) + m
                                at = (m // 2) * 512 + (m % 2) * 137
                                mm = pe.matmul(ps[:, at:at + 137], slot_b[:, b, half, :], lists[:, :], start=True, stop=True)
                            finish(mm, ("slots", r))

                pe.wait_ge(S["k_gathered"], L * 256 + 256)

                def sel_turn(r):
                    ps = begin(("sel_turn", r))
                    for m in range(8):
                        mm = transpose(ps[:, m * P:(m + 1) * P], k_sel[:, r * 4 + m // 2, (m % 2) * P:(m % 2) * P + P])
                    finish(mm, ("sel_turn", r))

                def sel_dots(r):
                    ps = begin(("sel_dots", r))
                    wait_drained(pe, L, ("sel_turn", r))
                    wait(pe, "q_sel_ready", L, 4, 4)
                    for m in range(8):
                        i, pr = r * 4 + m // 2, m % 2
                        mm = pe.matmul(ps[:, m * 4:m * 4 + 4], sel_turned[:, r % 2, m * P:(m + 1) * P],
                                       q_sel[:, pr, i % 8, 4 * pr:4 * pr + 4], start=True, stop=True)
                    finish(mm, ("sel_dots", r))

                sel_turn(0)
                sel_turn(1)
                sel_dots(0)
                sel_turn(2)
                sel_dots(1)
                sel_turn(3)
                sel_dots(2)
                sel_dots(3)
                ps = begin("sel_rows")
                wait(pe, "sel_scores", L, 1, 1)
                hold(pe)
                for half in range(2):
                    transpose(ps[0:64, half * P:(half + 1) * P], sel_s[:, half, :])
                for pr in range(2):
                    pe.matmul(ps[0:64, 512:520], q_sel[:, pr, :, :], A[:, 4 + pr, TP:T], start=pr == 0, stop=pr == 1)
                mm = pe.matmul(ps[0:64, 520:521], C("row_head"), flag[:, :], start=True, stop=True)
                finish(mm, "sel_rows")
                ps = begin("sel_probs")
                wait(pe, "sel_probs_ready", L, 2, 2)
                hold(pe)
                for half in range(2):
                    transpose(ps[:, half * 64:half * 64 + 64], sel_p[:, half * P:(half + 1) * P])
                mm = transpose(ps[0:NB, 128:192], sel_new[:, :])
                finish(mm, "sel_probs")
                ps = begin("sel_pv")
                wait_drained(pe, L, "sel_probs")
                pe.wait_ge(S["v_gathered"], L * 256 + 256)
                for pr in range(2):
                    pe.matmul(ps[:, pr * 32:pr * 32 + 32], s_tok[:, pr * P:pr * P + P],
                              sel_pT[0:NB, 128:192].rearrange("p (b h) -> p b h", h=8)[:, :, 4 * pr:4 * pr + 4],
                              start=pr == 0, stop=False, skip_group_check=True)
                for i in range(16):
                    half, b = i // 8, i % 8
                    for pr in range(2):
                        mm = pe.matmul(ps[:, pr * 32 + b * 4:pr * 32 + b * 4 + 4], v_sel[:, i, pr * P:(pr + 1) * P],
                                       sel_pT[:, half * 64 + b * 8 + 4 * pr:half * 64 + b * 8 + 4 * pr + 4],
                                       start=False, stop=i == 15, skip_group_check=True)
                finish(mm, "sel_pv")
                ps = begin("sel_swap")
                wait_drained(pe, L, "sel_pv")
                mm = pe.matmul(ps[:, 0:64], C("swap"), sel_o[:, :, :, :].rearrange("p a b c -> p (a b c)"),
                               start=True, stop=True)
                finish(mm, "sel_swap")

                for place_no, lev in enumerate(LEVELS):
                    if lev < 7:
                        wait(pe, "lev_ready", L, 14, 2 * lev + 2)
                        left = right = X[lev % 2]
                    else:
                        wait(pe, "forget", L, 9, 8)
                        left, right = K, B
                    for hp in range(2):
                        ps = begin(("level", lev, hp))
                        for m in range(8):
                            h, c = 2 * hp + m // 4, m % 4
                            mm = pe.matmul(ps[:, m * P:(m + 1) * P], left[:, h, c * P:(c + 1) * P],
                                           right[:, h, c * P:(c + 1) * P], start=True, stop=True)
                        finish(mm, ("level", lev, hp))
                    if lev >= 3:
                        ps = begin(("level_tail", lev))
                        for h in range(4):
                            mm = pe.matmul(ps[0:16, h * 16:h * 16 + 16], left[:, h, 512:528], right[:, h, 512:528],
                                           start=True, stop=True)
                        finish(mm, ("level_tail", lev))
                    if place_no < 5:
                        r0, n = TILES[place_no]
                        ps = begin(("v_turn", place_no))
                        for h in range(4):
                            mm = transpose(ps[0:n, h * P:(h + 1) * P], B[:, 8 + h, r0:r0 + n])
                        finish(mm, ("v_turn", place_no))
                    elif place_no < 7:
                        name, src = (("v_sample", B[:, 8:12, TP:T]), ("k_sample", K[:, :, TP:T]))[place_no - 5]
                        ps = begin(name)
                        for h in range(4):
                            mm = transpose(ps[0:NB, h * P:(h + 1) * P], src[:, h, :])
                        finish(mm, name)
                def rank1(h):
                    ps = begin(("rank1", h))
                    if h == 0:
                        wait_drained(pe, L, "k_sample")
                    wait(pe, "v_blk_ready", L, 4, h + 1)
                    for half in range(2):
                        mm = pe.matmul(ps[:, half * 512:(half + 1) * 512], k_s[:, h * P:(h + 1) * P],
                                       v_blk[:, half * 4:half * 4 + 4, :], start=True, stop=True)
                    finish(mm, ("rank1", h))

                def rec_sample(h):
                    ps = begin(("rec_sample", h))
                    wait(pe, "s0_ready", L, 32, 8 * h + 8)
                    for b in range(NB):
                        mm = pe.matmul(ps[:, b:b + 1], s0[:, h % 2, b, :], B[:, h, TP + b:TP + b + 1], start=True, stop=True)
                    finish(mm, ("rec_sample", h))

                for c in range(5):
                    r0, n = TILES[c]
                    ps = begin(("decayed", c))
                    wait(pe, "k_decayed", L, 1, 1)
                    for h in range(4):
                        mm = transpose(ps[0:n, h * P:(h + 1) * P], X1[:, h, r0:r0 + n])
                    finish(mm, ("decayed", c))
                    ps = begin(("rec_out", c))
                    wait(pe, "q_decayed", L, 1, 1)
                    wait(pe, "state_ready", L, 20, 4 * c) if c else wait(pe, "forget", L, 9, 9)
                    for h in range(4):
                        a = Asc[:, h, c * P:(c + 1) * P] if c < 4 else Atail[:, h, :]
                        pe.matmul(ps[:, h * P:h * P + n], v_tok[0:n, c, h * P:(h + 1) * P], a, start=True, stop=False)
                        mm = pe.matmul(ps[:, h * P:h * P + n], state[:, h, :], B[:, h, r0:r0 + n], start=False, stop=True)
                    finish(mm, ("rec_out", c))
                    ps = begin(("state", c))
                    wait_drained(pe, L, ("decayed", c))
                    for h in range(4):
                        mm = pe.matmul(ps[:, h * P:(h + 1) * P], decayed[0:n, c % 2, h * P:(h + 1) * P],
                                       v_tok[0:n, c, h * P:(h + 1) * P], start=True, stop=True)
                    finish(mm, ("state", c))
                    if c < 4:
                        rank1(c)
                    if c:
                        rec_sample(c - 1)
                for h in range(4):
                    sumsq_item(("rec_sumsq", h), h + 1, 4, "ones", h % 2, "rec_squares")
                    if h in (1, 2):
                        hold(pe)
                        unit(UM + h - 1, h - 1, KT, normed, 0, h - 1, OM // 2)

                wait(pe, "att_hi", L, 4, 4)
                wait(pe, "att_lo", L, 4, 4)
                hold(pe)
                unit(UM + 2, 0, 4, att_hl, 0, 0, OM // 2 + 1)
                wait(pe, "rec_hi", L, 4, 4)
                wait(pe, "rec_lo", L, 4, 4)
                hold(pe)
                unit(UM + 3, 1, 4, rec_hl, 0, 1, OM // 2 + 1)
                with pe.Fori(1, KT) as g:
                    unit(UM + g * 4, 0, KT, normed, 0, 0, OM // 2 + g * 2)
                    unit(UM + g * 4 + 1, 1, KT, normed, 0, 1, OM // 2 + g * 2)
                    unit(UM + g * 4 + 2, 0, 4, att_hl, 0, 0, OM // 2 + g * 2 + 1)
                    unit(UM + g * 4 + 3, 1, 4, rec_hl, 0, 1, OM // 2 + g * 2 + 1)
                wait(pe, "merged_hi", L, 8, 8)
                wait(pe, "merged_lo", L, 8, 8)
                hold(pe)
                with pe.Fori(0, 4) as g:
                    for i in range(2):
                        unit(UO + g * 2 + i, i, KT, merged, 0, i, OO // 2 + g)
                norm("norm2", 1)
                unit(UG[0], 0, KT, normed, 0, 0, OG[0] // 2, fresh=1)
                unit(UG[0] + 1, 1, KT, normed, 0, 1, OG[0] // 2)
                for part in range(2):
                    with pe.Fori(1 - part, HID[part]) as g:
                        for i in range(2):
                            unit(UG[part] + g * 2 + i, i, KT, normed, 0, i, OG[part] // 2 + g)
                    kt = HID[part] // 2
                    wait(pe, "hid_lo", L, 22, 12 if part == 0 else 22)
                    wait(pe, "hid_hi", L, 22, 12 if part == 0 else 22)
                    hold(pe)
                    with pe.Fori(0, 4) as g:
                        for i in range(4):
                            unit(UD[part] + g * 4 + i, i % 2, kt, hidden, kt * (i % 2), i // 2, OD[part] // 2 + g,
                                 start=i % 2 == 0, stop=i % 2 == 1)
                if ITEM.get("none") is not None:
                    pe.wait_ge(drained[1], L * (ITEMS // 2) + ITEMS // 2)
                    hold(pe)
                    pe.drain().then_inc(filled[1], 1)
            pe.wait_ge(S["x_updated"], 24 * DEPTH + 1)
            for j, (r0, n) in enumerate(TILES_ALL):
                pe.wait_ge(drained[j % 2], DEPTH * (ITEMS // 2) + j // 2 + 1)
                for k in range(KT):
                    mm = transpose(work[j % 2][0:n, k * P:(k + 1) * P], x[:, k, r0:r0 + n])
                mm.then_inc(filled[j % 2], 1)

        @block.scalar
        def _(act):
            for k in range(KT):
                act.wait_ge(S["x_turned"], k + 1)
                act.activation(x[:, k, :], acc[k % 2][:, :, :].rearrange("p a b -> p (a b)")[:, 0:T], ACT.Copy)\
                    .then_inc(S["x_ready"], 1)
            act.wait_ge(S["setup"], 1)
            act.wait_ge(S["loads_ready"], 304)
            act.wait_ge(S["masks_ready"], 2)
            act.wait_ge(S["x_ready"], KT)
            act.activation(lb_tmp[:, 2:4, :], lb_tmp[:, 0:2, :], ACT.Exp).then_inc(S["bounds_exp"], 1)
            with act.Fori(0, DEPTH) as L:
                so = Order(act, S["scalar_order"], L, SCA)

                def drain_to(dst, item, func=ACT.Copy, src=None, **kw):
                    ps = wait_filled(act, L, item)
                    act.activation(dst, ps if src is None else src, func, **kw).then_inc(drained[slot_of(item)], 1)

                def norm(item, w):
                    if w == 0:
                        act.wait_ge(S["x_updated"], L * 24 + 1)
                    for k in range(KT):
                        if w == 1:
                            wait(act, "x_updated", L, 24, k + 2)
                        else:
                            act.wait_ge(S["rope_landed"], L * 16 + 16)
                        if k >= 2:
                            act.wait_ge(S["squares_used"], L * (2 * (KT - 1)) + w * (KT - 1) + k - 1)
                        act.activation(sq[:, k % 2, :], x[:, k, :], ACT.Square).then_inc(S["squares"], 1)
                    drain_to(halves(std[:, :]), item, ACT.Sqrt, pair(work[slot_of(item)]), scale=1.0 / DM, bias=eps[:, 0:1])
                    for k in range(KT):
                        wait(act, "normed_f", L, NORMS * KT, w * KT + k + 1)
                        act.activation(normed[:, 0, k, :], tmp[:, k % 2, :], ACT.Copy).then_inc(S["normed_hi"], 1)

                def split(u, slot, q, kt=KT):
                    act.wait_ge(raw_ready[slot], L * (UNITS // 4 * 16) + q * 16 + 16)
                    act.wait_ge(unit_done, L * UNITS + u + 1)
                    act.activation(w_hi[slot % 2][:, 0:kt, :], raw[slot][:, 0:kt, :], ACT.Copy).then_inc(hi_done, 1)

                split(0, 0, 0)
                split(1, 1, 0)
                norm("norm1", 0)
                for n, tile in enumerate(A_TILES):
                    if n < 11:
                        split(n + 2, (n + 2) % 4, (n + 2) // 4)
                    wait_unit(act, L, n)
                    take(act.activation(halves(A[:, tile, :]), acc[n % 2][:, :, 0:HT], ACT.Copy), n)
                act.drain().then_inc(taken[1], 1)
                act.drain().then_inc(hi_done, 3)
                def qk_square(m):
                    if m == 0:
                        act.wait_ge(taken[0], L * (OUTS // 2) + 8)
                        act.wait_ge(taken[1], L * (OUTS // 2) + 8)
                    if m >= 2:
                        wait_filled(act, L, ("sumsq", order[m - 2]))
                    act.activation(sq[:, m % 2, :], A[:, order[m], :], ACT.Square).then_inc(S["qk_squares"], 1)

                qk_square(0)
                qk_square(1)
                for m, n in enumerate(order):
                    if m >= 1:
                        wait(act, "qk_normed", L, 6, m)
                    drain_to(halves(std[:, :]), ("sumsq", n), ACT.Sqrt, pair(work[slot_of(("sumsq", n))]),
                             scale=1.0 / 64, bias=eps[:, 0:1])
                    if m + 2 < 6:
                        qk_square(m + 2)
                wait(act, "roped", L, 11, 11)
                act.dma_start(ki_dup[64:128, :], A[0:64, 12, :]).then_inc(S["ki_dup_landed"], 16)
                for m in range(2):
                    act.dma_start(k_dup[0:64, m, :], A[64:128, 4 + m, :]).then_inc(S["dup_landed"], 16)
                    act.dma_start(k_dup[64:128, m, :], A[0:64, 4 + m, :]).then_inc(S["dup_landed"], 16)
                drain_to(s_tok[:, :], "sample_tokens", src=work[slot_of("sample_tokens")][0:NB, 0:328])
                for j, (r0, n) in enumerate(TILES_ALL):
                    drain_to(tok[0:n, j, :], ("tokens", j), src=work[slot_of(("tokens", j))][0:n, 0:584])
                drain_to(swapped[:, :, :].rearrange("p a b -> p (a b)"), "swapped", src=work[slot_of("swapped")][:, 0:64])
                drain_to(new_tmp[:, :], "new_key_dots", ACT.Relu, work[slot_of("new_key_dots")][0:NB, 0:64])

                def key_turn(r):
                    if r >= 2:
                        wait_filled(act, L, ("key_dots", r - 2))
                    drain_to(idx_turned[:, r % 2, :], ("key_turn", r))

                def key_dots(r):
                    if r >= 2:
                        wait(act, "index_done", L, 9, r)
                    drain_to(idx_relu[:, r % 2, :], ("key_dots", r), ACT.Relu)

                key_turn(0)
                for r in range(8):
                    if r < 7:
                        key_turn(r + 1)
                    key_dots(r)
                split(UB, 0, UB // 4)
                split(UB + 1, 1, UB // 4)
                for j in range(1, 5):
                    n = TILES[j][1]
                    for h in range(8):
                        m = (j - 1) * 8 + h
                        if m >= 2:
                            wait(act, "dots_done", L, 32, m - 1)
                        w = WIDTH[j]
                        drain_to(relu_buf(m, n, w), ("dots", j, h), ACT.Relu, work[slot_of(("dots", j, h))][0:n, 0:w])
                wait(act, "index_done", L, 9, 9)
                for kind, func in enumerate((ACT.Silu, ACT.Sigmoid, ACT.Copy, ACT.Silu)):
                    for i in range(4):
                        n = kind * 4 + i
                        split(UB + n + 2, (n + 2) % 4, (UB + n + 2) // 4)
                        wait_unit(act, L, UB + n)
                        take(act.activation(halves(B[:, n, :]), acc[n % 2][:, :, 0:HT], func), OB + n)
                for n2 in range(4):
                    for j in range(5):
                        n, w = TILES[j][1], WIDTH[j]
                        for s in range(2):
                            e = n2 * 10 + j * 2 + s
                            wait(act, "row_mask", L, 40, e + 1)
                            act.activation(E[0:n, s, 0:w], E[0:n, s, 0:w], ACT.Exp, bias=row_st[0:n, s, 1:2],
                                           accum_out=row_st[0:n, s, 2:3]).then_inc(S["exps"], 1)
                        for s in range(2):
                            h = 2 * n2 + s
                            ps = wait_filled(act, L, ("turn", h, j))
                            if j < 4:
                                act.activation(pT[:, s, 0:j + 1, 0:n], ps[:, 0:(j + 1) * P].rearrange("p (c t) -> p c t", t=P),
                                               ACT.Copy).then_inc(drained[slot_of(("turn", h, j))], 1)
                            else:
                                so(act.activation(pT[:, s, 0:4, 0:n], ps[:, 0:512].rearrange("p (c t) -> p c t", t=P)[:, :, 0:n],
                                                  ACT.Copy))
                                act.activation(pT[0:16, s, 4, 0:n], ps[0:16, 512:512 + n], ACT.Copy)\
                                    .then_inc(drained[slot_of(("turn", h, j))], 1)
                        r0 = TILES[j][0]
                        drain_to(A[:, n2, r0:r0 + n], ("pv", n2, j), src=work[slot_of(("pv", n2, j))][:, 0:n])
                for r in range(4):
                    if r == 2:
                        wait_filled(act, L, ("sel_dots", 0))
                    if r == 3:
                        wait_filled(act, L, ("sel_dots", 1))
                    drain_to(sel_turned[:, r % 2, :], ("sel_turn", r))
                wait(act, "sel_exp", L, 1, 1)
                act.activation(sel_p[:, 0:257], sel_p[:, 0:257], ACT.Exp, bias=sel_c[:, 1:2], scale=ATT_SCALE,
                               accum_out=sel_c[:, 2:3]).then_inc(S["sel_out"], 1)
                for h in range(4):
                    wait(act, "forget", L, 9, 2 * h + 2)
                    act.activation(B[:, 4 + h, 0:TP], B[:, 4 + h, 0:TP], ACT.Ln).then_inc(S["log_forget"], 1)
                for n in range(4):
                    wait(act, "att_ready", L, 4, 4)
                    act.wait_ge(S["tok_stored"], L * 144 + 144)
                    act.activation(att_hl[:, 0, n, :], A[:, n, :], ACT.Copy).then_inc(S["att_hi"], 1)
                for lev, hs in enumerate(HALVES):
                    w = 512 if hs >= 16 else TP
                    wait(act, "lev_diff", L, 14, 2 * lev + 2)
                    act.activation(X[lev % 2][:, :, 0:w], X[lev % 2][:, :, 0:w], ACT.Exp).then_inc(S["lev_exp"], 1)
                    if lev < 5:
                        n = TILES[lev][1]
                        drain_to(v_tok[0:n, lev, :], ("v_turn", lev), src=work[slot_of(("v_turn", lev))][0:n, 0:512])
                    elif lev == 5:
                        drain_to(v_s[:, :], "v_sample", src=work[slot_of("v_sample")][0:NB, 0:512])
                    else:
                        drain_to(k_s[:, :], "k_sample", src=work[slot_of("k_sample")][0:NB, 0:512])
                wait(act, "decay_sum", L, 20, 20)
                wait_filled(act, L, ("level_tail", 5))
                so(act.activation(last_decay[:, :, 0:4], B[:, 4:8, 0:512].rearrange("p h (c t) -> p h c t", t=P)[:, :, :, P - 1],
                                  ACT.Exp))
                so(act.activation(last_decay[:, :, 4:5], B[:, 4:8, TP - 1:TP], ACT.Exp))
                act.activation(X1[:, :, :], B[:, 4:8, 0:TP], ACT.Exp).then_inc(S["decay_last"], 1)
                wait(act, "q_decayed", L, 1, 1)
                for c, (r0, n) in enumerate(TILES):
                    for h in range(4):
                        act.activation(X1[:, h, r0:r0 + n], B[:, 4 + h, r0:r0 + n], ACT.Exp, scale=-1.0,
                                       bias=B[:, 4 + h, r0 + n - 1:r0 + n]).then_inc(S["k_exp"], 1)
                for c, (r0, n) in enumerate(TILES):
                    if c >= 2:
                        wait_filled(act, L, ("state", c - 2))
                    drain_to(decayed[0:n, c % 2, :], ("decayed", c), src=work[slot_of(("decayed", c))][0:n, 0:512])
                    ps = work[slot_of(("rec_out", c))][:, 0:512].rearrange("p (h t) -> p h t", t=P)[:, :, 0:n]
                    drain_to(B[:, 8:12, r0:r0 + n], ("rec_out", c), src=ps)
                    if c:
                        drain_to(B[:, 7 + c, TP:T], ("rec_sample", c - 1), src=work[slot_of(("rec_sample", c - 1))][:, 0:NB])
                wait_drained(act, L, ("rec_sample", 3))
                wait_drained(act, L, ("rec_sample", 2))

                def rec_square(h):
                    if h >= 2:
                        wait_filled(act, L, ("rec_sumsq", h - 2))
                    act.activation(sq[:, h % 2, :], B[:, 8 + h, :], ACT.Square).then_inc(S["rec_squares"], 1)

                rec_square(0)
                rec_square(1)
                for h in range(4):
                    if h >= 2:
                        wait(act, "rec_f", L, 4, h - 1)
                    drain_to(halves(rec_std[h % 2]), ("rec_sumsq", h), ACT.Sqrt, pair(work[slot_of(("rec_sumsq", h))]),
                             scale=1.0 / P, bias=eps[:, 0:1])
                    if h < 2:
                        rec_square(h + 2)

                def gates(g):
                    for i in range(2):
                        split(UM + g * 4 + i + 2, i + 2, UM // 4 + g, 4)
                        wait_unit(act, L, UM + g * 4 + i)
                        act.activation(halves(gate_s[:, i, :]), acc[i][:, :, 0:HT], ACT.Sigmoid).then_inc(taken[i], 1)

                def merged_high(g):
                    for i in range(2):
                        split(UM + g * 4 + i + 4, i, UM // 4 + g + 1)
                    act.wait_ge(S["mixed"], L * 8 + g + 1)
                    act.activation(merged[:, 0, ds(g, 1), :].rearrange("p a t -> p (a t)"), mix[:, 0, :], ACT.Copy)\
                        .then_inc(S["merged_hi"], 1)

                gates(0)
                for h in range(4):
                    wait(act, "rec_f", L, 4, h + 1)
                    act.activation(rec_hl[:, 0, h, :], B[:, 8 + h, :], ACT.Copy).then_inc(S["rec_hi"], 1)
                wait(act, "rec_lo", L, 4, 4)
                act.wait_ge(S["s0_stored"], L * 64 + 64)
                merged_high(0)
                with act.Fori(1, KT) as g:
                    gates(g)
                    merged_high(g)
                with act.Fori(0, 2) as g:
                    for i in range(4):
                        split(UO + g * 4 + i + 2, (i + 2) % 4, UO // 4 + g + (i + 2) // 4)
                norm("norm2", 1)
                for part in range(2):
                    with act.Fori(0, HID[part] // 2) as g:
                        for e in range(2):
                            i = 2 * e
                            split(UG[part] + g * 4 + i + 2, (i + 2) % 4, UG[part] // 4 + g + (i + 2) // 4)
                            wait_unit(act, L, UG[part] + g * 4 + i)
                            act.activation(halves(silu[:, :]), acc[0][:, :, 0:HT], ACT.Silu).then_inc(taken[0], 1)
                            split(UG[part] + g * 4 + i + 3, (i + 3) % 4, UG[part] // 4 + g + (i + 3) // 4)
                            act.wait_ge(S["act_done"], L * 22 + 12 * part + g * 2 + e + 1)
                            act.activation(hidden[:, 0, ds(g * 2 + e, 1), :].rearrange("p a t -> p (a t)"), act_f[:, :],
                                           ACT.Copy).then_inc(S["hid_hi"], 1)
                    with act.Fori(0, 4 - part) as g:
                        for i in range(4):
                            split(UD[part] + g * 4 + i + 2, (i + 2) % 4, UD[part] // 4 + g + (i + 2) // 4)
                split(UNITS - 2, 2, UNITS // 4 - 1)
                split(UNITS - 1, 3, UNITS // 4 - 1)
                so.end()
                act.wait_ge(S["act_done"], L * 22 + 22)

            for j, (r0, n) in enumerate(TILES_ALL):
                act.wait_ge(filled[j % 2], DEPTH * (ITEMS // 2) + j // 2 + 1)
                if j >= 2:
                    act.wait_ge(S[f"y_stored{j % 2}"], 16 * (j // 2))
                else:
                    act.wait_ge(unit_done, DEPTH * UNITS + 2)
                act.activation(y_rows[0:n, j % 2, :], work[j % 2][0:n, :], ACT.Copy).then_inc(S["y_ready"], 1)
                act.wait_ge(S["y_ready"], j + 1)
                act.sem_inc(drained[j % 2], 1)

        @block.vector
        def _(vec):
            TT, TS, STT = vec.tensor_tensor, vec.tensor_scalar, vec.scalar_tensor_tensor
            vec.sem_inc(S["topk"], 1)
            vec.memset(eps[:, :], EPS).then_inc(S["setup"], 1)
            vec.memset(q_idx[:, :], 0.0).then_inc(S["setup"], 1)
            vec.memset(q_sel[:, :, :, :], 0.0).then_inc(S["setup"], 1)
            vec.memset(row_base[:, :], 0.0)
            vec.wait_ge(S["loads_ready"], 304)
            vec.tensor_copy(level_mask[:, :, :], level_f[:, :, :])
            vec.tensor_copy(pages_f[:, :], pages_i[:, :]).then_inc(S["par_ready"], 1)
            vec.wait_ge(S["par_ready"], 1)
            TS(page_base[:, :], pages_f[:, :], float(PAGE), 1.0, ALU.mult, ALU.add).then_inc(S["masks_ready"], 1)
            raws = params[:, :, 19:23]
            TT(lb_tmp[:, 4, :], raws[:, 0, :], raws[:, 1, :], ALU.max).then_inc(S["setup"], 1)
            vec.wait_ge(S["setup"], 4)
            for l in range(2):
                TT(lb_tmp[:, l, :], raws[:, l, :], lb_tmp[:, 4, :], ALU.subtract).then_inc(S["setup"], 1)
            vec.wait_ge(S["setup"], 6)
            vec.drain().then_inc(S["masks_ready"], 1)
            vec.wait_ge(S["bounds_exp"], 1)
            TT(lb_tmp[:, 4, :], lb_tmp[:, 2, :], lb_tmp[:, 3, :], ALU.add).then_inc(S["setup"], 1)
            vec.wait_ge(S["setup"], 7)
            vec.reciprocal(lb_tmp[:, 5, :], lb_tmp[:, 4, :]).then_inc(S["setup"], 1)
            vec.wait_ge(S["setup"], 8)
            for l in range(2):
                TT(lb_tmp[:, l, :], lb_tmp[:, 2 + l, :], lb_tmp[:, 5, :], ALU.mult).then_inc(S["setup"], 1)
            vec.wait_ge(S["setup"], 10)
            TT(params[:, 0, 19:23], lb_tmp[:, 0, :], lb_tmp[:, 0, :], ALU.subtract).then_inc(S["setup"], 1)
            TT(lb_tmp[:, 4, :], lb_tmp[:, 0, :], lb_tmp[:, 1, :], ALU.add).then_inc(S["setup"], 1)
            vec.wait_ge(S["setup"], 12)
            TT(params[:, 1, 19:23], lb_tmp[:, 4, :], lb_tmp[:, 0, :], ALU.subtract).then_inc(S["setup"], 1)
            vec.wait_ge(S["setup"], 13)
            TS(params[:, :, 23:27], params[:, :, 19:23], -1.0, 1.0, ALU.mult, ALU.add).then_inc(S["setup"], 1)
            vec.wait_ge(S["setup"], 14)
            vec.wait_ge(S["par_ready"], 1)
            TS(page_rows_f[:, :], C("iota")[:, 0:4], 0.0, None, ALU.mult).then_inc(S["setup"], 1)
            vec.wait_ge(S["setup"], 15)
            for q in range(4):
                TS(page_rows_f[:, q:q + 1], pages_f[:, :], 4.0, float(q), ALU.mult, ALU.add).then_inc(S["setup"], 1)
            vec.wait_ge(S["setup"], 19)
            vec.wait_ge(S["x_ready"], KT)

            with vec.Fori(0, DEPTH) as L:
                vo = Order(vec, S["vector_order"], L, VEC)

                def drain_ins(ins, item):
                    ins.then_inc(drained[slot_of(item)], 1)

                vo(vec.tensor_copy(par[:, :], params[:, ds(L, 1), :].rearrange("p a n -> p (a n)")))
                for q in range(4):
                    vec.tensor_copy(page_rows[:, q:q + 1], page_rows_f[:, q:q + 1]).then_inc(S["page_rows_ready"], 1)
                vec.wait_ge(S["page_rows_ready"], L * 8 + 4)
                for q in range(4):
                    TS(page_rows_f[:, q:q + 1], page_rows_f[:, q:q + 1], float(NPOOL * 4), None, ALU.add)\
                        .then_inc(S["page_rows_ready"], 1)
                vec.drain().then_inc(S["layer_begun"], 1)
                vo.settle()

                def norm(item, w):
                    wait_drained(vec, L, item)
                    vo(vec.reciprocal(std[:, :], std[:, :]))
                    vo.settle()

                    def rest(k):
                        wait(vec, "normed_hi", L, NORMS * KT, w * KT + k + 1)
                        TT(normed[:, 1, k, :], tmp[:, k % 2, :], normed[:, 0, k, :].bitcast(f32), ALU.subtract)\
                            .then_inc(S["normed_lo"], 1)

                    for k in range(KT):
                        if k >= 2:
                            wait(vec, "normed_lo", L, NORMS * KT, w * KT + k - 1)
                        STT(tmp[:, k % 2, :], x[:, k, :], par[:, 8 * w + k:8 * w + k + 1], std[:, :], ALU.mult, ALU.mult)\
                            .then_inc(S["normed_f"], 1)
                        if k >= 1:
                            rest(k - 1)
                    rest(KT - 1)

                norm("norm1", 0)

                def rope_tile(n, m):
                    ps = wait_filled(vec, L, ("rope", n))
                    rows = 64 if n == 12 else P
                    if m >= 2:
                        wait(vec, "roped", L, 11, m - 1)
                    drain_ins(TT(halves(tmp[0:rows, m % 2, :]), pair(ps)[0:rows], halves(rope[0:rows, 1, :]), ALU.mult),
                              ("rope", n))

                vec.wait_ge(S["rope_landed"], L * 16 + 16)
                for m, n in enumerate((12, 8, 9, 10, 11)):
                    rope_tile(n, m)

                def qk_norm(m):
                    n = order[m]
                    wait_drained(vec, L, ("sumsq", n))
                    vo(vec.reciprocal(std[:, :], std[:, :]))
                    vo.settle()
                    gain = par[:, 17:18] if n >= 4 else par[:, 16:17]
                    STT(A[:, n, :], A[:, n, :], gain, std[:, :], ALU.mult, ALU.mult).then_inc(S["qk_normed"], 1)

                qk_norm(0)
                for m, n in enumerate(order):
                    if m < 5:
                        qk_norm(m + 1)
                    rope_tile(n, 5 + m)
                wait(vec, "roped", L, 11, 11)

                wait_drained(vec, L, "swapped")
                qi = A[:, 8:12, TP:T].rearrange("p i b -> p b i")
                sw = swapped[:, 4:8, :].rearrange("p i b -> p b i")
                for p0 in (0, 64):
                    dst = q_idx[p0:p0 + 64, p0:p0 + 64].rearrange("p (b i s) -> p b i s", i=4, s=2)
                    s = p0 // 64
                    vec.tensor_copy(dst[:, :, :, s], qi[p0:p0 + 64]).then_inc(S["weights_ready"], 1)
                    vec.tensor_copy(dst[:, :, :, 1 - s], sw[p0:p0 + 64]).then_inc(S["weights_ready"], 1)
                ps = wait_filled(vec, L, "index_weights")
                drain_ins(STT(w_page[:, :, :], ps[:, 0:8].unsqueeze(1).broadcast_to((P, 8, 8)), IDX_SCALE,
                              C("page_row").unsqueeze(2).broadcast_to((P, 8, 8)), ALU.mult, ALU.mult), "index_weights")
                wait_drained(vec, L, "sample_tokens")
                STT(w_new[:, :, :], s_tok[:, 320:328].unsqueeze(1).broadcast_to((NB, 8, 8)), IDX_SCALE,
                    C("ident")[0:8, 0:8].unsqueeze(2).broadcast_to((NB, 8, 8)), ALU.mult, ALU.mult)\
                    .then_inc(S["weights_ready"], 1)
                for p0 in (0, 64):
                    s = p0 // 64
                    for side in range(2):
                        src = (A if side == s else swapped)[p0:p0 + 64]
                        src = src[:, s:4:2, TP:T] if side == s else src[:, s:4:2, :]
                        for pr in range(2):
                            ins = vec.tensor_copy(q_sel[p0:p0 + 64, pr, :, 4 * pr + 2 * s + side], src[:, pr, :])
                            if pr == 0:
                                vo(ins)
                            else:
                                ins.then_inc(S["q_sel_ready"], 1)
                for j, (r0, n) in enumerate(TILES_ALL):
                    wait_drained(vec, L, ("tokens", j))
                    ins = TS(w_tok[0:n, j, :], tok[0:n, j, 576:584], IDX_SCALE, None, ALU.mult)
                    if j < 4:
                        ins.then_inc(S["weights_ready"], 1)
                    else:
                        vo(ins)
                wait_drained(vec, L, "new_key_dots")
                wait(vec, "weights_ready", L, 9, 9)
                vo.settle()
                vo(TT(new_tmp[:, :], new_tmp[:, :], w_new[:, :, :].rearrange("p a b -> p (a b)"), ALU.mult))
                vo.settle()
                vec.tensor_reduce(new_score[:, :], new_tmp[:, :], AX.X, ALU.add).then_inc(S["index_done"], 1)
                wait_drained(vec, L, "index_weights")
                for r in range(8):
                    wait_drained(vec, L, ("key_dots", r))
                    buf = idx_relu[:, r % 2, :].rearrange("p (k c) -> p k c", c=64)
                    vo(TT(buf, buf, w_page[:, :, :].rearrange("p a b -> p (a b)").unsqueeze(1).broadcast_to((P, 16, 64)),
                          ALU.mult))
                    vo.settle()
                    vec.tensor_reduce(sc_page[:, r * 16:r * 16 + 16], buf, AX.X, ALU.add).then_inc(S["index_done"], 1)

                ps = wait_filled(vec, L, "new_score")
                drain_ins(TT(sc_page[:, P:P + 1], ps[:, 0:1], C("not_last"), ALU.add), "new_score")
                wait_drained(vec, L, "new_score")
                vo(vec.memset(trial[:, :], 0))
                vo.settle()
                vo(TS(limit[:, :], trial[:, :], 0xFFFFFFFF, None, ALU.bitwise_xor))

                def count_trial():
                    vo.settle()
                    vo(TS(above[:, :], sc_page[:, :], trial[:, 0:1].bitcast(f32), None, ALU.is_ge))
                    vo.settle()
                    vec.tensor_reduce(counts[:, 0:1], above[:, :], AX.X, ALU.add).then_inc(S["count_ready"], 1)

                def decide(m):
                    wait(vec, "count_done", L, 32, m + 1)
                    vo(TS(enough[:, :], acc[0][:, 0, 500:501], TOPK_S - 0.5, None, ALU.is_ge))
                    vo.settle()
                    hold(vec)
                    vo(vec.copy_predicated(limit[:, :], enough[:, :], trial[:, :]))
                    if m < 31:
                        vo.settle()
                        vo(TS(trial[:, :], limit[:, :], 1 << (30 - m), None, ALU.bitwise_xor))

                count_trial()
                for j in range(1, 5):
                    n, w = TILES[j][1], WIDTH[j]
                    dst = sc[0:n, SC_AT[j]:SC_AT[j] + w]
                    for h in range(8):
                        m = (j - 1) * 8 + h
                        wait_drained(vec, L, ("dots", j, h))
                        wh = w_tok[0:n, j, h:h + 1]
                        if h == 0:
                            ins = TS(dst, relu_buf(m, n, w), wh, None, ALU.mult)
                        else:
                            wait(vec, "dots_done", L, 32, m)
                            ins = STT(dst, relu_buf(m, n, w), wh, dst, ALU.mult, ALU.add)
                        ins.then_inc(S["dots_done"], 1)
                        decide(m)
                        if m < 31:
                            count_trial()
                    wait(vec, "dots_done", L, 32, m + 1)
                    r0 = TILES[j][0]
                    tail = sc[0:n, SC_AT[j] + r0:SC_AT[j] + w]
                    vo(TT(tail, tail, C("causal")[0:n, 0:w - r0], ALU.add))
                vo.settle()
                hold(vec)
                vo(TS(above[:, :], sc_page[:, :], limit[:, 0:1].bitcast(f32), None, ALU.is_gt))
                vo(TS(equal[:, :], sc_page[:, :], limit[:, 0:1].bitcast(f32), None, ALU.is_equal))
                vo.settle()
                vec.tensor_reduce(counts[:, 0:1], above[:, :], AX.X, ALU.add).then_inc(S["mask_counts"], 1)
                vec.tensor_reduce(counts[:, 1:2], equal[:, :], AX.X, ALU.add).then_inc(S["mask_counts"], 1)
                vo(vec.tensor_tensor_scan(rank[:, :], C("ones")[:, 0:1].broadcast_to((P, 129)), equal[:, :], 0.0,
                                          ALU.mult, ALU.add))
                vo(TS(code[:, :], C("iota")[:, 0:129], page_base[:, 0:1], None, ALU.add))
                vo.settle()
                vo(vec.memset(code[:, P:P + 1], float(NPOOL * PAGE + 1)))
                ps = wait_filled(vec, L, "ties")
                vo(TS(ties_left[:, :], ps[:, 0:1], -1.0, float(TOPK_S), ALU.mult, ALU.add))
                vo.settle()
                drain_ins(TT(ties_left[:, :], ties_left[:, :], ps[:, 3:4], ALU.subtract), "ties")
                wait_drained(vec, L, "ties")
                vo(STT(equal[:, :], rank[:, :], ties_left[:, 0:1], equal[:, :], ALU.is_le, ALU.mult))
                vo.settle()
                vo(TT(above[:, :], above[:, :], equal[:, :], ALU.add))
                vo.settle()
                vec.tensor_reduce(counts[:, 0:1], above[:, :], AX.X, ALU.add).then_inc(S["mask_counts"], 1)
                vo(STT(unpicked[:, :], above[:, P:P + 1], 0.5, C("last_page"), ALU.is_lt, ALU.mult))
                vo(TT(code[:, :], code[:, :], above[:, :], ALU.mult))
                vo.settle()
                TS(unpicked[:, :], unpicked[:, :], NEG, None, ALU.mult).then_inc(S["flag_ready"], 1)
                hold(vec)
                with vec.Fori(0, 17) as r:
                    vec.max(top8[:, :], code[:, :]).then_inc(S["list_part"], 1)
                    vec.wait_ge(S["list_part"], L * 51 + r * 3 + 1)
                    hold(vec)
                    vec.tensor_copy(lists[:, ds(r * 8, 8)], top8[:, :]).then_inc(S["list_part"], 1)
                    vec.match_replace(code[:, :], top8[:, :], code[:, :], -1.0).then_inc(S["list_part"], 1)
                    vec.wait_ge(S["list_part"], L * 51 + r * 3 + 3)
                    hold(vec)
                ps = wait_filled(vec, L, "starts")
                vo(vec.tensor_copy(first_slot[:, :], ps[:, 0:1]))
                drain_ins(vec.tensor_copy(lists[:, 136:137], ps[:, 0:1]), "starts")
                vo.settle()
                for half in range(2):
                    vo(TS(slot_d[:, half, :], C("iota")[:, 0:P], first_slot[:, 0:1], float(half * P), ALU.subtract, ALU.add))
                vo.settle()
                vo(TS(slot_o[:, :, :], slot_d[:, :, :], 0.0, None, ALU.is_ge))
                vo.settle()
                wait(vec, "mask_counts", L, 3, 3)
                vo(STT(slot_o[:, :, :], slot_d[:, :, :], counts[:, 0:1], slot_o[:, :, :], ALU.is_lt, ALU.mult))
                vo.settle()
                wait_drained(vec, L, "starts")
                for half in range(2):
                    TT(slot_b[:, :, half, :], slot_o[:, half:half + 1, :].broadcast_to((P, NB, P)),
                       C("page_row").unsqueeze(2).broadcast_to((P, NB, P)), ALU.mult).then_inc(S["slots_ready"], 1)
                hold(vec)
                def score_tile(j):
                    return sc[0:TILES[j][1], SC_AT[j]:SC_AT[j] + WIDTH[j]]

                for pair_no in range(2):
                    d0, d1 = score_tile(2 * pair_no + 1), score_tile(2 * pair_no + 2)
                    t0, t1 = top8[:, :], top8b[0:TILES[2 * pair_no + 2][1], :]
                    with vec.Fori(0, TOPK_P // 8) as r:
                        seen = L * (TOPK_P // 8 * 8) + pair_no * (TOPK_P // 8 * 4) + r * 4 + 1
                        vec.max(t0, d0).then_inc(S["topk"], 1)
                        vec.wait_ge(S["topk"], seen)
                        hold(vec)
                        vec.max(t1, d1).then_inc(S["topk"], 1)
                        vec.wait_ge(S["topk"], seen + 1)
                        hold(vec)
                        vec.match_replace(d0, t0, d0, PICKED).then_inc(S["topk"], 1)
                        vec.wait_ge(S["topk"], seen + 2)
                        hold(vec)
                        vec.match_replace(d1, t1, d1, PICKED).then_inc(S["topk"], 1)
                        vec.wait_ge(S["topk"], seen + 3)
                        hold(vec)
                    vec.wait_ge(S["topk"], L * (TOPK_P // 8 * 8) + (pair_no + 1) * (TOPK_P // 8 * 4) + 1)
                    hold(vec)
                    vo(TS(d0, d0, PICKED, NEG, ALU.is_gt, ALU.mult))
                    vo(TS(d1, d1, PICKED, NEG, ALU.is_gt, ALU.mult))

                def pick_rows():
                    ps = wait_filled(vec, L, "new_flag")
                    drain_ins(vec.tensor_copy(flag[:, :], ps[0:NB, 0:1]), "new_flag")
                    for r in range(4):
                        ps = wait_filled(vec, L, ("slots", r))
                        got = ps[:, :].rearrange("p (k c) -> p k c", k=2)[:, :, 0:274].rearrange("p k (g c) -> p k g c", c=137)
                        rel = slot_l[:, :].rearrange("p (k g) -> p k g", k=2)
                        vo(TS(rel, got[:, :, :, 136], -1.0, C("row_number")[:, r // 2:r // 2 + 1], ALU.mult, ALU.add))
                        vo.settle()
                        vo(TT(slot_x[:, :, :, :], C("iota").rearrange("p (a b c) -> p a b c", a=1, b=1)
                              .broadcast_to((P, 2, 2, 136)), rel.unsqueeze(3).broadcast_to((P, 2, 2, 136)), ALU.is_equal))
                        vo.settle()
                        drain_ins(TT(slot_x[:, :, :, :], slot_x[:, :, :, :], got[:, :, :, 0:136], ALU.mult), ("slots", r))
                        wait_drained(vec, L, ("slots", r))
                        vo(vec.tensor_reduce(picks[:, 4 * r:4 * r + 4].rearrange("p (k g) -> p k g", k=2),
                                             slot_x[:, :, :, :], AX.X, ALU.add))
                        vo.settle()
                    vo(TS(new_mask[:, :], picks[:, :], NPOOL * PAGE + 0.5, NEG, ALU.is_gt, ALU.mult))
                    vo.settle()
                    vo(TS(picks[:, :], picks[:, :], float(NPOOL * PAGE), -1.0, ALU.min, ALU.add))
                    vo.settle()
                    vo(TT(row_idx[:, :], picks[:, :], row_base[:, 0:1].broadcast_to((P, 16)), ALU.add))
                    vo.settle()
                    TS(row_base[:, :], row_base[:, :], float(NPOOL * PAGE), None, ALU.add).then_inc(S["rows_ready"], 1)
                    vec.drain().then_inc(S["rows_ready"], 1)

                for n2 in range(4):
                    for j in range(5):
                        n, w = TILES[j][1], WIDTH[j]
                        mask = sc[0:n, SC_AT[j]:SC_AT[j] + w] if j else C("causal")
                        for s in range(2):
                            h = 2 * n2 + s
                            e = n2 * 10 + j * 2 + s
                            vec.wait_ge(qk_filled[s], L * 20 + n2 * 5 + j + 1)
                            ps = acc[s][:, :, :].rearrange("p a b -> p (a b)")
                            if e >= 2:
                                pj, pn = (j - 1, n2) if j else (4, n2 - 1)
                                wait_filled(vec, L, ("turn", 2 * pn + s, pj))
                            hold(vec)
                            vec.tensor_tensor_reduce(E[0:n, s, 0:w], ps[0:n, 0:w], mask, ATT_SCALE, -3e38,
                                                     ALU.add, ALU.max, row_st[0:n, s, 0:1]).then_inc(qk_drained[s], 1)
                            vec.wait_ge(qk_drained[s], L * 20 + n2 * 5 + j + 2)
                            TS(row_st[0:n, s, 1:2], row_st[0:n, s, 0:1], -1.0, None, ALU.mult).then_inc(S["row_mask"], 1)
                        for s in range(2):
                            e = n2 * 10 + j * 2 + s
                            wait(vec, "exps", L, 40, e + 1)
                            vo(vec.reciprocal(row_st[0:n, s, 3:4], row_st[0:n, s, 2:3]))
                            vo.settle()
                            TS(E[0:n, s, 0:w], E[0:n, s, 0:w], row_st[0:n, s, 3:4], None, ALU.mult).then_inc(S["probs"], 1)
                    if n2 == 0:
                        pick_rows()

                for r in range(4):
                    ps = wait_filled(vec, L, ("sel_dots", r))
                    dst = sel_s[:, :, :].rearrange("p a (b c) -> p (a b) c", c=8)[:, 4 * r:4 * r + 4, :]
                    drain_ins(TT(dst, ps[:, 0:32].rearrange("p (a c) -> p a c", c=8),
                                 new_mask[:, 4 * r:4 * r + 4].unsqueeze(2).broadcast_to((P, 4, 8)), ALU.add),
                              ("sel_dots", r))
                for r in (2, 3):
                    wait_drained(vec, L, ("sel_dots", r))
                hold(vec)
                vec.drain().then_inc(S["sel_scores"], 1)
                ps = wait_filled(vec, L, "sel_rows")
                vo(TT(sel_new[:, :], ps[0:64, 512:520], C("head_row"), ALU.mult))
                vo(vec.tensor_copy(sel_c[:, 3:4], ps[0:64, 520:521]))
                drain_ins(vec.tensor_copy(sel_p[:, 0:256], ps[0:64, 0:256]), "sel_rows")
                vo.settle()
                vo(vec.tensor_reduce(sel_p[:, 256:257], sel_new[:, :], AX.X, ALU.add))
                vo.settle()
                vo(TT(sel_p[:, 256:257], sel_p[:, 256:257], sel_c[:, 3:4], ALU.add))
                vo.settle()
                wait_drained(vec, L, "sel_rows")
                vo(vec.tensor_reduce(sel_c[:, 0:1], sel_p[:, 0:257], AX.X, ALU.max))
                vo.settle()
                TS(sel_c[:, 1:2], sel_c[:, 0:1], -ATT_SCALE, None, ALU.mult).then_inc(S["sel_exp"], 1)
                wait(vec, "sel_out", L, 1, 1)
                vo(vec.reciprocal(sel_c[:, 3:4], sel_c[:, 2:3]))
                vo.settle()
                vo(TS(sel_p[:, 0:257], sel_p[:, 0:257], sel_c[:, 3:4], None, ALU.mult))
                vo.settle()
                TS(sel_new[:, :], C("head_row"), sel_p[:, 256:257], None, ALU.mult).then_inc(S["sel_probs_ready"], 1)
                vec.drain().then_inc(S["sel_probs_ready"], 1)
                ps = wait_filled(vec, L, "sel_probs")
                vo(vec.tensor_copy(sel_pT[:, 0:128], ps[:, 0:128]))
                drain_ins(vec.tensor_copy(sel_pT[0:NB, 128:192], ps[0:NB, 128:192]), "sel_probs")
                ps = wait_filled(vec, L, "sel_pv")
                drain_ins(vec.tensor_copy(sel_o[:, :, :, :].rearrange("p a b c -> p (a b c)"), ps[:, 0:64]), "sel_pv")
                wait_drained(vec, L, "sel_pv")
                ps = wait_filled(vec, L, "sel_swap")
                pso = ps[:, 0:64].rearrange("p (a b c) -> p a b c", a=2, b=NB)
                for s in range(2):
                    for side in range(2):
                        src = (sel_o[:, :, :, :] if side == s else pso)[64 * side:64 * side + 64, :, :, 2 * s + side]
                        vec.tensor_copy(A[64 * side:64 * side + 64, s:4:2, TP:T], src).then_inc(S["att_ready"], 1)
                vec.drain().then_inc(drained[slot_of("sel_swap")], 1)
                wait(vec, "att_ready", L, 4, 4)
                wait_filled(vec, L, "sel_swap")
                for h in range(4):
                    TS(B[:, 4 + h, :], B[:, 4 + h, :], par[:, 23 + h:24 + h], par[:, 19 + h:20 + h], ALU.mult, ALU.add)\
                        .then_inc(S["forget"], 1)
                    wait(vec, "forget", L, 9, 2 * h + 1)
                    TS(K[:, h, :], B[:, 4 + h, :], -1.0, 1.0, ALU.mult, ALU.add).then_inc(S["forget"], 1)
                vec.wait_ge(S["state_stored"], L * 16 + 16)
                vec.memset(state[:, :, :], 0.0).then_inc(S["forget"], 1)
                for h in range(4):
                    wait(vec, "log_forget", L, 4, h + 1)
                    for r0, n in TILES:
                        lf = B[:, 4 + h, r0:r0 + n]
                        vec.tensor_tensor_scan(lf, C("ones")[:, 0:n], lf, 0.0, ALU.mult, ALU.add)\
                            .then_inc(S["decay_sum"], 1)
                wait(vec, "decay_sum", L, 20, 20)
                vo.settle()

                def level_scores(lev, hp):
                    ps = wait_filled(vec, L, ("level", lev, hp))
                    hold(vec)
                    drain_ins(vec.copy_predicated(
                        Asc[:, 2 * hp:2 * hp + 2, :].rearrange("p h (c t) -> p (h c) t", t=P),
                        level_mask[:, lev:lev + 1, :].broadcast_to((P, 8, P)),
                        ps[:, :].rearrange("p (c t) -> p c t", t=P)), ("level", lev, hp))
                    if hp == 1 and lev >= 3:
                        ps = wait_filled(vec, L, ("level_tail", lev))
                        hold(vec)
                        drain_ins(vec.copy_predicated(Atail[:, :, :], level_mask[0:16, lev:lev + 1, 0:16].broadcast_to((16, 4, 16)),
                                                      ps[0:16, 0:64].rearrange("p (h t) -> p h t", t=16)),
                                  ("level_tail", lev))

                for lev, hs in enumerate(HALVES):
                    w = 512 if hs >= 16 else TP
                    xv = X[lev % 2][:, :, 0:w].rearrange("p h (b c) -> p h b c", c=2 * hs)
                    if lev == 1:
                        wait(vec, "att_lo", L, 4, 4)
                        hold(vec)
                    bv = B[:, 4:8, 0:w].rearrange("p h (b c) -> p h b c", c=2 * hs)
                    qv = B[:, 0:4, 0:w].rearrange("p h (b c) -> p h b c", c=2 * hs)
                    kv = K[:, :, 0:w].rearrange("p h (b c) -> p h b c", c=2 * hs)
                    mid = bv[:, :, :, hs - 1:hs].broadcast_to((P, 4, w // (2 * hs), hs))
                    TT(xv[:, :, :, hs:], bv[:, :, :, hs:], mid, ALU.subtract).then_inc(S["lev_diff"], 1)
                    TT(xv[:, :, :, 0:hs], mid, bv[:, :, :, 0:hs], ALU.subtract).then_inc(S["lev_diff"], 1)
                    if lev >= 1:
                        level_scores(lev - 1, 0)
                    else:
                        for n in range(4):
                            wait(vec, "att_hi", L, 4, n + 1)
                            TT(att_hl[:, 1, n, :], A[:, n, :], att_hl[:, 0, n, :].bitcast(f32), ALU.subtract)\
                                .then_inc(S["att_lo"], 1)
                        wait(vec, "scores_cleared", L, 2, 2)
                        level_scores(7, 0)
                    wait(vec, "lev_exp", L, 7, lev + 1)
                    TT(xv[:, :, :, hs:], xv[:, :, :, hs:], qv[:, :, :, hs:], ALU.mult).then_inc(S["lev_ready"], 1)
                    TT(xv[:, :, :, 0:hs], xv[:, :, :, 0:hs], kv[:, :, :, 0:hs], ALU.mult).then_inc(S["lev_ready"], 1)
                    level_scores(lev - 1 if lev else 7, 1)
                wait(vec, "lev_ready", L, 14, 14)
                wait(vec, "decay_last", L, 1, 1)
                TT(B[:, 0:4, 0:TP], X1[:, :, :], B[:, 0:4, 0:TP], ALU.mult).then_inc(S["q_decayed"], 1)
                level_scores(6, 0)
                level_scores(6, 1)
                wait(vec, "k_exp", L, 20, 20)
                TT(X1[:, :, :], X1[:, :, :], K[:, :, 0:TP], ALU.mult).then_inc(S["k_decayed"], 1)
                def make_v_blk(h):
                    TT(v_blk[:, :, :], v_s[:, h * P:(h + 1) * P].unsqueeze(1).broadcast_to((NB, NB, P)),
                       C("ident")[0:8, 0:8].unsqueeze(2).broadcast_to((NB, NB, P)), ALU.mult)\
                        .then_inc(S["v_blk_ready"], 1)

                wait_drained(vec, L, "v_sample")
                make_v_blk(0)
                for c in range(5):
                    ps = wait_filled(vec, L, ("state", c))
                    for h in range(4):
                        if c:
                            wait(vec, "state_ready", L, 20, 4 * c - 3 + h)
                        STT(state[:, h, :], state[:, h, :], last_decay[:, h, c:c + 1], ps[:, h * P:(h + 1) * P],
                            ALU.mult, ALU.add).then_inc(S["state_ready"], 1)
                    vec.drain().then_inc(drained[slot_of(("state", c))], 1)
                    if c < 4:
                        ps = wait_filled(vec, L, ("rank1", c))
                        vec.wait_ge(S[f"s0_landed{c % 2}"], L * 32 + 16 * (c // 2) + 16)
                        for b in range(NB):
                            STT(s0[:, c % 2, b, :], s0[:, c % 2, b, :], B[:, 4 + c, TP + b:TP + b + 1],
                                ps[:, b * P:(b + 1) * P], ALU.mult, ALU.add).then_inc(S["s0_ready"], 1)
                        vec.drain().then_inc(drained[slot_of(("rank1", c))], 1)
                        if c < 3:
                            make_v_blk(c + 1)
                wait_drained(vec, L, ("rec_sample", 3))
                wait_drained(vec, L, ("rec_sample", 2))
                for h in range(4):
                    vo(TT(B[:, 12 + h, :], B[:, 12 + h, :], B[:, 8 + h, :], ALU.mult))
                for h in range(4):
                    wait_drained(vec, L, ("rec_sumsq", h))
                    vo(vec.reciprocal(rec_std[h % 2], rec_std[h % 2]))
                    vo.settle()
                    STT(B[:, 8 + h, :], B[:, 12 + h, :], par[:, 18:19], rec_std[h % 2], ALU.mult, ALU.mult)\
                        .then_inc(S["rec_f"], 1)
                for h in range(4):
                    wait(vec, "rec_hi", L, 4, h + 1)
                    TT(rec_hl[:, 1, h, :], B[:, 8 + h, :], rec_hl[:, 0, h, :].bitcast(f32), ALU.subtract)\
                        .then_inc(S["rec_lo"], 1)

                with vec.Fori(0, KT) as g:
                    wait_unit(vec, L, UM + g * 4 + 2)
                    vec.wait_ge(taken[0], L * (OUTS // 2) + OM // 2 + g * 2 + 2)
                    TT(halves(mix[:, 0, :]), acc[0][:, :, 0:HT], halves(gate_s[:, 0, :]), ALU.mult).then_inc(taken[0], 1)
                    wait_unit(vec, L, UM + g * 4 + 3)
                    vec.wait_ge(taken[1], L * (OUTS // 2) + OM // 2 + g * 2 + 2)
                    TT(halves(mix[:, 1, :]), acc[1][:, :, 0:HT], halves(gate_s[:, 1, :]), ALU.mult).then_inc(taken[1], 1)
                    vec.wait_ge(taken[0], L * (OUTS // 2) + OM // 2 + g * 2 + 3)
                    vec.wait_ge(taken[1], L * (OUTS // 2) + OM // 2 + g * 2 + 3)
                    TT(mix[:, 0, :], mix[:, 0, :], mix[:, 1, :], ALU.add).then_inc(S["mixed"], 1)
                    vec.wait_ge(S["merged_hi"], L * 8 + g + 1)
                    TT(merged[:, 1, ds(g, 1), :].rearrange("p a t -> p (a t)"), mix[:, 0, :],
                       merged[:, 0, ds(g, 1), :].rearrange("p a t -> p (a t)").bitcast(f32), ALU.subtract)\
                        .then_inc(S["merged_lo"], 1)
                    vec.wait_ge(S["merged_lo"], L * 8 + g + 1)
                    hold(vec)
                with vec.Fori(0, 4) as g:
                    for i in range(2):
                        wait_unit(vec, L, UO + g * 2 + i)
                        xk = x[:, ds(g * 2 + i, 1), :].rearrange("p a (b c) -> p (a b) c", b=2)
                        TT(xk, acc[i][:, :, 0:HT], xk, ALU.add).then_inc(taken[i], 1)
                        vec.drain().then_inc(S["x_updated"], 1)
                norm("norm2", 1)
                for part in range(2):
                    with vec.Fori(0, HID[part]) as g:
                        wait_unit(vec, L, UG[part] + g * 2 + 1)
                        vec.wait_ge(taken[0], L * (OUTS // 2) + OG[part] // 2 + g + 2)
                        TT(halves(act_f[:, :]), acc[1][:, :, 0:HT], halves(silu[:, :]), ALU.mult).then_inc(taken[1], 1)
                        vec.drain().then_inc(S["act_done"], 1)
                        vec.wait_ge(S["hid_hi"], L * 22 + 12 * part + g + 1)
                        vec.wait_ge(taken[1], L * (OUTS // 2) + OG[part] // 2 + g + 2)
                        TT(hidden[:, 1, ds(g, 1), :].rearrange("p a t -> p (a t)"), act_f[:, :],
                           hidden[:, 0, ds(g, 1), :].rearrange("p a t -> p (a t)").bitcast(f32), ALU.subtract)\
                            .then_inc(S["hid_lo"], 1)
                        vec.wait_ge(S["hid_lo"], L * 22 + 12 * part + g + 1)
                        hold(vec)
                    with vec.Fori(0, 4) as g:
                        for i in range(2):
                            wait_unit(vec, L, UD[part] + g * 4 + 2 * i + 1)
                            xk = x[:, ds(g * 2 + i, 1), :].rearrange("p a (b c) -> p (a b) c", b=2)
                            TT(xk, acc[i][:, :, 0:HT], xk, ALU.add).then_inc(taken[i], 1)
                            vec.drain().then_inc(S["x_updated"], 1)
                if ITEM.get("none") is not None:
                    wait_filled(vec, L, "none")
                    hold(vec)
                    vec.drain().then_inc(drained[1], 1)
                vo.end()


_STEPS = (246, 10)
_INS = ["x_prompt", "x_sample", "cache_k", "cache_v", "cache_idx_k", "state_rec", "page_table", "meta_tokens", "w_in",
        "norm_mix", "q_norm", "k_norm", "lb_raw", "rec_norm", "w_pa", "w_pb", "w_o", "norm_ffn", "w_gu", "w_down"]
_OUTS = [(1, 512, 1024), (8, 1, 1024), (2, 1, 528, 256), (2, 1, 528, 256), (2, 1, 528, 64), (2, 1, 4, 128, 128),
         (2, 8, 1, 256), (2, 8, 1, 256), (2, 8, 1, 64), (2, 8, 4, 128, 128)]
_SHAPES = [(1, 512, 1024), (8, 1, 1024), (2, 1, 528, 4, 64), (2, 1, 528, 4, 64), (2, 1, 528, 64), (2, 1, 4, 128, 128),
           (2, 8, 1, 4, 64), (2, 8, 1, 4, 64), (2, 8, 1, 64), (2, 8, 4, 128, 128)]


def kernel(**inputs):
    import numpy as np
    import concourse.bacc as bacc
    from concourse import mybir
    from concourse.bass_utils import run_bass_kernel_spmd

    nc = bacc.Bacc("TRN2", target_bir_lowering=False, num_devices=1)
    arrays, t = {}, {}

    def feed(name, a):
        arrays[f"in_{name}_dram"] = a
        t[name] = nc.dram_tensor(f"in_{name}_dram", a.shape, mybir.dt.from_np(a.dtype), kind="ExternalInput").ap()

    for name in _INS:
        feed(name, np.ascontiguousarray(inputs[name]))
    table, levels, where, resident = constants()
    feed("constants", table)
    feed("levels", levels)
    t["where"], t["resident"], t["steps"] = where, resident, _STEPS
    outs = [nc.dram_tensor(f"out_{i}_dram", shape, mybir.dt.float32, kind="ExternalOutput").ap()
            for i, shape in enumerate(_OUTS)]
    build(nc, t, outs)
    r = run_bass_kernel_spmd(nc, [arrays], core_ids=[0])
    return tuple(np.asarray(r.results[0][f"out_{i}_dram"]).reshape(s) for i, s in enumerate(_SHAPES))
```
